# Optimizing a Trainium2 kernel written in Bass

```python
import jax, jax.numpy as jnp
from jax import lax
import numpy as np

D_MODEL = 1024
BATCH = 1
SEQ = 256
DEPTH = 1
DEC_BATCH = 8
DEC_SEQ = 4
PAST_LEN = 2048
PAGE_SIZE = 128

POOL_WINDOWS = (2, 4, 8, 16)
POOL_GROUPS = 4
POOL_GROUP_DIM = D_MODEL // 8
D_POOL = POOL_GROUPS * POOL_GROUP_DIM
POOL_BUF = 16 - 1
RET_HEADS = 4
RET_DK = D_MODEL // 8
RET_DV = D_MODEL // 4
D_RET_K = RET_HEADS * RET_DK
D_RET_V = RET_HEADS * RET_DV
RET_CHUNK = 128
ROPE_BASE = 10000.0
IN_WIDTHS = (D_POOL, D_RET_K, D_RET_K, D_RET_V, D_RET_V, D_MODEL, D_MODEL)
D_IN = D_POOL + 2 * D_RET_K + 2 * D_RET_V + 2 * D_MODEL
N_EXPERTS = 64
TOP_K = 8
N_GROUPS = 8
TOPK_GROUPS = 4
D_EXPERT = D_MODEL // 4
ROUTED_SCALE = 2.5
N_MOD = 6
EPS = 1e-6

kernel_name = "hybrid_pool_retention_moe_decode_step"

def rmsnorm(x, g):
    xf = x.astype(jnp.float32)
    y = xf * lax.rsqrt(jnp.mean(xf * xf, axis=-1, keepdims=True) + EPS)
    return (y * g.astype(jnp.float32)).astype(x.dtype)

def modulate(h, shift, scale):
    return h * (1 + scale[:, None, :]) + shift[:, None, :]

def split_columns(z):
    outs, off = [], 0
    for w in IN_WIDTHS:
        outs.append(z[..., off:off + w])
        off += w
    return outs

def rotary(x, pos):
    half = x.shape[-1] // 2
    inv = jnp.power(ROPE_BASE, -jnp.arange(half, dtype=jnp.float32) / half)
    ang = pos.astype(jnp.float32)[:, None] * inv[None, :]
    cos = jnp.cos(ang)[None, :, None, :]
    sin = jnp.sin(ang)[None, :, None, :]
    xf = x.astype(jnp.float32)
    x1, x2 = xf[..., :half], xf[..., half:]
    return jnp.concatenate([x1 * cos - x2 * sin, x1 * sin + x2 * cos], axis=-1).astype(x.dtype)

def pool_mix(u_ext, start_pos, L):
    B = u_ext.shape[0]
    uf = u_ext.astype(jnp.float32)
    cs = jnp.concatenate([jnp.zeros((B, 1, D_POOL), jnp.float32), jnp.cumsum(uf, axis=1)], axis=1)
    pos = start_pos + jnp.arange(L, dtype=jnp.int32)
    outs = []
    for gi, w in enumerate(POOL_WINDOWS):
        lo, hi = gi * POOL_GROUP_DIM, (gi + 1) * POOL_GROUP_DIM
        win = cs[:, POOL_BUF + 1:POOL_BUF + 1 + L, lo:hi] - cs[:, POOL_BUF + 1 - w:POOL_BUF + 1 - w + L, lo:hi]
        cnt = jnp.minimum(w, pos + 1).astype(jnp.float32)
        outs.append(win / cnt[None, :, None])
    mean = jnp.concatenate(outs, axis=-1)
    return (mean - uf[:, POOL_BUF:]).astype(u_ext.dtype)

def retention_scan(S0, q, k, v, log_g, chunk):
    B, L, H, _ = q.shape
    nc = L // chunk
    idx = jnp.arange(chunk, dtype=jnp.float32)
    diff = idx[:, None] - idx[None, :]
    causal = diff >= 0
    intra = jnp.where(causal[None], jnp.exp(log_g[:, None, None] * jnp.maximum(diff, 0.0)[None]), 0.0)
    q_dec = jnp.exp(log_g[None, :] * (idx[:, None] + 1.0))
    k_dec = jnp.exp(log_g[None, :] * (chunk - 1.0 - idx[:, None]))
    s_dec = jnp.exp(log_g * chunk)

    def to_chunks(t):
        return t.reshape(B, nc, chunk, *t.shape[2:]).swapaxes(0, 1)

    def step(S, qkv):
        qc, kc, vc = qkv
        qf, kf, vf = qc.astype(jnp.float32), kc.astype(jnp.float32), vc.astype(jnp.float32)
        scores = jnp.einsum('bchd,bmhd->bhcm', qf, kf) * intra[None]
        inner = jnp.einsum('bhcm,bmhe->bche', scores, vf)
        cross = jnp.einsum('bchd,bhde->bche', qf * q_dec[None, :, :, None], S)
        S_new = s_dec[None, :, None, None] * S + jnp.einsum('bchd,bche->bhde', kf * k_dec[None, :, :, None], vf)
        return S_new, inner + cross

    S_fin, o = lax.scan(step, S0, (to_chunks(q), to_chunks(k), to_chunks(v)))
    o = o.swapaxes(0, 1).reshape(B, L, H, -1)
    return o, S_fin

def token_mixer(h, pool_prefix, S0, start_pos, chunk, log_g,
                w_in, w_pool_group, pool_scale, w_branch_pool, w_branch_ret, w_out):
    B, L, _ = h.shape
    u, q, k, v, g, gate_a, gate_b = split_columns(h @ w_in)
    u_ext = jnp.concatenate([pool_prefix.astype(u.dtype), u], axis=1)
    pm = pool_mix(u_ext, start_pos, L)
    pm = jnp.einsum('blgc,gcd->blgd', pm.reshape(B, L, POOL_GROUPS, POOL_GROUP_DIM), w_pool_group)
    pm = pm.reshape(B, L, D_POOL) * pool_scale
    a = pm @ w_branch_pool
    pos = start_pos + jnp.arange(L, dtype=jnp.int32)
    qh = rotary(q.reshape(B, L, RET_HEADS, RET_DK), pos)
    kh = rotary(k.reshape(B, L, RET_HEADS, RET_DK), pos) * (RET_DK ** -0.5)
    vh = v.reshape(B, L, RET_HEADS, RET_DV)
    o, S_new = retention_scan(S0, qh, kh, vh, log_g, chunk)
    o = o * lax.rsqrt(jnp.mean(o * o, axis=-1, keepdims=True) + EPS)
    o = o.reshape(B, L, D_RET_V).astype(h.dtype)
    r = (jax.nn.silu(g) * o) @ w_branch_ret
    merged = jax.nn.sigmoid(gate_a) * a + jax.nn.sigmoid(gate_b) * r
    return merged @ w_out, u_ext[:, -POOL_BUF:], S_new

def moe(h, w_router, b_router, w_exp_gate, w_exp_up, w_exp_down, w_sh_gate, w_sh_up, w_sh_down):
    T = h.shape[0]
    s = jax.nn.sigmoid(h.astype(jnp.float32) @ w_router.astype(jnp.float32))
    sb = s + b_router.astype(jnp.float32)
    grp_score = lax.top_k(sb.reshape(T, N_GROUPS, N_EXPERTS // N_GROUPS), 2)[0].sum(-1)
    _, gidx = lax.top_k(grp_score, TOPK_GROUPS)
    gmask = jax.nn.one_hot(gidx, N_GROUPS, dtype=jnp.float32).sum(1) > 0
    emask = jnp.repeat(gmask, N_EXPERTS // N_GROUPS, axis=1)
    _, eidx = lax.top_k(jnp.where(emask, sb, -jnp.inf), TOP_K)
    sel = jnp.take_along_axis(s, eidx, axis=1)
    wts = sel / jnp.sum(sel, axis=-1, keepdims=True) * ROUTED_SCALE
    gates = jnp.einsum('tke,tk->te', jax.nn.one_hot(eidx, N_EXPERTS, dtype=jnp.float32), wts)

    def expert_step(acc, ew):
        g_e, wg, wu, wd = ew
        hid = jax.nn.silu(h @ wg) * (h @ wu)
        return acc + g_e[:, None] * (hid @ wd).astype(jnp.float32), None

    acc, _ = lax.scan(expert_step, jnp.zeros((T, D_MODEL), jnp.float32),
                      (gates.T, w_exp_gate, w_exp_up, w_exp_down))
    shared = (jax.nn.silu(h @ w_sh_gate) * (h @ w_sh_up)) @ w_sh_down
    return (acc + shared.astype(jnp.float32)).astype(h.dtype)

def setup_inputs(seed: int = 0) -> dict:
    key = jax.random.key(seed)
    ks = jax.random.split(key, 32)
    nrm = jax.random.normal
    f32 = jnp.float32
    inp = {
        "x_prompt": nrm(ks[0], (BATCH, SEQ, D_MODEL), f32),
        "x_sample": nrm(ks[1], (DEC_BATCH, DEC_SEQ, D_MODEL), f32),
        "c_prompt": nrm(ks[2], (BATCH, D_MODEL), f32),
        "c_sample": nrm(ks[3], (DEC_BATCH, D_MODEL), f32),
        "state_pool": nrm(ks[4], (DEPTH, DEC_BATCH, POOL_BUF, D_POOL), f32),
        "state_ret": 0.5 * nrm(ks[5], (DEPTH, DEC_BATCH, RET_HEADS, RET_DK, RET_DV), f32),
        "w_ada": 0.5 * D_MODEL ** -0.5 * nrm(ks[6], (DEPTH, D_MODEL, N_MOD * D_MODEL), f32),
        "b_ada": 0.01 * nrm(ks[7], (DEPTH, N_MOD * D_MODEL), f32),
        "g_norm1": 1.0 + 0.01 * nrm(ks[8], (DEPTH, D_MODEL), f32),
        "w_in": D_MODEL ** -0.5 * nrm(ks[9], (DEPTH, D_MODEL, D_IN), f32),
        "w_pool_group": POOL_GROUP_DIM ** -0.5 * nrm(ks[10], (DEPTH, POOL_GROUPS, POOL_GROUP_DIM, POOL_GROUP_DIM), f32),
        "pool_scale": 1.0 + 0.1 * nrm(ks[11], (DEPTH, D_POOL), f32),
        "w_branch_pool": D_POOL ** -0.5 * nrm(ks[12], (DEPTH, D_POOL, D_MODEL), f32),
        "w_branch_ret": D_RET_V ** -0.5 * nrm(ks[13], (DEPTH, D_RET_V, D_MODEL), f32),
        "w_out": D_MODEL ** -0.5 * nrm(ks[14], (DEPTH, D_MODEL, D_MODEL), f32),
        "g_norm2": 1.0 + 0.01 * nrm(ks[15], (DEPTH, D_MODEL), f32),
        "w_router": D_MODEL ** -0.5 * nrm(ks[16], (DEPTH, D_MODEL, N_EXPERTS), f32),
        "b_router": 0.01 * nrm(ks[17], (DEPTH, N_EXPERTS), f32),
        "w_exp_gate": D_MODEL ** -0.5 * nrm(ks[18], (DEPTH, N_EXPERTS, D_MODEL, D_EXPERT), f32),
        "w_exp_up": D_MODEL ** -0.5 * nrm(ks[19], (DEPTH, N_EXPERTS, D_MODEL, D_EXPERT), f32),
        "w_exp_down": D_EXPERT ** -0.5 * nrm(ks[20], (DEPTH, N_EXPERTS, D_EXPERT, D_MODEL), f32),
        "w_sh_gate": D_MODEL ** -0.5 * nrm(ks[21], (DEPTH, D_MODEL, D_EXPERT), f32),
        "w_sh_up": D_MODEL ** -0.5 * nrm(ks[22], (DEPTH, D_MODEL, D_EXPERT), f32),
        "w_sh_down": D_EXPERT ** -0.5 * nrm(ks[23], (DEPTH, D_EXPERT, D_MODEL), f32),
        "g_final": 1.0 + 0.01 * nrm(ks[24], (D_MODEL,), f32),
    }
    return inp

def reference(x_prompt, x_sample, c_prompt, c_sample, state_pool, state_ret,
              w_ada, b_ada, g_norm1, w_in, w_pool_group, pool_scale, w_branch_pool,
              w_branch_ret, w_out, g_norm2, w_router, b_router, w_exp_gate, w_exp_up,
              w_exp_down, w_sh_gate, w_sh_up, w_sh_down, g_final):
    B, S, D = x_prompt.shape
    DB, DS, _ = x_sample.shape
    log_g = jnp.log(1.0 - jnp.power(2.0, -5.0 - jnp.arange(RET_HEADS, dtype=jnp.float32)))
    xp, xs = x_prompt, x_sample
    pool_p, ret_p, pool_s, ret_s = [], [], [], []
    for l in range(DEPTH):
        mod_p = (c_prompt @ w_ada[l] + b_ada[l]).reshape(B, N_MOD, D)
        mod_s = (c_sample @ w_ada[l] + b_ada[l]).reshape(DB, N_MOD, D)
        mix_w = (log_g, w_in[l], w_pool_group[l], pool_scale[l], w_branch_pool[l], w_branch_ret[l], w_out[l])
        hp = modulate(rmsnorm(xp, g_norm1[l]), mod_p[:, 0], mod_p[:, 1])
        hs = modulate(rmsnorm(xs, g_norm1[l]), mod_s[:, 0], mod_s[:, 1])
        mp, bp, sp = token_mixer(hp, jnp.zeros((B, POOL_BUF, D_POOL), hp.dtype),
                                 jnp.zeros((B, RET_HEADS, RET_DK, RET_DV), jnp.float32),
                                 0, RET_CHUNK, *mix_w)
        ms, bs, ss = token_mixer(hs, state_pool[l], state_ret[l].astype(jnp.float32),
                                 PAST_LEN, DS, *mix_w)
        xp = xp + mod_p[:, 2][:, None, :] * mp
        xs = xs + mod_s[:, 2][:, None, :] * ms
        pool_p.append(bp)
        ret_p.append(sp.astype(x_prompt.dtype))
        pool_s.append(bs)
        ret_s.append(ss.astype(state_ret.dtype))
        hp2 = modulate(rmsnorm(xp, g_norm2[l]), mod_p[:, 3], mod_p[:, 4])
        hs2 = modulate(rmsnorm(xs, g_norm2[l]), mod_s[:, 3], mod_s[:, 4])
        flat = jnp.concatenate([hp2.reshape(B * S, D), hs2.reshape(DB * DS, D)], axis=0)
        f = moe(flat, w_router[l], b_router[l], w_exp_gate[l], w_exp_up[l], w_exp_down[l],
                w_sh_gate[l], w_sh_up[l], w_sh_down[l])
        xp = xp + mod_p[:, 5][:, None, :] * f[:B * S].reshape(B, S, D)
        xs = xs + mod_s[:, 5][:, None, :] * f[B * S:].reshape(DB, DS, D)
    y_prompt = rmsnorm(xp, g_final)
    y_sample = rmsnorm(xs, g_final)
    new_pool_prompt = jnp.stack(pool_p, axis=0)
    new_ret_prompt = jnp.stack(ret_p, axis=0)
    new_pool_sample = jnp.stack(pool_s, axis=0)
    new_ret_sample = jnp.stack(ret_s, axis=0)
    return (y_prompt, y_sample, new_pool_prompt, new_ret_prompt, new_pool_sample, new_ret_sample)


_drawn_inputs = setup_inputs


def setup_inputs(seed=0):
    import zlib

    import numpy as np

    out = dict(_drawn_inputs(seed))
    spreads = {}
    factors = {}
    for name, (base, spread) in spreads.items():
        noise = np.random.default_rng([zlib.crc32(name.encode()), seed]).standard_normal(out[name].shape)
        drawn = base * np.exp(spread * noise) if base else spread * noise
        out[name] = __import__('jax').numpy.asarray(drawn.astype(out[name].dtype))
    for name, factor in factors.items():
        out[name] = (out[name] * factor).astype(out[name].dtype)
    return out
```

```python
from contextlib import ExitStack

import numpy as np
import concourse.bass as bass
from concourse import mybir

ALU = mybir.AluOpType
ACT = mybir.ActivationFunctionType
F32 = mybir.dt.float32
AX_X = mybir.AxisListType.X

P = 128
D = 1024
KD = D // P
SEQ, DEC_B, DEC_L = 256, 8, 4
NS = DEC_B * DEC_L
T = SEQ + NS
TOK = [(0, P), (P, P), (SEQ, NS)]
PAST = 2048
WINDOWS = (2, 4, 8, 16)
PB = 15
G = 4
DV = 256
CHUNK = 128
NMOD = 6
NSEQ = 1 + DEC_B
E = 64
NG, EG = 8, 8
DE = 256
SCALE_OUT = 2.5
EPS = 1e-6
BC = 512
RING = 3
LOW = -1e30

C_ID, C_SWAP, C_ONES = 0, P, 2 * P
C_COS = 3 * P
C_SIN = C_COS + T
C_INTRA = C_SIN + T
C_QDEC = C_INTRA + G * P
C_INTRAS = C_QDEC + G * (CHUNK + NS)
C_ICNT = C_INTRAS + G * NS
C_KDEC = C_ICNT + G * 16
C_KDECS = C_KDEC + G
C_ROWB = C_KDECS + G
C_IOTA = C_ROWB + DEC_B
NC_COLS = C_IOTA + 8

Z_U, Z_Q, Z_K, Z_G, Z_A, Z_B = 0, 4, 8, 12, 20, 28
NZ = 36

V_ADA, V_G1, V_G2, V_GF, V_PS = 0, 48, 56, 64, 72
NV = 76


def log_decays():
    f = np.float32
    return np.log(f(1.0) - np.power(f(2.0), f(-5.0) - np.arange(G, dtype=f))).astype(f)


def shape_constants():
    c = np.zeros((P, NC_COLS), np.float64)
    c[:, C_ID:C_ID + P] = np.eye(P)
    c[:, C_SWAP:C_SWAP + P] = np.roll(np.eye(P), P // 2, axis=0)
    c[:, C_ONES:C_ONES + P] = 1.0
    f = np.float32
    inv = np.power(f(10000.0), -np.arange(64, dtype=f) / f(64)).astype(f)
    pos = np.concatenate([np.arange(SEQ), np.tile(PAST + np.arange(DEC_L), DEC_B)]).astype(f)
    ang = (np.concatenate([inv, inv])[:, None] * pos[None, :]).astype(f).astype(np.float64)
    c[:, C_COS:C_COS + T] = np.cos(ang)
    c[:, C_SIN:C_SIN + T] = np.sin(ang) * np.where(np.arange(P) < 64, -1.0, 1.0)[:, None]
    lg = log_decays().astype(np.float64)
    ks = P ** -0.5
    m, q = np.arange(P)[:, None], np.arange(P)[None, :]
    ms, qs = np.arange(NS)[:, None], np.arange(NS)[None, :]
    for h in range(G):
        c[:, C_INTRA + h * P:C_INTRA + (h + 1) * P] = np.where(q >= m, np.exp(lg[h] * np.maximum(q - m, 0)), 0) * ks
        c[:NS, C_INTRAS + h * NS:C_INTRAS + (h + 1) * NS] = np.where(
            (qs >= ms) & (qs // DEC_L == ms // DEC_L), np.exp(lg[h] * np.maximum(qs - ms, 0)), 0) * ks
        w = C_QDEC + h * (CHUNK + NS)
        c[:, w:w + CHUNK] = np.exp(lg[h] * (np.arange(CHUNK) + 1.0))[None, :]
        c[:, w + CHUNK:w + CHUNK + NS] = np.exp(lg[h] * (np.arange(NS) % DEC_L + 1.0))[None, :]
        c[:, C_KDEC + h] = np.exp(lg[h] * (CHUNK - 1.0 - np.arange(P))) * ks
        c[:NS, C_KDECS + h] = np.exp(lg[h] * (DEC_L - 1.0 - np.arange(NS) % DEC_L)) * ks
        c[:, C_ICNT + h * 16:C_ICNT + (h + 1) * 16] = 1.0 / np.minimum(WINDOWS[h], np.arange(16) + 1.0)[None, :]
    for b in range(DEC_B):
        c[b * DEC_L:(b + 1) * DEC_L, C_ROWB + b] = 1.0
    return c.astype(np.float32)


def bcast(ap, at, n):
    wide = ap.unsqueeze(at)
    shape = list(wide.shape)
    shape[at] = n
    return wide.broadcast_to(shape)


def build(nc, consts, x_prompt, x_sample, c_prompt, c_sample, state_pool, state_ret, w_ada, b_ada, g_norm1,
          w_in, w_pool_group, pool_scale, w_branch_pool, w_branch_ret, w_out, g_norm2, w_router, b_router,
          w_exp_gate, w_exp_up, w_exp_down, w_sh_gate, w_sh_up, w_sh_down, g_final,
          y_prompt, y_sample, new_pool_prompt, new_ret_prompt, new_pool_sample, new_ret_sample):
    lg = log_decays().astype(np.float64)
    s_dec = [float(np.exp(v * CHUNK)) for v in lg]
    s_dec_s = [float(np.exp(v * DEC_L)) for v in lg]

    with ExitStack() as ctx:
        def sb(name, shape):
            return ctx.enter_context(nc.sbuf_tensor(name, shape, F32))

        def sem(name):
            return ctx.enter_context(nc.semaphore(name))

        xT = sb("xT", [P, KD, T])
        hT = sb("hT", [P, KD, T])
        zT = sb("zT", [P, NZ, T])
        v = sb("v", [P, 3, D])
        ring = sb("ring", [P, RING, KD * BC])
        S = sb("S", [P, G, DEC_B, DV])
        SP0 = sb("SP0", [P, G, DV])
        ktok = sb("ktok", [P, 2, G * P])
        qd = sb("qd", [P, G, CHUNK + NS])
        sT = sb("sT", [P, 2, T])
        cst = sb("cst", [P, NC_COLS])
        scratch = sb("scratch", [P, 5100])
        modT = sb("modT", [P, NMOD * KD, NSEQ])
        vecT = sb("vecT", [P, NV])
        cT = sb("cT", [P, KD, NSEQ])
        gs = sb("gs", [P, KD, NSEQ])
        rstd = sb("rstd", [P, T])
        wpg = sb("wpg", [P, G, P])
        wrt = sb("wrt", [P, KD, E])
        brow = sb("brow", [P, E])
        eps_col = sb("eps_col", [P, 1])

        ident = cst[:, C_ID:C_ID + P]
        swap = cst[:, C_SWAP:C_SWAP + P]
        ones = cst[:, C_ONES:C_ONES + P]
        xin = scratch[:, 0:3 * D].rearrange("p (t d) -> p t d", t=3)
        vrow = scratch[:, 3072:3072 + P]
        crow = scratch[0:NSEQ, 3200:3200 + D]
        prow = scratch[0:DEC_B * PB, 4224:4224 + 512]
        LP, LS = SEQ + PB, DEC_L + PB
        PW = G * LP + G * DEC_B * LS
        extp = scratch[:, 0:G * LP].rearrange("p (g l) -> p g l", g=G)
        exts = scratch[:, G * LP:PW].rearrange("p (g b l) -> p g b l", g=G, b=DEC_B)
        sumA = scratch[:, PW:2 * PW]
        sumB = scratch[:, 2 * PW:3 * PW]
        assert 3 * PW <= 5100
        kblk = scratch[0:NS, 0:DEC_B * G * P].rearrange("p (b n) -> p b n", b=DEC_B)
        ktoks = scratch[0:NS, 4096:4096 + G * P]
        pst = S[:, 0, 0:4, :].rearrange("p b e -> p (b e)")
        stT = sb("stT", [P, G, DEC_B * PB])
        ptail = sb("ptail", [NS, 2, G * P])

        bank = [ctx.enter_context(nc.psum_tensor(f"bank{i}", [P, 512], F32)) for i in range(8)]
        ready = [sem(f"ready{i}") for i in range(8)]
        free = [sem(f"free{i}") for i in range(8)]

        class Tiles:
            def __init__(self, first):
                self.first, self.n = first, 0

            def take(self, k=1):
                a = self.n
                self.n += k
                return a if k == 1 else range(a, a + k)

        def bk(ringno, n):
            return ringno * 4 + n % 4

        def fill_wait(pe, r, n, more=0):
            if isinstance(more, int) and n + 4 * more < 4:
                return
            pe.wait_ge(free[bk(r, n)], n // 4 + more)

        def read_wait(eng, r, n, more=0):
            eng.wait_ge(ready[bk(r, n)], n // 4 + 1 + more)

        def drain_wait(eng, r, n, more=0):
            eng.wait_ge(free[bk(r, n)], n // 4 + 1 + more)

        Z, Y = Tiles(0), Tiles(4)
        z_x = Z.take(KD)
        z_vec = Z.take()
        z_n1 = Z.take()
        y_moda = Y.take()
        z_uqk = Z.take(12)
        z_swap = Z.take(8)
        z_v = Z.take(6)
        z_pool = Z.take()
        z_fm = Z.take(24)
        y_modb = Y.take()
        z_tail = Z.take(2)
        z_pg = Z.take(4)
        z_kt = Z.take(3)
        y_sc, y_s0, y_s1, y_ss, z_o = [], [], [], [], []
        for h in range(G + 1):
            if h < G:
                y_sc.append(Y.take())
                y_s0.append(Y.take())
            if h > 0:
                z_o.append(Z.take(2))
                y_s1.append(Y.take())
                y_ss.append(Y.take(4))
        z_a = Z.take(KD)
        y_hn = Y.take(4)
        z_r = Z.take(KD)
        z_m = Z.take(KD)
        y_n2 = Y.take()
        y_rt = Y.take(3)
        z_shu = Z.take(4)
        z_shd = Z.take(6)
        z_exp = Z.n
        LOOP_Z = 20
        Z.n = z_exp + LOOP_Z * (E // 2)
        Z_END = Z.n
        z_f = Z.take(KD)
        y_nf = Y.take()
        z_y = Z.take(6)

        ld = {k: sem(f"loaded_{k}") for k in ("consts", "x", "small", "pool", "state", "wpg", "router")}
        ring_in = [sem(f"ring_in{i}") for i in range(RING)]
        ada_used = sem("ada_used")
        stored = sem("stored")
        S_ = {}
        for name in ("eps", "xT_sq", "h1", "rot", "qd_s", "pm", "kbl", "osq", "sig_ab", "silu_g",
                     "gated", "merged", "x1_sq", "h2", "router_set", "x2_sq", "yT"):
            S_[name] = sem(name)
        dve_chain = sem("dve_chain")

        N_ADA_A, N_UQK, N_V, N_FM, N_ADA_B = 4, 3, 2, 6, 8
        n_uqk = N_ADA_A
        n_v = n_uqk + N_UQK
        n_fm = n_v + N_V
        n_adab = n_fm + N_FM
        n_bp = n_adab + N_ADA_B
        n_br = n_bp + 1
        n_wo = n_br + 2
        n_sg = n_wo + 2
        n_sd = n_sg + 1
        n_exp = n_sd + 1

        ada_step = {j: j + 1 for j in range(N_ADA_A - 1)}
        ada_step.update({n_adab + j: N_ADA_A - 1 + j + 1 for j in range(N_ADA_B - 1)})
        last_fill = {N_ADA_A - 1: (1, y_moda), n_adab + N_ADA_B - 1: (1, y_modb), n_bp: (0, z_a[-1]),
                     n_sg: (0, z_shu[-1]), n_sd: (0, z_shd[-1])}
        last_fill.update({n_uqk + j: (0, z_uqk[4 * j + 3]) for j in range(N_UQK)})
        last_fill.update({n_v + j: (0, z_v[3 * j + 2]) for j in range(N_V)})
        last_fill.update({n_fm + j: (0, z_fm[4 * j + 3]) for j in range(N_FM)})
        last_fill.update({n_br + j: (0, z_r[4 * j + 3]) for j in range(2)})
        last_fill.update({n_wo + j: (0, z_m[4 * j + 3]) for j in range(2)})
        EXP_UP1, EXP_DN5 = 3, 9

        def slot(n):
            return n % RING

        def wblk(n):
            return ring[:, slot(n), :].rearrange("p (k c) -> p k c", k=KD)

        def arrived(pe, n, more=0):
            pe.wait_ge(ring_in[slot(n)], 16 * (n // RING + 1) + more)

        def cols(w, c0):
            return w.rearrange("(k p) c -> p k c", p=P)[:, :, bass.ds(c0, BC)]

        win, wada = w_in[0], w_ada[0]

        exp_in = [sem("exp_in0"), sem("exp_in1")]
        exp_din = [sem("exp_din0"), sem("exp_din1")]

        def pair_wait(at, i):
            n = z_exp + at
            return ready[bk(0, n)], i * (LOOP_Z // 4) + (n // 4 + 1 - LOOP_Z // 4)

        def egu(j):
            return ring[:, j, :].rearrange("p (k c) -> p k c", k=KD)

        def edown(j):
            return ring[:, 2, j * 2 * D:(j + 1) * 2 * D].rearrange("p (k c) -> p k c", k=2)

        zf = zT[:, :, :].rearrange("p n t -> p (n t)")
        HID = [0, 2]
        SG = [4, 6]
        R0 = 8 * T

        def area(k, n):
            nonlocal_at[0] += n
            return zf[:, nonlocal_at[0] - n:nonlocal_at[0]]

        nonlocal_at = [R0]
        sc_s = area(0, 3 * E).rearrange("p (t e) -> p t e", t=3)
        sc_b = area(0, 3 * E).rearrange("p (t e) -> p t e", t=3)
        sc_m = area(0, 3 * E).rearrange("p (t e) -> p t e", t=3)
        sc_r = area(0, 3 * E).rearrange("p (t e) -> p t e", t=3)
        gates = area(0, 3 * E).rearrange("p (t e) -> p t e", t=3)
        gtop = area(0, 3 * NG * 8).rearrange("p (t g e) -> p t g e", t=3, g=NG)
        gsc = area(0, 3 * 12).rearrange("p (t g) -> p t g", t=3)
        grep = area(0, 3 * 12).rearrange("p (t g) -> p t g", t=3)
        gsort = area(0, 3 * 8).rearrange("p (t g) -> p t g", t=3)
        gmask = area(0, 3 * 8).rearrange("p (t g) -> p t g", t=3)
        gfill = area(0, 3 * 8).rearrange("p (t g) -> p t g", t=3)
        etop = area(0, 3 * 8).rearrange("p (t g) -> p t g", t=3)
        wsum = area(0, 3)
        winv = area(0, 3)
        acc = v

        block = ctx.enter_context(nc.Block())

        @block.sync
        def _(sp):
            sp.dma_start(xin[:, 0:2, :], x_prompt[0].rearrange("(t p) d -> p t d", p=P)).then_inc(ld["x"], 16)
            sp.dma_start(xin[0:NS, 2, :], x_sample.rearrange("b l d -> (b l) d")).then_inc(ld["x"], 16)
            sp.dma_start(cst[:, :], consts).then_inc(ld["consts"], 16)
            sp.dma_start(crow[0:1, :], c_prompt).then_inc(ld["small"], 16)
            sp.dma_start(crow[1:NSEQ, :], c_sample).then_inc(ld["small"], 16)
            for row, src, n in ((V_ADA, b_ada, 48), (V_G1, g_norm1, 8), (V_G2, g_norm2, 8), (V_PS, pool_scale, 4)):
                sp.dma_start(vrow[row:row + n, :], src[0].rearrange("(r c) -> r c", c=P)).then_inc(ld["small"], 16)
            sp.dma_start(vrow[V_GF:V_GF + 8, :], g_final.rearrange("(r c) -> r c", c=P)).then_inc(ld["small"], 16)

            def used(n):
                if n in ada_step:
                    sp.wait_ge(ada_used, ada_step[n])
                else:
                    read_wait(sp, *last_fill[n])

            def stream(n, src):
                if n >= RING:
                    used(n - RING)
                sp.dma_start(wblk(n), src).then_inc(ring_in[slot(n)], 16)

            for j in range(N_ADA_A):
                stream(j, cols(wada, BC * j))
            sp.dma_start(prow, state_pool[0].rearrange("b r c -> (b r) c")).then_inc(ld["pool"], 16)
            for j in range(N_UQK + N_V):
                stream(n_uqk + j, cols(win, BC * j))
            sp.dma_start(wpg[:, :, :], w_pool_group[0].rearrange("g c d -> c g d")).then_inc(ld["wpg"], 16)
            sp.dma_start(wrt[:, :, :], w_router[0].rearrange("(k p) e -> p k e", p=P)).then_inc(ld["router"], 16)
            sp.dma_start(brow[:, :], bcast(b_router[0], 0, P)).then_inc(ld["router"], 16)
            for j in range(N_FM):
                stream(n_fm + j, cols(win, BC * (N_UQK + N_V + j)))
            for h in range(G):
                sp.dma_start(S[:, h, :, :], state_ret[0, :, h].rearrange("b d e -> d b e")).then_inc(ld["state"], 16)
            sp.dma_start(new_pool_sample[0, :, 0:PB - DEC_L, :], state_pool[0, :, DEC_L:PB, :]).then_inc(stored, 16)
            for j in range(N_ADA_B):
                stream(n_adab + j, cols(wada, BC * (N_ADA_A + j)))
            used(n_bp - RING)
            sp.dma_start(ring[:, slot(n_bp), :].rearrange("p (k c) -> p k c", k=G),
                         w_branch_pool[0].rearrange("(k p) c -> p k c", p=P)).then_inc(ring_in[slot(n_bp)], 16)
            for n in z_tail:
                drain_wait(sp, 0, n)
            sp.dma_start(new_pool_prompt[0, 0], ptail[0:PB, 0, :]).then_inc(stored, 16)
            sp.dma_start(new_pool_sample[0, :, PB - DEC_L:PB, :],
                         ptail[0:NS, 1, :]).then_inc(stored, 16)
            for j in range(2):
                stream(n_br + j, cols(w_branch_ret[0], BC * j))
            for j in range(2):
                stream(n_wo + j, cols(w_out[0], BC * j))
            drain_wait(sp, 1, y_s1[G - 1])
            sp.dma_start(new_ret_prompt[0, 0].rearrange("h d e -> d h e"), SP0[:, :, :]).then_inc(stored, 16)
            for h in range(G):
                for n in y_ss[h]:
                    drain_wait(sp, 1, n)
                sp.dma_start(new_ret_sample[0, :, h].rearrange("b d e -> d b e"), S[:, h, :, :]).then_inc(stored, 16)

            def gate_up(n, wg, wu):
                sp.dma_start(wblk(n)[:, :, 0:DE], wg).then_inc(ring_in[slot(n)], 16)
                sp.dma_start(wblk(n)[:, :, DE:2 * DE], wu).then_inc(ring_in[slot(n)], 16)

            used(n_sg - RING)
            gate_up(n_sg, w_sh_gate[0].rearrange("(k p) f -> p k f", p=P), w_sh_up[0].rearrange("(k p) f -> p k f", p=P))
            used(n_sd - RING)
            sp.dma_start(ring[:, slot(n_sd), 0:2 * D].rearrange("p (k c) -> p k c", k=2),
                         w_sh_down[0].rearrange("(k p) c -> p k c", p=P)).then_inc(ring_in[slot(n_sd)], 16)
            for n in range(n_exp - RING, n_exp):
                used(n)
            with sp.Fori(0, E // 2) as i:
                for j in range(2):
                    w1 = w_exp_gate[0, bass.ds(i * 2 + j, 1)].rearrange("a (k p) f -> p (a k) f", p=P)
                    w2 = w_exp_up[0, bass.ds(i * 2 + j, 1)].rearrange("a (k p) f -> p (a k) f", p=P)
                    w3 = w_exp_down[0, bass.ds(i * 2 + j, 1)].rearrange("a (k p) f -> p (a k) f", p=P)
                    sp.wait_ge(*pair_wait(EXP_UP1 + 10 * j, i))
                    sp.dma_start(egu(j)[:, :, 0:DE], w1).then_inc(exp_in[j], 16)
                    sp.dma_start(egu(j)[:, :, DE:2 * DE], w2).then_inc(exp_in[j], 16)
                    sp.wait_ge(*pair_wait(EXP_DN5 + 10 * j, i))
                    sp.dma_start(edown(j), w3).then_inc(exp_din[j], 16)
            for n in z_y:
                drain_wait(sp, 0, n)
            sp.dma_start(y_prompt[0].rearrange("(t p) d -> p t d", p=P), xin[:, 0:2, :]).then_inc(stored, 16)
            sp.dma_start(y_sample.rearrange("b l d -> (b l) d"), xin[0:NS, 2, :]).then_inc(stored, 16)
            sp.wait_ge(stored, 16 * (3 + 1 + G + 2))

        @block.tensor
        def _(pe):
            def done(ins, r, n):
                ins.then_inc(ready[bk(r, n)], 1)

            def out(r, n):
                return bank[bk(r, n)]

            def sums(r, n, rows, arrive=None):
                fill_wait(pe, r, n)
                for k, row in enumerate(rows):
                    if arrive is not None:
                        pe.wait_ge(arrive, k + 1)
                    last = pe.matmul(out(r, n)[:, 0:T], ones, row, start=(k == 0), stop=(k == len(rows) - 1))
                done(last, r, n)

            def ada(n0, count, y):
                fill_wait(pe, 1, y)
                for j in range(count):
                    arrived(pe, n0 + j)
                    w = wblk(n0 + j)
                    for f in range(4):
                        c = (4 * j + f) * NSEQ
                        for k in range(KD):
                            last = pe.matmul(out(1, y)[:, c:c + NSEQ], w[:, k, f * P:(f + 1) * P], cT[:, k, :],
                                             start=(k == 0), stop=(k == KD - 1))
                    if j < count - 1:
                        last.then_inc(ada_used, 1)
                done(last, 1, y)

            def feature_major(z0, w, srcT, kt=KD, nf=4, more=0):
                for f in range(nf):
                    fill_wait(pe, 0, z0 + f, more)
                    for k in range(kt):
                        last = pe.matmul(out(0, z0 + f)[:, 0:T], w[:, k, f * P:(f + 1) * P], srcT[:, k, :],
                                         start=(k == 0), stop=(k == kt - 1))
                    done(last, 0, z0 + f)

            pe.wait_ge(ld["consts"], 16)
            pe.wait_ge(ld["x"], 32)
            for k in range(KD):
                n = z_x[k]
                fill_wait(pe, 0, n)
                for t, (t0, w) in enumerate(TOK):
                    last = pe.transpose(out(0, n)[:, t0:t0 + w], xin[0:w, t, k * P:(k + 1) * P], ident[0:w, 0:w])
                done(last, 0, n)
            pe.wait_ge(ld["small"], 16 * 7)
            fill_wait(pe, 0, z_vec)
            pe.transpose(out(0, z_vec)[:, 0:NV], vrow[0:NV, :], ident[0:NV, 0:NV])
            for k in range(KD):
                last = pe.transpose(out(0, z_vec)[:, P + k * NSEQ:P + (k + 1) * NSEQ],
                                    crow[:, k * P:(k + 1) * P], ident[0:NSEQ, 0:NSEQ])
            done(last, 0, z_vec)
            sums(0, z_n1, [zT[:, k, :] for k in range(KD)], S_["xT_sq"])
            drain_wait(pe, 0, z_vec)
            ada(0, N_ADA_A, y_moda)
            pe.wait_ge(S_["h1"], 1)
            for j in range(N_UQK):
                arrived(pe, n_uqk + j)
                feature_major(z_uqk[4 * j], wblk(n_uqk + j), hT)
            for j in range(8):
                fill_wait(pe, 0, z_swap[j])
                drain_wait(pe, 0, z_uqk[4 + j])
                done(pe.matmul(out(0, z_swap[j])[:, 0:T], swap, zT[:, Z_Q + j, :], start=True, stop=True), 0, z_swap[j])
            for j in range(N_V):
                arrived(pe, n_v + j)
                for t, (t0, w) in enumerate(TOK):
                    n = z_v[3 * j + t]
                    fill_wait(pe, 0, n)
                    for k in range(KD):
                        last = pe.matmul(out(0, n)[0:w, :], hT[:, k, t0:t0 + w], wblk(n_v + j)[:, k, :],
                                         start=(k == 0), stop=(k == KD - 1))
                    done(last, 0, n)
            pe.wait_ge(ld["pool"], 16)
            fill_wait(pe, 0, z_pool)
            for g in range(G):
                last = pe.transpose(out(0, z_pool)[:, g * 120:(g + 1) * 120], prow[:, g * P:(g + 1) * P],
                                    ident[0:120, 0:120])
            done(last, 0, z_pool)
            with pe.Fori(0, N_FM // RING) as i:
                for j in range(RING):
                    arrived(pe, n_fm + j, i * 16)
                    feature_major(z_fm[4 * j], wblk(n_fm + j), hT, more=i * 3)
            ada(n_adab, N_ADA_B, y_modb)
            for t, (t0, w) in enumerate([(SEQ - PB, PB), (SEQ, NS)]):
                fill_wait(pe, 0, z_tail[t])
                for g in range(G):
                    last = pe.transpose(out(0, z_tail[t])[0:w, g * P:(g + 1) * P], zT[:, Z_U + g, t0:t0 + w], ident)
                done(last, 0, z_tail[t])
            pe.wait_ge(ld["wpg"], 16)
            for g in range(G):
                fill_wait(pe, 0, z_pg[g])
                pe.wait_ge(S_["pm"], g + 1)
                done(pe.matmul(out(0, z_pg[g])[:, 0:T], wpg[:, g, :], zT[:, Z_U + g, :], start=True, stop=True),
                     0, z_pg[g])
            pe.wait_ge(S_["rot"], 8)
            for t, (t0, w) in enumerate(TOK):
                fill_wait(pe, 0, z_kt[t])
                for h in range(G):
                    last = pe.transpose(out(0, z_kt[t])[0:w, h * P:(h + 1) * P], zT[:, Z_K + h, t0:t0 + w], ident)
                done(last, 0, z_kt[t])
            for n in z_v:
                drain_wait(pe, 0, n)
            for n in z_kt:
                drain_wait(pe, 0, n)

            def scores(h):
                n = y_sc[h]
                fill_wait(pe, 1, n)
                for t, (t0, w) in enumerate(TOK):
                    last = pe.matmul(out(1, n)[0:w, t0:t0 + w], zT[:, Z_K + h, t0:t0 + w], zT[:, Z_Q + h, t0:t0 + w],
                                     start=True, stop=True)
                done(last, 1, n)

            def state_step(n, h, c):
                fill_wait(pe, 1, n)
                done(pe.matmul(out(1, n)[:, 0:DV], ktok[:, c, h * P:(h + 1) * P], v[:, c, h * DV:(h + 1) * DV],
                               start=True, stop=True), 1, n)

            for h in range(G + 1):
                if h < G:
                    scores(h)
                    state_step(y_s0[h], h, 0)
                if h == 0:
                    pe.wait_ge(ld["state"], 16 * G)
                    pe.wait_ge(S_["qd_s"], G)
                    pe.wait_ge(S_["kbl"], 1)
                    continue
                g = h - 1
                drain_wait(pe, 1, y_sc[g])
                drain_wait(pe, 1, y_s0[g])
                for et in range(2):
                    n = z_o[g][et]
                    e0 = g * DV + et * P
                    o = out(0, n)
                    fill_wait(pe, 0, n)
                    pe.matmul(o[:, 0:P], v[:, 0, e0:e0 + P], sT[:, g % 2, 0:P], start=True, stop=True)
                    pe.matmul(o[:, P:SEQ], v[:, 1, e0:e0 + P], sT[:, g % 2, P:SEQ], start=True, stop=False)
                    pe.matmul(o[:, P:SEQ], SP0[:, g, et * P:(et + 1) * P], qd[:, g, 0:CHUNK], start=False, stop=True)
                    pe.matmul(o[:, SEQ:T], v[0:NS, 2, e0:e0 + P], sT[0:NS, g % 2, SEQ:T], start=True, stop=False,
                              skip_group_check=True)
                    for b in range(DEC_B):
                        c = CHUNK + b * DEC_L
                        last = pe.matmul(o[:, SEQ + b * DEC_L:SEQ + (b + 1) * DEC_L], S[:, g, b, et * P:(et + 1) * P],
                                         qd[:, g, c:c + DEC_L], start=False, stop=(b == DEC_B - 1),
                                         skip_group_check=True)
                    done(last, 0, n)
                state_step(y_s1[g], g, 1)
                for bp in range(DEC_B // 2):
                    n = y_ss[g][bp]
                    fill_wait(pe, 1, n)
                    for u in range(2):
                        last = pe.matmul(out(1, n)[:, u * DV:(u + 1) * DV], kblk[:, 2 * bp + u, g * P:(g + 1) * P],
                                         v[0:NS, 2, g * DV:(g + 1) * DV], start=True, stop=True)
                    done(last, 1, n)
            arrived(pe, n_bp)
            for n in z_pg:
                drain_wait(pe, 0, n)
            feature_major(z_a[0], ring[:, slot(n_bp), :].rearrange("p (k c) -> p k c", k=G), hT, kt=G, nf=KD)
            for h in range(G):
                pe.wait_ge(S_["osq"], h + 1)
                sums(1, y_hn[h], [hT[:, 4 + 2 * (h % 2) + et, :] for et in range(2)])
            pe.wait_ge(S_["gated"], G)
            for j in range(2):
                arrived(pe, n_br + j)
                feature_major(z_r[4 * j], wblk(n_br + j), zT[:, Z_G:Z_G + KD, :])
            pe.wait_ge(S_["merged"], KD)
            for j in range(2):
                arrived(pe, n_wo + j)
                feature_major(z_m[4 * j], wblk(n_wo + j), zT[:, Z_A:Z_A + KD, :])
            sums(1, y_n2, [zT[:, k, :] for k in range(KD)], S_["x1_sq"])
            pe.wait_ge(S_["h2"], 1)
            pe.wait_ge(ld["router"], 32)
            for t, (t0, w) in enumerate(TOK):
                fill_wait(pe, 1, y_rt[t])
                for k in range(KD):
                    last = pe.matmul(out(1, y_rt[t])[0:w, 0:E], hT[:, k, t0:t0 + w], wrt[:, k, :],
                                     start=(k == 0), stop=(k == KD - 1))
                done(last, 1, y_rt[t])

            def down(z0, w, hid, more=0):
                for t, (t0, rows) in enumerate(TOK):
                    for c in range(2):
                        n = z0 + 2 * t + c
                        fill_wait(pe, 0, n, more)
                        for f in range(2):
                            last = pe.matmul(out(0, n)[0:rows, :], hid[:, f, t0:t0 + rows],
                                             w[:, f, c * BC:(c + 1) * BC], start=(f == 0), stop=(f == 1))
                        done(last, 0, n)

            arrived(pe, n_sg, 16)
            feature_major(z_shu[0], wblk(n_sg), hT)
            arrived(pe, n_sd)
            drain_wait(pe, 0, z_shu[2])
            drain_wait(pe, 0, z_shu[3])
            down(z_shd[0], ring[:, slot(n_sd), 0:2 * D].rearrange("p (k c) -> p k c", k=2), zT[:, HID[1]:HID[1] + 2, :])
            with pe.Fori(0, E // 2) as i:
                for j in range(2):
                    z0 = z_exp + 10 * j
                    pe.wait_ge(exp_in[j], i * 32 + 32)
                    feature_major(z0, egu(j), hT, more=i * (LOOP_Z // 4))
                    pe.wait_ge(exp_din[j], i * 16 + 16)
                    drain_wait(pe, 0, z0 + 2, i * (LOOP_Z // 4))
                    drain_wait(pe, 0, z0 + 3, i * (LOOP_Z // 4))
                    down(z0 + 4, edown(j), zT[:, HID[j]:HID[j] + 2, :], more=i * (LOOP_Z // 4))
            for n in range(Z_END - 4, Z_END):
                drain_wait(pe, 0, n)
            for k in range(KD):
                fill_wait(pe, 0, z_f[k])
                for t, (t0, w) in enumerate(TOK):
                    last = pe.transpose(out(0, z_f[k])[:, t0:t0 + w], acc[0:w, t, k * P:(k + 1) * P], ident[0:w, 0:w])
                done(last, 0, z_f[k])
            sums(1, y_nf, [zT[:, k, :] for k in range(KD)], S_["x2_sq"])
            pe.wait_ge(S_["yT"], 1)
            for t, (t0, w) in enumerate(TOK):
                for c in range(2):
                    n = z_y[2 * t + c]
                    fill_wait(pe, 0, n)
                    for k in range(4):
                        last = pe.transpose(out(0, n)[0:w, k * P:(k + 1) * P], hT[:, 4 * c + k, t0:t0 + w], ident)
                    done(last, 0, n)

        @block.scalar
        def _(act):
            def copy(dst, src, **kw):
                return act.activation(dst, src, ACT.Copy, **kw)

            def src(r, n):
                return bank[bk(r, n)]

            def freed(ins, r, n):
                ins.then_inc(free[bk(r, n)], 1)

            def root(r, n, mean_of, dst):
                read_wait(act, r, n)
                act.wait_ge(S_["eps"], 1)
                freed(act.activation(dst, src(r, n)[:, 0:T], ACT.Sqrt, scale=1.0 / mean_of, bias=eps_col[:, 0:1]), r, n)

            for k in range(KD):
                read_wait(act, 0, z_x[k])
                freed(copy(xT[:, k, :], src(0, z_x[k])[:, 0:T]), 0, z_x[k])
            root(0, z_n1, D, rstd[:, :])
            for j in range(12):
                read_wait(act, 0, z_uqk[j])
                if j == 0:
                    act.wait_ge(S_["h1"], 1)
                freed(copy(zT[:, Z_U + j, :], src(0, z_uqk[j])[:, 0:T]), 0, z_uqk[j])
            for j in range(N_V):
                for t, (t0, w) in enumerate(TOK):
                    n = z_v[3 * j + t]
                    read_wait(act, 0, n)
                    freed(copy(v[0:w, t, j * BC:(j + 1) * BC], src(0, n)[0:w, :]), 0, n)
            read_wait(act, 0, z_pool)
            freed(copy(stT[:, :, :].rearrange("p g r -> p (g r)"), src(0, z_pool)[:, 0:480]), 0, z_pool)
            with act.Fori(0, 2) as i:
                for j in range(12):
                    n = z_fm[j]
                    read_wait(act, 0, n, i * 3)
                    freed(copy(zT[:, bass.ds(i * 12 + (Z_G + j), 1), :].rearrange("p a t -> p (a t)"),
                               src(0, n)[:, 0:T]), 0, n)
            for t, w in enumerate([PB, NS]):
                read_wait(act, 0, z_tail[t])
                freed(copy(ptail[0:w, t, :], src(0, z_tail[t])[0:w, :]), 0, z_tail[t])
            for n in z_fm[-4:]:
                drain_wait(act, 0, n)
            act.activation(zT[:, Z_A:Z_A + 16, :], zT[:, Z_A:Z_A + 16, :], ACT.Sigmoid).then_inc(S_["sig_ab"], 1)
            act.activation(zT[:, Z_G:Z_G + 8, :], zT[:, Z_G:Z_G + 8, :], ACT.Silu).then_inc(S_["silu_g"], 1)
            for g in range(G):
                read_wait(act, 0, z_pg[g])
                freed(act.activation(hT[:, g, :], src(0, z_pg[g])[:, 0:T], ACT.Copy,
                                     scale=vecT[:, V_PS + g:V_PS + g + 1]), 0, z_pg[g])
            for h in range(G):
                for et in range(2):
                    n = z_o[h][et]
                    read_wait(act, 0, n)
                    freed(copy(zT[:, (Z_Q, Z_K)[et] + h, :], src(0, n)[:, 0:T]), 0, n)
            for h in range(G):
                if h >= 2:
                    read_wait(act, 1, y_hn[h - 2])
                for et in range(2):
                    drain_wait(act, 0, z_o[h][et])
                    last = act.activation(hT[:, 4 + 2 * (h % 2) + et, :], zT[:, (Z_Q, Z_K)[et] + h, :], ACT.Square)
                last.then_inc(S_["osq"], 1)
            for h in range(G):
                root(1, y_hn[h], DV, zT[:, Z_U + h, :])
            root(1, y_n2, D, rstd[:, :])
            act.wait_ge(S_["router_set"], 1)
            for t, (t0, w) in enumerate(TOK):
                read_wait(act, 1, y_rt[t])
                freed(act.activation(sc_s[0:w, t, :], src(1, y_rt[t])[0:w, 0:E], ACT.Sigmoid), 1, y_rt[t])

            def gate_silu(z0, sg, more=0):
                for f in range(2):
                    read_wait(act, 0, z0 + f, more)
                    freed(act.activation(zT[:, sg + f, :], src(0, z0 + f)[:, 0:T], ACT.Silu), 0, z0 + f)

            gate_silu(z_shu[0], SG[1])
            with act.Fori(0, E // 2) as i:
                for j in range(2):
                    gate_silu(z_exp + 10 * j, SG[j], i * (LOOP_Z // 4))
            root(1, y_nf, D, rstd[:, :])
            for t, (t0, w) in enumerate(TOK):
                for c in range(2):
                    n = z_y[2 * t + c]
                    read_wait(act, 0, n)
                    freed(copy(xin[0:w, t, c * BC:(c + 1) * BC], src(0, n)[0:w, :]), 0, n)

        @block.vector
        def _(dve):
            chain = [0]

            def link(ins):
                chain[0] += 1
                ins.then_inc(dve_chain, 1)
                dve.wait_ge(dve_chain, chain[0])

            def src(r, n):
                return bank[bk(r, n)]

            def freed(ins, r, n):
                ins.then_inc(free[bk(r, n)], 1)

            def toks(ap):
                return ap.rearrange("p k (b l) -> p k b l", b=DEC_B)

            def modulate(g_at, shift, scale, sums_at):
                drain_wait(dve, *sums_at)
                link(dve.reciprocal(rstd[:, :], rstd[:, :]))
                link(dve.tensor_tensor(hT[:, :, :], xT[:, :, :], bcast(rstd[:, :], 1, KD), ALU.mult))
                link(dve.scalar_tensor_tensor(gs[:, :, :], modT[:, scale:scale + KD, :], 1.0,
                                              bcast(vecT[:, g_at:g_at + KD], 2, NSEQ), ALU.add, ALU.mult))
                for k in range(KD):
                    dve.tensor_scalar(hT[:, k, 0:SEQ], hT[:, k, 0:SEQ], gs[:, k, 0:1], modT[:, shift + k, 0:1],
                                      ALU.mult, ALU.add)
                hs = toks(hT[:, :, SEQ:T])
                link(dve.tensor_tensor(hs, hs, bcast(gs[:, :, 1:NSEQ], 3, DEC_L), ALU.mult))
                return dve.tensor_tensor(hs, hs, bcast(modT[:, shift:shift + KD, 1:NSEQ], 3, DEC_L), ALU.add)

            def mod_rows(y, j0, count):
                read_wait(dve, 1, y)
                freed(dve.tensor_tensor(modT[:, j0:j0 + count, :],
                                        src(1, y)[:, 0:count * NSEQ].rearrange("p (j s) -> p j s", s=NSEQ),
                                        bcast(vecT[:, V_ADA + j0:V_ADA + j0 + count], 2, NSEQ), ALU.add), 1, y)

            dve.memset(eps_col[:, :], EPS).then_inc(S_["eps"], 1)
            for k in range(KD):
                drain_wait(dve, 0, z_x[k])
                dve.tensor_tensor(zT[:, k, :], xT[:, k, :], xT[:, k, :], ALU.mult).then_inc(S_["xT_sq"], 1)
            read_wait(dve, 0, z_vec)
            link(dve.tensor_copy(vecT[:, :], src(0, z_vec)[:, 0:NV]))
            freed(dve.tensor_copy(cT[:, :, :], src(0, z_vec)[:, P:P + KD * NSEQ].rearrange("p (k s) -> p k s", s=NSEQ)),
                  0, z_vec)
            mod_rows(y_moda, 0, 2 * KD)
            drain_wait(dve, 1, y_moda)
            modulate(V_G1, 0, KD, (0, z_n1)).then_inc(S_["h1"], 1)
            rt = qd[:, :, :].rearrange("p h c -> p (h c)")
            for j in range(8):
                q = zT[:, Z_Q + j, :]
                read_wait(dve, 0, z_swap[j])
                dve.tensor_tensor(rt[:, 0:T], q, cst[:, C_COS:C_COS + T], ALU.mult)
                freed(dve.tensor_tensor(rt[:, T:2 * T], src(0, z_swap[j])[:, 0:T], cst[:, C_SIN:C_SIN + T], ALU.mult),
                      0, z_swap[j])
                drain_wait(dve, 0, z_swap[j])
                dve.tensor_tensor(q, rt[:, 0:T], rt[:, T:2 * T], ALU.add).then_inc(S_["rot"], 1)
                dve.wait_ge(S_["rot"], j + 1)
            for h in range(G):
                w = C_QDEC + h * (CHUNK + NS)
                dve.tensor_tensor(qd[:, h, :], zT[:, Z_Q + h, CHUNK:T], cst[:, w:w + CHUNK + NS], ALU.mult)\
                   .then_inc(S_["qd_s"], 1)
            link(dve.memset(extp[:, :, 0:PB], 0.0))
            dve.tensor_copy(extp[:, :, PB:LP], zT[:, Z_U:Z_U + G, 0:SEQ])
            for g in range(G):
                if g == 0:
                    drain_wait(dve, 0, z_pool)
                dve.tensor_copy(exts[:, g, :, 0:PB], stT[:, g, :].rearrange("p (b r) -> p b r", b=DEC_B))
                last = dve.tensor_copy(exts[:, g, :, PB:LS], zT[:, Z_U + g, SEQ:T].rearrange("p (b l) -> p b l", b=DEC_B))
            link(last)
            views = []
            for area_ in (sumA, sumB):
                views.append((area_[:, 0:G * LP].rearrange("p (g l) -> p g l", g=G),
                              area_[:, G * LP:PW].rearrange("p (g b l) -> p g b l", g=G, b=DEC_B)))
            prev = (extp, exts)
            for s in range(G):
                cur = views[s % 2]
                sh, lo = 1 << s, (2 << s) - 1
                dve.tensor_tensor(cur[0][:, s:G, lo:LP], prev[0][:, s:G, lo:LP], prev[0][:, s:G, lo - sh:LP - sh],
                                  ALU.add)
                for g in range(s, G):
                    last = dve.tensor_tensor(cur[1][:, g, :, lo:LS], prev[1][:, g, :, lo:LS],
                                             prev[1][:, g, :, lo - sh:LS - sh], ALU.add)
                link(last)
                prev = cur
            for t in range(2):
                read_wait(dve, 0, z_tail[t])
            for g in range(G):
                sp_, ss_ = views[g % 2]
                u = zT[:, Z_U + g, :]
                link(dve.tensor_tensor(sp_[:, g, PB:PB + 16], sp_[:, g, PB:PB + 16],
                                       cst[:, C_ICNT + 16 * g:C_ICNT + 16 * (g + 1)], ALU.mult))
                dve.tensor_tensor(u[:, 0:16], sp_[:, g, PB:PB + 16], u[:, 0:16], ALU.subtract)
                dve.scalar_tensor_tensor(u[:, 16:SEQ], sp_[:, g, PB + 16:LP], 1.0 / WINDOWS[g], u[:, 16:SEQ],
                                         ALU.mult, ALU.subtract)
                us = u[:, SEQ:T].rearrange("p (b l) -> p b l", b=DEC_B)
                dve.scalar_tensor_tensor(us, ss_[:, g, :, PB:LS], 1.0 / WINDOWS[g], us, ALU.mult, ALU.subtract)\
                   .then_inc(S_["pm"], 1)
            mod_rows(y_modb, 2 * KD, 4 * KD)
            drain_wait(dve, 1, y_modb)
            dve.wait_ge(S_["pm"], G)
            for t, (t0, w) in enumerate(TOK):
                read_wait(dve, 0, z_kt[t])
                dst, dec = (ktok[:, t, :], C_KDEC) if t < 2 else (ktoks, C_KDECS)
                last = dve.tensor_tensor(dst.rearrange("p (h d) -> p h d", h=G),
                                         src(0, z_kt[t])[0:w, :].rearrange("p (h d) -> p h d", h=G),
                                         bcast(cst[0:w, dec:dec + G], 2, P), ALU.mult)
                freed(last, 0, z_kt[t])
            drain_wait(dve, 0, z_kt[2])
            for b in range(DEC_B):
                last = dve.tensor_scalar(kblk[:, b, :], ktoks, cst[0:NS, C_ROWB + b:C_ROWB + b + 1], None, ALU.mult)
            last.then_inc(S_["kbl"], 1)

            def masked(h):
                n = y_sc[h]
                read_wait(dve, 1, n)
                dve.tensor_tensor(sT[:, h % 2, 0:SEQ].rearrange("p (c q) -> p c q", c=2),
                                  src(1, n)[:, 0:SEQ].rearrange("p (c q) -> p c q", c=2),
                                  bcast(cst[:, C_INTRA + h * P:C_INTRA + (h + 1) * P], 1, 2), ALU.mult)
                freed(dve.tensor_tensor(sT[0:NS, h % 2, SEQ:T], src(1, n)[0:NS, SEQ:T],
                                        cst[0:NS, C_INTRAS + h * NS:C_INTRAS + (h + 1) * NS], ALU.mult), 1, n)
                read_wait(dve, 1, y_s0[h])
                freed(dve.tensor_copy(SP0[:, h, :], src(1, y_s0[h])[:, 0:DV]), 1, y_s0[h])

            for h in range(G + 1):
                if h < G:
                    masked(h)
                if h > 0:
                    g = h - 1
                    read_wait(dve, 1, y_s1[g])
                    drain_wait(dve, 1, y_s0[g])
                    freed(dve.scalar_tensor_tensor(SP0[:, g, :], SP0[:, g, :], s_dec[g], src(1, y_s1[g])[:, 0:DV],
                                                   ALU.mult, ALU.add), 1, y_s1[g])
                    for bp in range(DEC_B // 2):
                        n = y_ss[g][bp]
                        read_wait(dve, 1, n)
                        st = S[:, g, 2 * bp:2 * bp + 2, :].rearrange("p b e -> p (b e)")
                        freed(dve.scalar_tensor_tensor(st, st, s_dec_s[g], src(1, n)[:, :], ALU.mult, ALU.add), 1, n)
            dve.wait_ge(S_["sig_ab"], 1)
            for j in range(KD):
                read_wait(dve, 0, z_a[j])
                a = zT[:, Z_A + j, :]
                freed(dve.tensor_tensor(a, a, src(0, z_a[j])[:, 0:T], ALU.mult), 0, z_a[j])
            dve.wait_ge(S_["silu_g"], 1)
            for h in range(G):
                drain_wait(dve, 1, y_hn[h])
                u = zT[:, Z_U + h, :]
                link(dve.reciprocal(u, u))
                gg = zT[:, Z_G + 2 * h:Z_G + 2 * h + 2, :]
                link(dve.tensor_tensor(gg, gg, bcast(u, 1, 2), ALU.mult))
                for et in range(2):
                    o = zT[:, (Z_Q, Z_K)[et] + h, :]
                    g_ = zT[:, Z_G + 2 * h + et, :]
                    last = dve.tensor_tensor(g_, g_, o, ALU.mult)
                last.then_inc(S_["gated"], 1)
            for j in range(KD):
                read_wait(dve, 0, z_r[j])
                b = zT[:, Z_B + j, :]
                freed(dve.tensor_tensor(b, b, src(0, z_r[j])[:, 0:T], ALU.mult), 0, z_r[j])
                drain_wait(dve, 0, z_r[j])
                drain_wait(dve, 0, z_a[j])
                dve.tensor_tensor(zT[:, Z_A + j, :], zT[:, Z_A + j, :], b, ALU.add).then_inc(S_["merged"], 1)

            def residual(z, k, gate, last_sem):
                read_wait(dve, 0, z)
                m = src(0, z)
                tmp = zT[:, 8 + k, SEQ:T]
                dve.scalar_tensor_tensor(xT[:, k, 0:SEQ], m[:, 0:SEQ], modT[:, gate + k, 0:1], xT[:, k, 0:SEQ],
                                         ALU.mult, ALU.add)
                freed(dve.tensor_tensor(tmp.rearrange("p (b l) -> p b l", b=DEC_B),
                                        m[:, SEQ:T].rearrange("p (b l) -> p b l", b=DEC_B),
                                        bcast(modT[:, gate + k, 1:NSEQ], 2, DEC_L), ALU.mult), 0, z)
                drain_wait(dve, 0, z)
                link(dve.tensor_tensor(xT[:, k, SEQ:T], xT[:, k, SEQ:T], tmp, ALU.add))
                dve.tensor_tensor(zT[:, k, :], xT[:, k, :], xT[:, k, :], ALU.mult).then_inc(last_sem, 1)

            for k in range(KD):
                residual(z_m[k], k, 2 * KD, S_["x1_sq"])
            modulate(V_G2, 3 * KD, 4 * KD, (1, y_n2)).then_inc(S_["h2"], 1)

            dve.memset(sc_s[:, :, :], 0.5).then_inc(S_["router_set"], 1)
            for t in range(3):
                drain_wait(dve, 1, y_rt[t])
            dve.wait_ge(ld["router"], 32)
            dve.memset(gsc[:, :, 8:12], LOW)
            dve.memset(etop[:, :, :], LOW)
            link(dve.tensor_tensor(sc_b, sc_s, bcast(brow[:, :], 1, 3), ALU.add))
            for t in range(3):
                for g in range(NG):
                    last = dve.max(gtop[:, t, g, :], sc_b[:, t, g * EG:(g + 1) * EG])
            link(last)
            link(dve.tensor_tensor(gsc[:, :, 0:NG], gtop[:, :, :, 0], gtop[:, :, :, 1], ALU.add))
            for t in range(3):
                last = dve.max(gsort[:, t, :], gsc[:, t, 0:NG])
            link(last)
            link(dve.tensor_copy(etop[:, :, 0:4], gsort[:, :, 0:4]))
            for t in range(3):
                last = dve.match_replace(grep[:, t, :], etop[:, t, :], gsc[:, t, :], 2 * LOW)
            link(last)
            link(dve.tensor_scalar(gmask, grep[:, :, 0:NG], 1.5 * LOW, None, ALU.is_le))
            link(dve.tensor_scalar(gfill, gmask, 1.0, -LOW, ALU.subtract, ALU.mult))
            by_group = lambda ap: ap.rearrange("p t (g e) -> p (t g) e", g=NG)
            one = lambda ap: bcast(ap.rearrange("p t g -> p (t g)"), 2, EG)
            link(dve.tensor_tensor(by_group(sc_m), by_group(sc_b), one(gmask), ALU.mult))
            link(dve.tensor_tensor(by_group(sc_m), by_group(sc_m), one(gfill), ALU.add))
            for t in range(3):
                last = dve.max(etop[:, t, :], sc_m[:, t, :])
            link(last)
            for t in range(3):
                last = dve.match_replace(sc_r[:, t, :], etop[:, t, :], sc_m[:, t, :], 2 * LOW)
            link(last)
            link(dve.scalar_tensor_tensor(gates, sc_r, 1.5 * LOW, sc_s, ALU.is_le, ALU.mult))
            link(dve.tensor_reduce(wsum, gates, AX_X, ALU.add))
            link(dve.reciprocal(winv, wsum))
            link(dve.tensor_scalar(winv, winv, SCALE_OUT, None, ALU.mult))
            link(dve.tensor_tensor(gates, gates, bcast(winv, 2, E), ALU.mult))

            def hidden(z0, sg, hid, more=0):
                for f in range(2):
                    drain_wait(dve, 0, z0 + f, more)
                    read_wait(dve, 0, z0 + 2 + f, more)
                    freed(dve.tensor_tensor(zT[:, hid + f, :], zT[:, sg + f, :], src(0, z0 + 2 + f)[:, 0:T], ALU.mult),
                          0, z0 + 2 + f)

            hidden(z_shu[0], SG[1], HID[1])
            for t, (t0, w) in enumerate(TOK):
                for c in range(2):
                    n = z_shd[2 * t + c]
                    read_wait(dve, 0, n)
                    freed(dve.tensor_copy(acc[0:w, t, c * BC:(c + 1) * BC], src(0, n)[0:w, :]), 0, n)
            with dve.Fori(0, E // 2) as i:
                for j in range(2):
                    z0 = z_exp + 10 * j
                    hidden(z0, SG[j], HID[j], i * (LOOP_Z // 4))
                    for t, (t0, w) in enumerate(TOK):
                        for c in range(2):
                            n = z0 + 4 + 2 * t + c
                            read_wait(dve, 0, n, i * (LOOP_Z // 4))
                            a = acc[0:w, t, c * BC:(c + 1) * BC]
                            freed(dve.scalar_tensor_tensor(a, src(0, n)[0:w, :],
                                                           gates[0:w, t, bass.ds(i * 2 + j, 1)],
                                                           a, ALU.mult, ALU.add), 0, n)
            for k in range(KD):
                residual(z_f[k], k, 5 * KD, S_["x2_sq"])
            drain_wait(dve, 1, y_nf)
            link(dve.reciprocal(rstd[:, :], rstd[:, :]))
            link(dve.tensor_tensor(hT[:, :, :], xT[:, :, :], bcast(rstd[:, :], 1, KD), ALU.mult))
            dve.tensor_tensor(hT[:, :, :], hT[:, :, :], bcast(vecT[:, V_GF:V_GF + KD], 2, T), ALU.mult)\
               .then_inc(S_["yT"], 1)


_INS = ["x_prompt", "x_sample", "c_prompt", "c_sample", "state_pool", "state_ret", "w_ada", "b_ada", "g_norm1",
        "w_in", "w_pool_group", "pool_scale", "w_branch_pool", "w_branch_ret", "w_out", "g_norm2", "w_router",
        "b_router", "w_exp_gate", "w_exp_up", "w_exp_down", "w_sh_gate", "w_sh_up", "w_sh_down", "g_final"]
_OUTS = [(1, SEQ, D), (DEC_B, DEC_L, D), (1, 1, PB, 512), (1, 1, G, P, DV), (1, DEC_B, PB, 512), (1, DEC_B, G, P, DV)]


def kernel(**inputs):
    import concourse.bacc as bacc
    from concourse.bass_utils import run_bass_kernel_spmd

    nc = bacc.Bacc("TRN2", target_bir_lowering=False, num_devices=1)
    arrays = {"consts": shape_constants()}
    args = [nc.dram_tensor("consts", arrays["consts"].shape, F32, kind="ExternalInput").ap()]
    for name in _INS:
        arrays[f"in_{name}"] = np.ascontiguousarray(inputs[name])
        args.append(nc.dram_tensor(f"in_{name}", arrays[f"in_{name}"].shape, F32, kind="ExternalInput").ap())
    for i, shape in enumerate(_OUTS):
        args.append(nc.dram_tensor(f"out_{i}", shape, F32, kind="ExternalOutput").ap())
    build(nc, *args)
    r = run_bass_kernel_spmd(nc, [arrays], core_ids=[0])
    return tuple(r.results[0][f"out_{i}"] for i in range(len(_OUTS)))
```

```python
from contextlib import ExitStack

import numpy as np
import concourse.bass as bass
from concourse import mybir

ALU = mybir.AluOpType
ACT = mybir.ActivationFunctionType
F32 = mybir.dt.float32
F32R = mybir.dt.float32r
I32 = mybir.dt.int32
AX_X = mybir.AxisListType.X

P = 128
D = 1024
KD = D // P
SEQ, DEC_B, DEC_L = 256, 8, 4
NS = DEC_B * DEC_L
T = SEQ + NS
TOK = [(0, P), (P, P), (SEQ, NS)]
PAST = 2048
WINDOWS = (2, 4, 8, 16)
PB = 15
G = 4
DV = 256
CHUNK = 128
NMOD = 6
NSEQ = 1 + DEC_B
E = 64
NG, EG = 8, 8
DE = 256
SCALE_OUT = 2.5
EPS = 1e-6
BC = 512
RING = 3
LOW = -1e30

C_ID, C_SWAP, C_ONES = 0, P, 2 * P
C_COS = 3 * P
C_SIN = C_COS + T
C_INTRA = C_SIN + T
C_QDEC = C_INTRA + G * P
C_INTRAS = C_QDEC + G * (CHUNK + NS)
C_ICNT = C_INTRAS + G * NS
C_KDEC = C_ICNT + G * 16
C_KDECS = C_KDEC + G
C_ROWB = C_KDECS + G
C_UP = C_ROWB + DEC_B
C_SLOT = C_UP + P
C_ENUM = C_SLOT + 64
C_OVER = C_ENUM + 1
C_FULL = C_OVER + 40
C_QUAD = C_FULL + 4
NC_COLS = C_QUAD + 9

C = 64
KEY0 = 1000.0
MAX_OVER = 36
NCH = E + 40
MIN_Q, MAX_Q = E // 4, (E + MAX_OVER) // 4

Z_U, Z_Q, Z_K, Z_G, Z_A, Z_B = 0, 4, 8, 12, 20, 28
NZ = 36

V_ADA, V_G1, V_G2, V_GF, V_PS = 0, 48, 56, 64, 72
NV = 76


def log_decays():
    f = np.float32
    return np.log(f(1.0) - np.power(f(2.0), f(-5.0) - np.arange(G, dtype=f))).astype(f)


def shape_constants():
    c = np.zeros((P, NC_COLS), np.float64)
    c[:, C_ID:C_ID + P] = np.eye(P)
    c[:, C_SWAP:C_SWAP + P] = np.roll(np.eye(P), P // 2, axis=0)
    c[:, C_ONES:C_ONES + P] = 1.0
    f = np.float32
    inv = np.power(f(10000.0), -np.arange(64, dtype=f) / f(64)).astype(f)
    pos = np.concatenate([np.arange(SEQ), np.tile(PAST + np.arange(DEC_L), DEC_B)]).astype(f)
    ang = (np.concatenate([inv, inv])[:, None] * pos[None, :]).astype(f).astype(np.float64)
    c[:, C_COS:C_COS + T] = np.cos(ang)
    c[:, C_SIN:C_SIN + T] = np.sin(ang) * np.where(np.arange(P) < 64, -1.0, 1.0)[:, None]
    lg = log_decays().astype(np.float64)
    ks = P ** -0.5
    m, q = np.arange(P)[:, None], np.arange(P)[None, :]
    ms, qs = np.arange(NS)[:, None], np.arange(NS)[None, :]
    for h in range(G):
        c[:, C_INTRA + h * P:C_INTRA + (h + 1) * P] = np.where(q >= m, np.exp(lg[h] * np.maximum(q - m, 0)), 0) * ks
        c[:NS, C_INTRAS + h * NS:C_INTRAS + (h + 1) * NS] = np.where(
            (qs >= ms) & (qs // DEC_L == ms // DEC_L), np.exp(lg[h] * np.maximum(qs - ms, 0)), 0) * ks
        w = C_QDEC + h * (CHUNK + NS)
        c[:, w:w + CHUNK] = np.exp(lg[h] * (np.arange(CHUNK) + 1.0))[None, :]
        c[:, w + CHUNK:w + CHUNK + NS] = np.exp(lg[h] * (np.arange(NS) % DEC_L + 1.0))[None, :]
        c[:, C_KDEC + h] = np.exp(lg[h] * (CHUNK - 1.0 - np.arange(P))) * ks
        c[:NS, C_KDECS + h] = np.exp(lg[h] * (DEC_L - 1.0 - np.arange(NS) % DEC_L)) * ks
        c[:, C_ICNT + h * 16:C_ICNT + (h + 1) * 16] = 1.0 / np.minimum(WINDOWS[h], np.arange(16) + 1.0)[None, :]
    for b in range(DEC_B):
        c[b * DEC_L:(b + 1) * DEC_L, C_ROWB + b] = 1.0
    c[:, C_UP:C_UP + P] = m < q
    c[:, C_SLOT:C_SLOT + C] = KEY0 + np.arange(C)
    c[:, C_ENUM] = np.arange(P)
    c[:, C_OVER:C_OVER + 40] = np.arange(40)
    c[:, C_FULL:C_FULL + 4] = C * (1 + np.arange(4))
    c[:, C_QUAD:C_QUAD + 9] = 4 * np.arange(9)
    return c.astype(np.float32)


def bcast(ap, at, n):
    wide = ap.unsqueeze(at)
    shape = list(wide.shape)
    shape[at] = n
    return wide.broadcast_to(shape)


def build(nc, consts, x_prompt, x_sample, c_prompt, c_sample, state_pool, state_ret, w_ada, b_ada, g_norm1,
          w_in, w_pool_group, pool_scale, w_branch_pool, w_branch_ret, w_out, g_norm2, w_router, b_router,
          w_exp_gate, w_exp_up, w_exp_down, w_sh_gate, w_sh_up, w_sh_down, g_final,
          y_prompt, y_sample, new_pool_prompt, new_ret_prompt, new_pool_sample, new_ret_sample):
    lg = log_decays().astype(np.float64)
    s_dec = [float(np.exp(v * CHUNK)) for v in lg]
    s_dec_s = [float(np.exp(v * DEC_L)) for v in lg]

    with ExitStack() as ctx:
        def sb(name, shape):
            return ctx.enter_context(nc.sbuf_tensor(name, shape, F32))

        def sb_r(name, shape):
            return ctx.enter_context(nc.sbuf_tensor(name, shape, F32R))

        def sem(name):
            return ctx.enter_context(nc.semaphore(name))

        xT = sb("xT", [P, KD, T])
        hT = sb("hT", [P, KD, T])
        cst = sb("cst", [P, NC_COLS])
        modT = sb("modT", [P, NMOD * KD, NSEQ])
        vecT = sb("vecT", [P, NV])
        cT = sb("cT", [P, KD, NSEQ])
        gs = sb("gs", [P, KD, NSEQ])
        rstd = sb("rstd", [P, T])
        wpg = sb("wpg", [P, G, P])
        wrt = sb("wrt", [P, KD, E])
        brow = sb("brow", [P, E])
        eps_col = sb("eps_col", [P, 1])

        mixer = ExitStack()

        def mb(name, shape):
            return mixer.enter_context(nc.sbuf_tensor(name, shape, F32))

        ring = mb("ring", [P, RING, KD * BC])
        S = mb("S", [P, G, DEC_B, DV])
        scratch = mb("scratch", [P, 5100])
        v = mb("v", [P, 3, D])
        zT = mb("zT", [P, NZ, T])
        SP0 = mb("SP0", [P, G, DV])
        ktok = mb("ktok", [P, 2, G * P])
        qd = mb("qd", [P, G, CHUNK + NS])
        sT = mb("sT", [P, 2, T])
        stT = mb("stT", [P, G, DEC_B * PB])
        ptail = mb("ptail", [NS, 2, G * P])
        mixer.close()

        W_GU = KD * 2 * DE
        wexp = [sb(f"wexp{j}", [P, W_GU + 2 * D]) for j in range(3)]
        yh = sb_r("yh", [P, D])
        yl = sb_r("yl", [P, D])
        wexp.append(sb("wexp3", [P, W_GU + 2 * D]))
        yT = sb("yT", [P, KD, 2 * C])
        xsel = [sb(f"xsel{j}", [P, KD, 2 * C]) for j in range(2)]
        xh = sb_r("xh", [P, 2, D])
        xl = sb_r("xl", [P, 2, D])
        xs = sb_r("xs", [2 * NS, D])
        oh = sb_r("oh", [P, 3, 2 * C])
        ohg = sb("ohg", [P, 3, 2 * C])
        pt = [sb_r(f"pt{j}", [P, T]) for j in range(2)]
        gslot = [sb(f"gslot{j}", [P, 1]) for j in range(2)]
        hid = sb("hid", [P, 2, 2 * C])
        sg = sb("sg", [P, 2, 2 * C])
        hidS = sb("hidS", [P, 2, T])
        sgS = sb("sgS", [P, 2, T])
        rwork = sb("rwork", [P, 1800])
        keyT = sb("keyT", [E, T + NS])
        gateT = sb("gateT", [E, T])
        selc = sb("selc", [E, NCH])
        selb = sb("selb", [E, NCH])
        ework = sb("ework", [E, 64])
        keyc = sb("keyc", [P, 3, NCH])
        gatec = sb("gatec", [P, 3, NCH])
        ids = ctx.enter_context(nc.sbuf_tensor("ids", [1, NCH], I32))
        nquads = ctx.enter_context(nc.sbuf_tensor("nquads", [1, 1], I32))
        acc = hT
        ystage = wexp[0][:, 0:3 * D].rearrange("p (t d) -> p t d", t=3)

        ident = cst[:, C_ID:C_ID + P]
        swap = cst[:, C_SWAP:C_SWAP + P]
        ones = cst[:, C_ONES:C_ONES + P]
        xin = scratch[:, 0:3 * D].rearrange("p (t d) -> p t d", t=3)
        vrow = scratch[:, 3072:3072 + P]
        crow = scratch[0:NSEQ, 3200:3200 + D]
        prow = scratch[0:DEC_B * PB, 4224:4224 + 512]
        LP, LS = SEQ + PB, DEC_L + PB
        PW = G * LP + G * DEC_B * LS
        extp = scratch[:, 0:G * LP].rearrange("p (g l) -> p g l", g=G)
        exts = scratch[:, G * LP:PW].rearrange("p (g b l) -> p g b l", g=G, b=DEC_B)
        sumA = scratch[:, PW:2 * PW]
        sumB = scratch[:, 2 * PW:3 * PW]
        assert 3 * PW <= 5100
        arow = ktok[0:NSEQ, :, :]
        kblk = scratch[0:NS, 0:DEC_B * G * P].rearrange("p (b n) -> p b n", b=DEC_B)
        ktoks = scratch[0:NS, 4096:4096 + G * P]

        bank = [ctx.enter_context(nc.psum_tensor(f"bank{i}", [P, 512], F32)) for i in range(8)]
        ready = [sem(f"ready{i}") for i in range(8)]
        free = [sem(f"free{i}") for i in range(8)]

        class Tiles:
            def __init__(self):
                self.n = 0

            def take(self, k=1):
                a = self.n
                self.n += k
                return a if k == 1 else range(a, a + k)

        def bk(ringno, n):
            return ringno * 4 + n % 4

        def fill_wait(pe, r, n, more=0):
            if isinstance(more, int) and n + 4 * more < 4:
                return
            pe.wait_ge(free[bk(r, n)], n // 4 + more)

        def read_wait(eng, r, n, more=0):
            eng.wait_ge(ready[bk(r, n)], n // 4 + 1 + more)

        def drain_wait(eng, r, n, more=0):
            eng.wait_ge(free[bk(r, n)], n // 4 + 1 + more)

        Z, Y = Tiles(), Tiles()
        z_x = Z.take(KD)
        z_vec = Z.take()
        z_n1 = Z.take()
        z_ara = Z.take(4)
        y_moda = Y.take()
        z_uqk = Z.take(12)
        z_swap = Z.take(8)
        z_v = Z.take(6)
        z_pool = Z.take()
        z_fm = Z.take(24)
        z_arb = Z.take(8)
        y_modb = Y.take()
        z_tail = Z.take(2)
        z_pg = Z.take(4)
        z_kt = Z.take(3)
        y_sc, y_s0, y_s1, y_ss, z_o = [], [], [], [], []
        for h in range(G + 1):
            if h < G:
                y_sc.append(Y.take())
                y_s0.append(Y.take())
            if h > 0:
                z_o.append(Z.take(2))
                y_s1.append(Y.take())
                y_ss.append(Y.take(4))
        z_a = Z.take(KD)
        y_hn = Y.take(4)
        z_r = Z.take(KD)
        z_m = Z.take(KD)
        y_n2 = Y.take()
        Z_END, Y_END = Z.n, Y.n

        mready = [sem(f"mready{i}") for i in range(8)]
        mfree = [sem(f"mfree{i}") for i in range(8)]
        M = Tiles()
        m_rt = M.take(3)
        m_sgu = M.take(4)
        m_rank = M.take()
        m_hx = M.take(6)
        m_keyT = M.take()
        m_gateT = M.take()
        m_sd = M.take(KD)
        m_ob = M.take()
        m_ids = M.take()
        m_keyc = M.take()
        m_gatec = M.take()
        m_a0 = M.take(2)
        M_B, M_T, M_D, M_A, M_C, M_E, M_PAIR = 0, 1, 2, 4, 6, 8, 16
        m_loop = M.n
        m_dl = M.take(2)
        m_el = M.take(KD)
        m_nf = M.take()
        m_y = M.take(6)

        def m_fill_wait(pe, n, more=0):
            if n >= 8:
                pe.wait_ge(mfree[n % 8], n // 8 + more)

        def m_read_wait(eng, n, more=0):
            eng.wait_ge(mready[n % 8], n // 8 + 1 + more)

        def m_drain_wait(eng, n, more=0):
            eng.wait_ge(mfree[n % 8], n // 8 + 1 + more)

        ld = {k: sem(f"loaded_{k}") for k in ("consts", "x", "small", "pool", "state", "wpg", "router")}
        ring_in = [sem(f"ring_in{i}") for i in range(RING)]
        stored = sem("stored")
        S_ = {}
        for name in ("eps", "arow_t", "xT_sq", "h1", "rot", "qd_s", "pm", "kbl", "osq", "sig_ab", "silu_g",
                     "gated", "merged", "x1_sq", "h2", "router_set", "x2_sq", "yT", "gates_s", "yh_s", "sg_s",
                     "sel_s", "no_s", "chunks_s", "tables_s", "oh_s", "ohg_s", "zero_s", "pt_s"):
            S_[name] = sem(name)
        dve_chain = sem("dve_chain")

        N_ADA_A, N_UQK, N_V, N_FM, N_ADA_B = 4, 3, 2, 6, 8
        n_uqk = N_ADA_A
        n_v = n_uqk + N_UQK
        n_fm = n_v + N_V
        n_adab = n_fm + N_FM
        n_bp = n_adab + N_ADA_B
        n_br = n_bp + 1
        n_wo = n_br + 2
        n_end = n_wo + 2

        last_fill = {n_bp: (0, z_a[-1])}
        last_fill.update({j: (0, z_ara[j]) for j in range(N_ADA_A)})
        last_fill.update({n_adab + j: (0, z_arb[j]) for j in range(N_ADA_B)})
        last_fill.update({n_uqk + j: (0, z_uqk[4 * j + 3]) for j in range(N_UQK)})
        last_fill.update({n_v + j: (0, z_v[3 * j + 2]) for j in range(N_V)})
        last_fill.update({n_fm + j: (0, z_fm[4 * j + 3]) for j in range(N_FM)})
        last_fill.update({n_br + j: (0, z_r[4 * j + 3]) for j in range(2)})
        last_fill.update({n_wo + j: (0, z_m[4 * j + 3]) for j in range(2)})

        def slot(n):
            return n % RING

        def wblk(n):
            return ring[:, slot(n), :].rearrange("p (k c) -> p k c", k=KD)

        def arrived(pe, n, more=0):
            pe.wait_ge(ring_in[slot(n)], 16 * (n // RING + 1) + more)

        def cols(w, c0):
            return w.rearrange("(k p) c -> p k c", p=P)[:, :, bass.ds(c0, BC)]

        win, wada = w_in[0], w_ada[0]

        gu_in = [sem(f"gu_in{j}") for j in range(4)]
        dn_in = [sem(f"dn_in{j}") for j in range(4)]

        def w_gate_up(j):
            return wexp[j][:, 0:W_GU].rearrange("p (m k f) -> p m k f", m=2, k=KD)

        def w_down(j):
            return wexp[j][:, W_GU:W_GU + 2 * D].rearrange("p (f d) -> p f d", f=2)

        rat = [0]

        def part(n):
            rat[0] += n
            return rwork[:, rat[0] - n:rat[0]]

        def by_token(n):
            return part(3 * n).rearrange("p (t e) -> p t e", t=3)

        sc_s, sc_b, sc_m, sc_r, gates, sel, keys = (by_token(E) for _ in range(7))
        gtop = part(3 * NG * 8).rearrange("p (t g e) -> p t g e", t=3, g=NG)
        gsc, grep = by_token(12), by_token(12)
        gsort, gmask, gfill, etop = (by_token(8) for _ in range(4))
        wsum, winv = part(3), part(3)
        e_cnt, e_no, e_ob = ework[:, 0:1], ework[:, 1:2], ework[:, 2:3]
        e_full = ework[:, 4:8]
        sgE = sgS[0:E, 0, :]
        oE = ework[:, 22:62]
        sq2 = wexp[1][:, 0:KD * T].rearrange("p (k t) -> p k t", k=KD)
        q_full, q_n = ework[0:1, 8:17], ework[0:1, 18:19]
        N_FRONT_STORES = 1 + 2 + 1 + G

        block = ctx.enter_context(nc.Block())

        def load_turns(eng):
            eng.wait_ge(S_["chunks_s"], 1)
            return eng.value_load(nquads[0:1, 0:1], min_val=MIN_Q, max_val=MAX_Q)

        @block.sync
        def _(sp):
            sp.dma_start(xin[:, 0:2, :], x_prompt[0].rearrange("(t p) d -> p t d", p=P)).then_inc(ld["x"], 16)
            sp.dma_start(xin[0:NS, 2, :], x_sample.rearrange("b l d -> (b l) d")).then_inc(ld["x"], 16)
            sp.dma_start(cst[:, :], consts).then_inc(ld["consts"], 16)
            sp.dma_start(crow[0:1, :], c_prompt).then_inc(ld["small"], 16)
            sp.dma_start(crow[1:NSEQ, :], c_sample).then_inc(ld["small"], 16)
            for row, src, n in ((V_ADA, b_ada, 48), (V_G1, g_norm1, 8), (V_G2, g_norm2, 8), (V_PS, pool_scale, 4)):
                sp.dma_start(vrow[row:row + n, :], src[0].rearrange("(r c) -> r c", c=P)).then_inc(ld["small"], 16)
            sp.dma_start(vrow[V_GF:V_GF + 8, :], g_final.rearrange("(r c) -> r c", c=P)).then_inc(ld["small"], 16)

            def used(n):
                read_wait(sp, *last_fill[n])

            def stream(n, src):
                if n >= RING:
                    used(n - RING)
                sp.dma_start(wblk(n), src).then_inc(ring_in[slot(n)], 16)

            def load_expert(j, wg, wu, wd):
                sp.dma_start(w_gate_up(j)[:, 0], wg).then_inc(gu_in[j], 16)
                sp.dma_start(w_gate_up(j)[:, 1], wu).then_inc(gu_in[j], 16)
                sp.dma_start(w_down(j), wd).then_inc(dn_in[j], 16)

            def routed(e):
                return (w_exp_gate[0, bass.ds(e, 1)].rearrange("a (k p) f -> p (a k) f", p=P),
                        w_exp_up[0, bass.ds(e, 1)].rearrange("a (k p) f -> p (a k) f", p=P),
                        w_exp_down[0, bass.ds(e, 1)].rearrange("a (f p) d -> p (a f) d", p=P))

            for j in range(N_ADA_A):
                stream(j, cols(wada, BC * j))
            sp.dma_start(prow, state_pool[0].rearrange("b r c -> (b r) c")).then_inc(ld["pool"], 16)
            for j in range(N_UQK + N_V):
                stream(n_uqk + j, cols(win, BC * j))
            sp.dma_start(wpg[:, :, :], w_pool_group[0].rearrange("g c d -> c g d")).then_inc(ld["wpg"], 16)
            sp.dma_start(wrt[:, :, :], w_router[0].rearrange("(k p) e -> p k e", p=P)).then_inc(ld["router"], 16)
            sp.dma_start(brow[:, :], bcast(b_router[0], 0, P)).then_inc(ld["router"], 16)
            for j in range(N_FM):
                stream(n_fm + j, cols(win, BC * (N_UQK + N_V + j)))
            for h in range(G):
                sp.dma_start(S[:, h, :, :], state_ret[0, :, h].rearrange("b d e -> d b e")).then_inc(ld["state"], 16)
            sp.dma_start(new_pool_sample[0, :, 0:PB - DEC_L, :], state_pool[0, :, DEC_L:PB, :]).then_inc(stored, 16)
            for j in range(N_ADA_B):
                stream(n_adab + j, cols(wada, BC * (N_ADA_A + j)))
            used(n_bp - RING)
            sp.dma_start(ring[:, slot(n_bp), :].rearrange("p (k c) -> p k c", k=G),
                         w_branch_pool[0].rearrange("(k p) c -> p k c", p=P)).then_inc(ring_in[slot(n_bp)], 16)
            for n in z_tail:
                drain_wait(sp, 0, n)
            sp.dma_start(new_pool_prompt[0, 0], ptail[0:PB, 0, :]).then_inc(stored, 16)
            sp.dma_start(new_pool_sample[0, :, PB - DEC_L:PB, :],
                         ptail[0:NS, 1, :]).then_inc(stored, 16)
            for j in range(2):
                stream(n_br + j, cols(w_branch_ret[0], BC * j))
            read_wait(sp, 0, z_o[-1][1])
            read_wait(sp, 1, y_ss[-1][3])
            load_expert(3, w_sh_gate[0].rearrange("(k p) f -> p k f", p=P), w_sh_up[0].rearrange("(k p) f -> p k f", p=P),
                        w_sh_down[0].rearrange("(f p) d -> p f d", p=P))
            for j in range(2):
                stream(n_wo + j, cols(w_out[0], BC * j))
            drain_wait(sp, 1, y_s1[G - 1])
            sp.dma_start(new_ret_prompt[0, 0].rearrange("h d e -> d h e"), SP0[:, :, :]).then_inc(stored, 16)
            for h in range(G):
                for n in y_ss[h]:
                    drain_wait(sp, 1, n)
                sp.dma_start(new_ret_sample[0, :, h].rearrange("b d e -> d b e"), S[:, h, :, :]).then_inc(stored, 16)

            sp.wait_ge(stored, 16 * N_FRONT_STORES)
            load_expert(2, *routed(2))
            for n in range(n_end - RING, n_end):
                used(n)
            load_expert(0, *routed(0))
            load_expert(1, *routed(1))
            m_read_wait(sp, m_sgu[3])
            m_read_wait(sp, m_sd[-1])
            load_expert(3, *routed(3))
            turns = load_turns(sp)
            with sp.Fori(1, turns) as q:
                for pair in range(2):
                    experts = []
                    m_read_wait(sp, m_loop + pair * M_PAIR + M_B, (q - 1) * 4)
                    for j in (2 * pair, 2 * pair + 1):
                        experts.append(sp.value_load(ids[0:1, bass.ds(q * 4 + j, 1)], min_val=0, max_val=E - 1))
                        wg, wu, _ = routed(experts[-1])
                        sp.dma_start(w_gate_up(j)[:, 0], wg).then_inc(gu_in[j], 16)
                        sp.dma_start(w_gate_up(j)[:, 1], wu).then_inc(gu_in[j], 16)
                    m_read_wait(sp, m_loop + pair * M_PAIR + M_C + 1, (q - 1) * 4)
                    for j in (2 * pair, 2 * pair + 1):
                        sp.dma_start(w_down(j), routed(experts[j % 2])[2]).then_inc(dn_in[j], 16)
            for n in m_y:
                m_drain_wait(sp, n, turns * 4)
            sp.dma_start(y_prompt[0].rearrange("(t p) d -> p t d", p=P), ystage[:, 0:2, :]).then_inc(stored, 16)
            sp.dma_start(y_sample.rearrange("b l d -> (b l) d"), ystage[0:NS, 2, :]).then_inc(stored, 16)
            sp.wait_ge(stored, 16 * (N_FRONT_STORES + 2))

        @block.tensor
        def _(pe):
            def done(ins, r, n):
                ins.then_inc(ready[bk(r, n)], 1)

            def out(r, n):
                return bank[bk(r, n)]

            def sums(r, n, rows, arrive=None):
                fill_wait(pe, r, n)
                for k, row in enumerate(rows):
                    if arrive is not None:
                        pe.wait_ge(arrive, k + 1)
                    last = pe.matmul(out(r, n)[:, 0:T], ones, row, start=(k == 0), stop=(k == len(rows) - 1))
                done(last, r, n)

            def ada(n0, z, y):
                fill_wait(pe, 1, y)

                def turn(j):
                    drain_wait(pe, 0, z[j])
                    for f in range(4):
                        c = (4 * j + f) * NSEQ
                        last = pe.transpose(out(1, y)[:, c:c + NSEQ], arow[:, j % 2, f * P:(f + 1) * P],
                                            ident[0:NSEQ, 0:NSEQ])
                    return last

                for j in range(len(z)):
                    arrived(pe, n0 + j)
                    fill_wait(pe, 0, z[j])
                    for k in range(KD):
                        last = pe.matmul(out(0, z[j])[0:NSEQ, :], cT[:, k, :], wblk(n0 + j)[:, k, :],
                                         start=(k == 0), stop=(k == KD - 1))
                    done(last, 0, z[j])
                    if j > 0:
                        turn(j - 1).then_inc(S_["arow_t"], 1)
                done(turn(len(z) - 1), 1, y)

            def feature_major(z0, w, srcT, kt=KD, nf=4, more=0):
                for f in range(nf):
                    fill_wait(pe, 0, z0 + f, more)
                    for k in range(kt):
                        last = pe.matmul(out(0, z0 + f)[:, 0:T], w[:, k, f * P:(f + 1) * P], srcT[:, k, :],
                                         start=(k == 0), stop=(k == kt - 1))
                    done(last, 0, z0 + f)

            pe.wait_ge(ld["consts"], 16)
            pe.wait_ge(ld["x"], 32)
            for k in range(KD):
                n = z_x[k]
                fill_wait(pe, 0, n)
                for t, (t0, w) in enumerate(TOK):
                    last = pe.transpose(out(0, n)[:, t0:t0 + w], xin[0:w, t, k * P:(k + 1) * P], ident[0:w, 0:w])
                done(last, 0, n)
            pe.wait_ge(ld["small"], 16 * 7)
            fill_wait(pe, 0, z_vec)
            pe.transpose(out(0, z_vec)[:, 0:NV], vrow[0:NV, :], ident[0:NV, 0:NV])
            for k in range(KD):
                last = pe.transpose(out(0, z_vec)[:, P + k * NSEQ:P + (k + 1) * NSEQ],
                                    crow[:, k * P:(k + 1) * P], ident[0:NSEQ, 0:NSEQ])
            done(last, 0, z_vec)
            sums(0, z_n1, [zT[:, k, :] for k in range(KD)], S_["xT_sq"])
            drain_wait(pe, 0, z_vec)
            ada(0, z_ara, y_moda)
            pe.wait_ge(S_["h1"], 1)
            for j in range(N_UQK):
                arrived(pe, n_uqk + j)
                feature_major(z_uqk[4 * j], wblk(n_uqk + j), hT)
            for j in range(8):
                fill_wait(pe, 0, z_swap[j])
                drain_wait(pe, 0, z_uqk[4 + j])
                done(pe.matmul(out(0, z_swap[j])[:, 0:T], swap, zT[:, Z_Q + j, :], start=True, stop=True), 0, z_swap[j])
            for j in range(N_V):
                arrived(pe, n_v + j)
                for t, (t0, w) in enumerate(TOK):
                    n = z_v[3 * j + t]
                    fill_wait(pe, 0, n)
                    for k in range(KD):
                        last = pe.matmul(out(0, n)[0:w, :], hT[:, k, t0:t0 + w], wblk(n_v + j)[:, k, :],
                                         start=(k == 0), stop=(k == KD - 1))
                    done(last, 0, n)
            pe.wait_ge(ld["pool"], 16)
            fill_wait(pe, 0, z_pool)
            for g in range(G):
                last = pe.transpose(out(0, z_pool)[:, g * 120:(g + 1) * 120], prow[:, g * P:(g + 1) * P],
                                    ident[0:120, 0:120])
            done(last, 0, z_pool)
            with pe.Fori(0, N_FM // RING) as i:
                for j in range(RING):
                    arrived(pe, n_fm + j, i * 16)
                    feature_major(z_fm[4 * j], wblk(n_fm + j), hT, more=i * 3)
            ada(n_adab, z_arb, y_modb)
            for t, (t0, w) in enumerate([(SEQ - PB, PB), (SEQ, NS)]):
                fill_wait(pe, 0, z_tail[t])
                for g in range(G):
                    last = pe.transpose(out(0, z_tail[t])[0:w, g * P:(g + 1) * P], zT[:, Z_U + g, t0:t0 + w], ident)
                done(last, 0, z_tail[t])
            pe.wait_ge(ld["wpg"], 16)
            for g in range(G):
                fill_wait(pe, 0, z_pg[g])
                pe.wait_ge(S_["pm"], g + 1)
                done(pe.matmul(out(0, z_pg[g])[:, 0:T], wpg[:, g, :], zT[:, Z_U + g, :], start=True, stop=True),
                     0, z_pg[g])
            pe.wait_ge(S_["rot"], 8)
            for t, (t0, w) in enumerate(TOK):
                fill_wait(pe, 0, z_kt[t])
                for h in range(G):
                    last = pe.transpose(out(0, z_kt[t])[0:w, h * P:(h + 1) * P], zT[:, Z_K + h, t0:t0 + w], ident)
                done(last, 0, z_kt[t])
            for n in z_v:
                drain_wait(pe, 0, n)
            for n in z_kt:
                drain_wait(pe, 0, n)

            def scores(h):
                n = y_sc[h]
                fill_wait(pe, 1, n)
                for t, (t0, w) in enumerate(TOK):
                    last = pe.matmul(out(1, n)[0:w, t0:t0 + w], zT[:, Z_K + h, t0:t0 + w], zT[:, Z_Q + h, t0:t0 + w],
                                     start=True, stop=True)
                done(last, 1, n)

            def state_step(n, h, c):
                fill_wait(pe, 1, n)
                done(pe.matmul(out(1, n)[:, 0:DV], ktok[:, c, h * P:(h + 1) * P], v[:, c, h * DV:(h + 1) * DV],
                               start=True, stop=True), 1, n)

            for h in range(G + 1):
                if h < G:
                    scores(h)
                    state_step(y_s0[h], h, 0)
                if h == 0:
                    pe.wait_ge(ld["state"], 16 * G)
                    pe.wait_ge(S_["qd_s"], G)
                    pe.wait_ge(S_["kbl"], 1)
                    continue
                g = h - 1
                drain_wait(pe, 1, y_sc[g])
                drain_wait(pe, 1, y_s0[g])
                for et in range(2):
                    n = z_o[g][et]
                    e0 = g * DV + et * P
                    o = out(0, n)
                    fill_wait(pe, 0, n)
                    pe.matmul(o[:, 0:P], v[:, 0, e0:e0 + P], sT[:, g % 2, 0:P], start=True, stop=True)
                    pe.matmul(o[:, P:SEQ], v[:, 1, e0:e0 + P], sT[:, g % 2, P:SEQ], start=True, stop=False)
                    pe.matmul(o[:, P:SEQ], SP0[:, g, et * P:(et + 1) * P], qd[:, g, 0:CHUNK], start=False, stop=True)
                    pe.matmul(o[:, SEQ:T], v[0:NS, 2, e0:e0 + P], sT[0:NS, g % 2, SEQ:T], start=True, stop=False,
                              skip_group_check=True)
                    for b in range(DEC_B):
                        c = CHUNK + b * DEC_L
                        last = pe.matmul(o[:, SEQ + b * DEC_L:SEQ + (b + 1) * DEC_L], S[:, g, b, et * P:(et + 1) * P],
                                         qd[:, g, c:c + DEC_L], start=False, stop=(b == DEC_B - 1),
                                         skip_group_check=True)
                    done(last, 0, n)
                state_step(y_s1[g], g, 1)
                for bp in range(DEC_B // 2):
                    n = y_ss[g][bp]
                    fill_wait(pe, 1, n)
                    for u in range(2):
                        last = pe.matmul(out(1, n)[:, u * DV:(u + 1) * DV], kblk[:, 2 * bp + u, g * P:(g + 1) * P],
                                         v[0:NS, 2, g * DV:(g + 1) * DV], start=True, stop=True)
                    done(last, 1, n)
            arrived(pe, n_bp)
            for n in z_pg:
                drain_wait(pe, 0, n)
            feature_major(z_a[0], ring[:, slot(n_bp), :].rearrange("p (k c) -> p k c", k=G), hT, kt=G, nf=KD)
            for h in range(G):
                pe.wait_ge(S_["osq"], h + 1)
                sums(1, y_hn[h], [hT[:, 4 + 2 * (h % 2) + et, :] for et in range(2)])
            pe.wait_ge(S_["gated"], G)
            for j in range(2):
                arrived(pe, n_br + j)
                feature_major(z_r[4 * j], wblk(n_br + j), zT[:, Z_G:Z_G + KD, :])
            pe.wait_ge(S_["merged"], KD)
            for j in range(2):
                arrived(pe, n_wo + j)
                feature_major(z_m[4 * j], wblk(n_wo + j), zT[:, Z_A:Z_A + KD, :])
            sums(1, y_n2, [zT[:, k, :] for k in range(KD)], S_["x1_sq"])
            for b in range(4):
                drain_wait(pe, 0, Z_END - 1 - b)
                drain_wait(pe, 1, Y_END - 1 - b)

            def filled(ins, n):
                ins.then_inc(mready[n % 8], 1)

            def mout(n):
                return bank[n % 8]

            pe.wait_ge(S_["h2"], 1)
            pe.wait_ge(ld["router"], 32)
            for t, (t0, w) in enumerate(TOK):
                m_fill_wait(pe, m_rt[t])
                for k in range(KD):
                    last = pe.matmul(mout(m_rt[t])[0:w, 0:E], hT[:, k, t0:t0 + w], wrt[:, k, :],
                                     start=(k == 0), stop=(k == KD - 1))
                filled(last, m_rt[t])
            pe.wait_ge(gu_in[3], 32)
            for i, (m, f) in enumerate([(0, 0), (0, 1), (1, 0), (1, 1)]):
                m_fill_wait(pe, m_sgu[i])
                for k in range(KD):
                    last = pe.matmul(mout(m_sgu[i])[:, 0:T], w_gate_up(3)[:, m, k, f * P:(f + 1) * P], hT[:, k, :],
                                     start=(k == 0), stop=(k == KD - 1))
                filled(last, m_sgu[i])
            pe.wait_ge(S_["sel_s"], 1)
            m_fill_wait(pe, m_rank)
            up = cst[:, C_UP:C_UP + P]
            for t, (t0, w) in enumerate(TOK):
                for b in range(t + 1):
                    last = pe.matmul(mout(m_rank)[0:w, t * E:(t + 1) * E], (up if b == t else ones)[0:TOK[b][1], 0:w],
                                     sel[0:TOK[b][1], b, :], start=(b == 0), stop=(b == t))
            filled(last, m_rank)
            for t, (t0, w) in enumerate(TOK):
                for c in range(2):
                    n = m_hx[2 * t + c]
                    m_fill_wait(pe, n)
                    for k in range(4):
                        last = pe.transpose(mout(n)[0:w, k * P:(k + 1) * P], hT[:, 4 * c + k, t0:t0 + w], ident)
                    filled(last, n)
            m_drain_wait(pe, m_rank)
            for n, rows in ((m_keyT, keys), (m_gateT, gates)):
                m_fill_wait(pe, n)
                for t, (t0, w) in enumerate(TOK):
                    last = pe.transpose(mout(n)[0:E, t0:t0 + w], rows[0:w, t, :], ident[0:w, 0:w])
                filled(last, n)
            pe.wait_ge(dn_in[3], 16)
            m_drain_wait(pe, m_sgu[2])
            m_drain_wait(pe, m_sgu[3])
            for k in range(KD):
                m_fill_wait(pe, m_sd[k])
                for f in range(2):
                    last = pe.matmul(mout(m_sd[k])[:, 0:T], w_down(3)[:, f, k * P:(k + 1) * P], hidS[:, f, :],
                                     start=(f == 0), stop=(f == 1))
                filled(last, m_sd[k])
            pe.wait_ge(S_["no_s"], 1)
            m_fill_wait(pe, m_ob)
            filled(pe.matmul(mout(m_ob)[0:E, 0:1], cst[0:E, C_UP:C_UP + E], e_no, start=True, stop=True), m_ob)
            pe.wait_ge(S_["tables_s"], 1)
            m_fill_wait(pe, m_ids)
            pe.matmul(mout(m_ids)[0:1, 0:NCH], cst[0:E, C_ENUM:C_ENUM + 1], selc[:, :], start=True, stop=True)
            filled(pe.matmul(mout(m_ids)[0:1, NCH:NCH + 1], ones[0:E, 0:1], e_no, start=True, stop=True), m_ids)
            for n, rows in ((m_keyc, keyT), (m_gatec, gateT)):
                m_fill_wait(pe, n)
                for t, (t0, w) in enumerate(TOK):
                    w = 2 * NS if t == 2 and n == m_keyc else w
                    o = mout(n)[0:w, t * NCH:(t + 1) * NCH]
                    last = pe.matmul(o, rows[:, t0:t0 + w], selc[:, :], start=True, stop=(n != m_keyc))
                    if n == m_keyc:
                        last = pe.matmul(o, ones[0:E, 0:w], selb[:, :], start=False, stop=True)
                filled(last, n)

            def gather(n0, more=0):
                for c in range(2):
                    n = n0 + c
                    m_fill_wait(pe, n, more)
                    for k in range(4):
                        f0 = (4 * c + k) * P
                        o = mout(n)[:, k * P:(k + 1) * P]
                        for t in range(2):
                            pe.matmul(o, xh[:, t, f0:f0 + P], oh[:, t, :], start=(t == 0), stop=False)
                            pe.matmul(o, xl[:, t, f0:f0 + P], oh[:, t, :], start=False, stop=False)
                        last = pe.matmul(o, xs[:, f0:f0 + P], oh[0:2 * NS, 2, :], start=False, stop=True)
                    filled(last, n)

            def slot_major(n0, more=0):
                for c in range(2):
                    m_fill_wait(pe, n0 + c, more)
                    for k in range(4):
                        last = pe.transpose(mout(n0 + c)[:, k * P:(k + 1) * P], yT[:, 4 * c + k, :], ident)
                    filled(last, n0 + c)

            def scatter(n0, buf, more=0):
                for k in range(KD):
                    m_fill_wait(pe, n0 + k, more)
                    pe.matmul(mout(n0 + k)[:, 0:T], yh[:, k * P:(k + 1) * P], pt[buf][:, :], start=True, stop=False)
                    filled(pe.matmul(mout(n0 + k)[:, 0:T], yl[:, k * P:(k + 1) * P], pt[buf][:, :],
                                     start=False, stop=True), n0 + k)

            turns = load_turns(pe)
            for n in m_hx:
                m_drain_wait(pe, n)
            pe.wait_ge(S_["oh_s"], 1)
            gather(m_a0[0])
            m_drain_wait(pe, m_a0[0])
            m_drain_wait(pe, m_a0[1])
            with pe.Fori(0, turns) as q:
                for s in range(2):
                    base = m_loop + s * M_PAIR
                    more = q * 4
                    m_fill_wait(pe, base + M_B, more)
                    if s == 0:
                        m_drain_wait(pe, base + M_A + 1 - M_PAIR, more)
                        m_drain_wait(pe, base + M_A - M_PAIR, more)
                    else:
                        m_drain_wait(pe, base + M_A + 1 - M_PAIR, more)
                        m_drain_wait(pe, base + M_A - M_PAIR, more)
                    for j in range(2):
                        pe.wait_ge(gu_in[2 * s + j], (q + 1 + (2 * s + j == 3)) * 32)
                        w = w_gate_up(2 * s + j)
                        for m in range(2):
                            for f in range(2):
                                c0 = (2 * m + f) * 2 * C + j * C
                                for k in range(KD):
                                    last = pe.matmul(mout(base + M_B)[:, c0:c0 + C], w[:, m, k, f * P:(f + 1) * P],
                                                     xsel[s][:, k, j * C:(j + 1) * C], start=(k == 0), stop=(k == KD - 1))
                    filled(last, base + M_B)
                    m_fill_wait(pe, base + M_T, more)
                    pe.wait_ge(S_["ohg_s"], q * 2 + (s + 1))
                    for t, (t0, w) in enumerate(TOK):
                        last = pe.transpose(mout(base + M_T)[:, t0:t0 + w], ohg[0:w, t, :], ident[0:w, 0:w])
                    filled(last, base + M_T)
                    if s == 0:
                        pe.wait_ge(S_["zero_s"], 1)
                        m_drain_wait(pe, base + M_C - M_PAIR, more)
                        m_drain_wait(pe, base + M_C + 1 - M_PAIR, more)
                    else:
                        m_drain_wait(pe, base + M_C - M_PAIR, more)
                        m_drain_wait(pe, base + M_C + 1 - M_PAIR, more)
                    slot_major(base + M_D, more)
                    pe.wait_ge(S_["oh_s"], q * 2 + (s + 2))
                    gather(base + M_A, more)
                    m_drain_wait(pe, base + M_B, more)
                    for c in range(2):
                        m_fill_wait(pe, base + M_C + c, more)
                        for j in range(2):
                            if c == 0:
                                pe.wait_ge(dn_in[2 * s + j], (q + 1 + (2 * s + j == 3)) * 16)
                            w = w_down(2 * s + j)
                            for k in range(4):
                                f0 = (4 * c + k) * P
                                c0 = k * 2 * C + j * C
                                for f in range(2):
                                    last = pe.matmul(mout(base + M_C + c)[:, c0:c0 + C], w[:, f, f0:f0 + P],
                                                     hid[:, f, j * C:(j + 1) * C], start=(f == 0), stop=(f == 1))
                        filled(last, base + M_C + c)
                    m_drain_wait(pe, base + M_D, more)
                    m_drain_wait(pe, base + M_D + 1, more)
                    scatter(base + M_E, 1 - s, more)
            more = turns * 4
            m_drain_wait(pe, m_loop - M_PAIR + M_C, more)
            m_drain_wait(pe, m_loop - M_PAIR + M_C + 1, more)
            slot_major(m_dl[0], more)
            m_drain_wait(pe, m_dl[0], more)
            m_drain_wait(pe, m_dl[1], more)
            scatter(m_el[0], 1, more)
            m_fill_wait(pe, m_nf, more)
            for k in range(KD):
                pe.wait_ge(S_["x2_sq"], k + 1)
                last = pe.matmul(mout(m_nf)[:, 0:T], ones, sq2[:, k, :], start=(k == 0), stop=(k == KD - 1))
            filled(last, m_nf)
            pe.wait_ge(S_["yT"], 1)
            for t, (t0, w) in enumerate(TOK):
                for c in range(2):
                    n = m_y[2 * t + c]
                    m_fill_wait(pe, n, more)
                    for k in range(4):
                        last = pe.transpose(mout(n)[0:w, k * P:(k + 1) * P], hT[:, 4 * c + k, t0:t0 + w], ident)
                    filled(last, n)

        @block.scalar
        def _(act):
            def copy(dst, src, **kw):
                return act.activation(dst, src, ACT.Copy, **kw)

            def src(r, n):
                return bank[bk(r, n)]

            def freed(ins, r, n):
                ins.then_inc(free[bk(r, n)], 1)

            def root(r, n, mean_of, dst):
                read_wait(act, r, n)
                act.wait_ge(S_["eps"], 1)
                freed(act.activation(dst, src(r, n)[:, 0:T], ACT.Sqrt, scale=1.0 / mean_of, bias=eps_col[:, 0:1]), r, n)

            def ada_rows(z, turned):
                for j, n in enumerate(z):
                    read_wait(act, 0, n)
                    if j >= 2:
                        act.wait_ge(S_["arow_t"], turned + j - 1)
                    freed(copy(arow[:, j % 2, :], src(0, n)[0:NSEQ, :]), 0, n)

            for k in range(KD):
                read_wait(act, 0, z_x[k])
                freed(copy(xT[:, k, :], src(0, z_x[k])[:, 0:T]), 0, z_x[k])
            root(0, z_n1, D, rstd[:, :])
            ada_rows(z_ara, 0)
            for j in range(12):
                read_wait(act, 0, z_uqk[j])
                if j == 0:
                    act.wait_ge(S_["h1"], 1)
                freed(copy(zT[:, Z_U + j, :], src(0, z_uqk[j])[:, 0:T]), 0, z_uqk[j])
            for j in range(N_V):
                for t, (t0, w) in enumerate(TOK):
                    n = z_v[3 * j + t]
                    read_wait(act, 0, n)
                    freed(copy(v[0:w, t, j * BC:(j + 1) * BC], src(0, n)[0:w, :]), 0, n)
            read_wait(act, 0, z_pool)
            freed(copy(stT[:, :, :].rearrange("p g r -> p (g r)"), src(0, z_pool)[:, 0:480]), 0, z_pool)
            with act.Fori(0, 2) as i:
                for j in range(12):
                    n = z_fm[j]
                    read_wait(act, 0, n, i * 3)
                    freed(copy(zT[:, bass.ds(i * 12 + (Z_G + j), 1), :].rearrange("p a t -> p (a t)"),
                               src(0, n)[:, 0:T]), 0, n)
            ada_rows(z_arb, N_ADA_A - 1)
            for t, w in enumerate([PB, NS]):
                read_wait(act, 0, z_tail[t])
                freed(copy(ptail[0:w, t, :], src(0, z_tail[t])[0:w, :]), 0, z_tail[t])
            for n in z_fm[-4:]:
                drain_wait(act, 0, n)
            act.activation(zT[:, Z_A:Z_A + 16, :], zT[:, Z_A:Z_A + 16, :], ACT.Sigmoid).then_inc(S_["sig_ab"], 1)
            act.activation(zT[:, Z_G:Z_G + 8, :], zT[:, Z_G:Z_G + 8, :], ACT.Silu).then_inc(S_["silu_g"], 1)
            for g in range(G):
                read_wait(act, 0, z_pg[g])
                freed(act.activation(hT[:, g, :], src(0, z_pg[g])[:, 0:T], ACT.Copy,
                                     scale=vecT[:, V_PS + g:V_PS + g + 1]), 0, z_pg[g])
            for h in range(G):
                for et in range(2):
                    n = z_o[h][et]
                    read_wait(act, 0, n)
                    freed(copy(zT[:, (Z_Q, Z_K)[et] + h, :], src(0, n)[:, 0:T]), 0, n)
            for h in range(G):
                if h >= 2:
                    read_wait(act, 1, y_hn[h - 2])
                for et in range(2):
                    drain_wait(act, 0, z_o[h][et])
                    last = act.activation(hT[:, 4 + 2 * (h % 2) + et, :], zT[:, (Z_Q, Z_K)[et] + h, :], ACT.Square)
                last.then_inc(S_["osq"], 1)
            for h in range(G):
                root(1, y_hn[h], DV, zT[:, Z_U + h, :])
            root(1, y_n2, D, rstd[:, :])
            def msrc(n):
                return bank[n % 8]

            def mfreed(ins, n):
                ins.then_inc(mfree[n % 8], 1)

            act.wait_ge(S_["router_set"], 1)
            for t, (t0, w) in enumerate(TOK):
                m_read_wait(act, m_rt[t])
                mfreed(act.activation(sc_s[0:w, t, :], msrc(m_rt[t])[0:w, 0:E], ACT.Sigmoid), m_rt[t])
            for f in range(2):
                m_read_wait(act, m_sgu[f])
                mfreed(act.activation(sgS[:, f, :], msrc(m_sgu[f])[:, 0:T], ACT.Silu), m_sgu[f])
            for t, (t0, w) in enumerate(TOK):
                for c in range(2):
                    n = m_hx[2 * t + c]
                    m_read_wait(act, n)
                    dst = xh[:, t, c * BC:(c + 1) * BC] if t < 2 else xs[0:NS, c * BC:(c + 1) * BC]
                    copy(dst, msrc(n)[0:w, :]).then_inc(S_["yh_s"], 1)
            for k in range(KD):
                m_read_wait(act, m_sd[k])
                mfreed(copy(acc[:, k, :], msrc(m_sd[k])[:, 0:T]), m_sd[k])

            def gathered(n0, buf, more=0):
                for c in range(2):
                    m_read_wait(act, n0 + c, more)
                    mfreed(copy(xsel[buf][:, 4 * c:4 * c + 4, :].rearrange("p k s -> p (k s)"), msrc(n0 + c)[:, :]), n0 + c)

            def high_parts(n0, buf, more=0):
                for c in range(2):
                    m_read_wait(act, n0 + c, more)
                    act.activation(yh[:, c * BC:(c + 1) * BC], msrc(n0 + c)[:, :], ACT.Copy, scale=gslot[buf][:, 0:1])\
                       .then_inc(S_["yh_s"], 1)

            gathered(m_a0[0], 0)
            turns = load_turns(act)
            act.wait_ge(S_["zero_s"], 1)
            with act.Fori(0, turns) as q:
                for s in range(2):
                    base = m_loop + s * M_PAIR
                    more = q * 4
                    m_read_wait(act, base + M_B, more)
                    act.activation(sg[:, :, :].rearrange("p f s -> p (f s)"), msrc(base + M_B)[:, 0:4 * C], ACT.Silu)\
                       .then_inc(S_["sg_s"], 1)
                    act.wait_ge(S_["pt_s"], q * 2 + (s + 1))
                    high_parts(base + M_D, 1 - s, more)
                    gathered(base + M_A, 1 - s, more)
                    for c in range(2):
                        m_read_wait(act, base + M_C + c, more)
                        mfreed(copy(yT[:, 4 * c:4 * c + 4, :].rearrange("p k s -> p (k s)"), msrc(base + M_C + c)[:, :]),
                               base + M_C + c)
            more = turns * 4
            act.wait_ge(S_["pt_s"], turns * 2 + 1)
            high_parts(m_dl[0], 1, more)
            m_read_wait(act, m_nf, more)
            mfreed(act.activation(rstd[:, :], msrc(m_nf)[:, 0:T], ACT.Sqrt, scale=1.0 / D, bias=eps_col[:, 0:1]), m_nf)
            for t, (t0, w) in enumerate(TOK):
                for c in range(2):
                    n = m_y[2 * t + c]
                    m_read_wait(act, n, more)
                    mfreed(copy(ystage[0:w, t, c * BC:(c + 1) * BC], msrc(n)[0:w, :]), n)

        @block.vector
        def _(dve):
            chain = [0]

            def link(ins):
                chain[0] += 1
                ins.then_inc(dve_chain, 1)
                dve.wait_ge(dve_chain, chain[0])

            def src(r, n):
                return bank[bk(r, n)]

            def freed(ins, r, n):
                ins.then_inc(free[bk(r, n)], 1)

            def toks(ap):
                return ap.rearrange("p k (b l) -> p k b l", b=DEC_B)

            def modulate(g_at, shift, scale, sums_at):
                drain_wait(dve, *sums_at)
                link(dve.reciprocal(rstd[:, :], rstd[:, :]))
                link(dve.tensor_tensor(hT[:, :, :], xT[:, :, :], bcast(rstd[:, :], 1, KD), ALU.mult))
                link(dve.scalar_tensor_tensor(gs[:, :, :], modT[:, scale:scale + KD, :], 1.0,
                                              bcast(vecT[:, g_at:g_at + KD], 2, NSEQ), ALU.add, ALU.mult))
                for k in range(KD):
                    dve.tensor_scalar(hT[:, k, 0:SEQ], hT[:, k, 0:SEQ], gs[:, k, 0:1], modT[:, shift + k, 0:1],
                                      ALU.mult, ALU.add)
                hs = toks(hT[:, :, SEQ:T])
                link(dve.tensor_tensor(hs, hs, bcast(gs[:, :, 1:NSEQ], 3, DEC_L), ALU.mult))
                return dve.tensor_tensor(hs, hs, bcast(modT[:, shift:shift + KD, 1:NSEQ], 3, DEC_L), ALU.add)

            def mod_rows(y, j0, count):
                read_wait(dve, 1, y)
                freed(dve.tensor_tensor(modT[:, j0:j0 + count, :],
                                        src(1, y)[:, 0:count * NSEQ].rearrange("p (j s) -> p j s", s=NSEQ),
                                        bcast(vecT[:, V_ADA + j0:V_ADA + j0 + count], 2, NSEQ), ALU.add), 1, y)

            dve.memset(eps_col[:, :], EPS).then_inc(S_["eps"], 1)
            for k in range(KD):
                drain_wait(dve, 0, z_x[k])
                dve.tensor_tensor(zT[:, k, :], xT[:, k, :], xT[:, k, :], ALU.mult).then_inc(S_["xT_sq"], 1)
            read_wait(dve, 0, z_vec)
            link(dve.tensor_copy(vecT[:, :], src(0, z_vec)[:, 0:NV]))
            freed(dve.tensor_copy(cT[:, :, :], src(0, z_vec)[:, P:P + KD * NSEQ].rearrange("p (k s) -> p k s", s=NSEQ)),
                  0, z_vec)
            mod_rows(y_moda, 0, 2 * KD)
            drain_wait(dve, 1, y_moda)
            modulate(V_G1, 0, KD, (0, z_n1)).then_inc(S_["h1"], 1)
            rt = qd[:, :, :].rearrange("p h c -> p (h c)")
            for j in range(8):
                q = zT[:, Z_Q + j, :]
                read_wait(dve, 0, z_swap[j])
                dve.tensor_tensor(rt[:, 0:T], q, cst[:, C_COS:C_COS + T], ALU.mult)
                freed(dve.tensor_tensor(rt[:, T:2 * T], src(0, z_swap[j])[:, 0:T], cst[:, C_SIN:C_SIN + T], ALU.mult),
                      0, z_swap[j])
                drain_wait(dve, 0, z_swap[j])
                dve.tensor_tensor(q, rt[:, 0:T], rt[:, T:2 * T], ALU.add).then_inc(S_["rot"], 1)
                dve.wait_ge(S_["rot"], j + 1)
            for h in range(G):
                w = C_QDEC + h * (CHUNK + NS)
                dve.tensor_tensor(qd[:, h, :], zT[:, Z_Q + h, CHUNK:T], cst[:, w:w + CHUNK + NS], ALU.mult)\
                   .then_inc(S_["qd_s"], 1)
            link(dve.memset(extp[:, :, 0:PB], 0.0))
            dve.tensor_copy(extp[:, :, PB:LP], zT[:, Z_U:Z_U + G, 0:SEQ])
            for g in range(G):
                if g == 0:
                    drain_wait(dve, 0, z_pool)
                dve.tensor_copy(exts[:, g, :, 0:PB], stT[:, g, :].rearrange("p (b r) -> p b r", b=DEC_B))
                last = dve.tensor_copy(exts[:, g, :, PB:LS], zT[:, Z_U + g, SEQ:T].rearrange("p (b l) -> p b l", b=DEC_B))
            link(last)
            views = []
            for area_ in (sumA, sumB):
                views.append((area_[:, 0:G * LP].rearrange("p (g l) -> p g l", g=G),
                              area_[:, G * LP:PW].rearrange("p (g b l) -> p g b l", g=G, b=DEC_B)))
            prev = (extp, exts)
            for s in range(G):
                cur = views[s % 2]
                sh, lo = 1 << s, (2 << s) - 1
                dve.tensor_tensor(cur[0][:, s:G, lo:LP], prev[0][:, s:G, lo:LP], prev[0][:, s:G, lo - sh:LP - sh],
                                  ALU.add)
                for g in range(s, G):
                    last = dve.tensor_tensor(cur[1][:, g, :, lo:LS], prev[1][:, g, :, lo:LS],
                                             prev[1][:, g, :, lo - sh:LS - sh], ALU.add)
                link(last)
                prev = cur
            for t in range(2):
                read_wait(dve, 0, z_tail[t])
            for g in range(G):
                sp_, ss_ = views[g % 2]
                u = zT[:, Z_U + g, :]
                link(dve.tensor_tensor(sp_[:, g, PB:PB + 16], sp_[:, g, PB:PB + 16],
                                       cst[:, C_ICNT + 16 * g:C_ICNT + 16 * (g + 1)], ALU.mult))
                dve.tensor_tensor(u[:, 0:16], sp_[:, g, PB:PB + 16], u[:, 0:16], ALU.subtract)
                dve.scalar_tensor_tensor(u[:, 16:SEQ], sp_[:, g, PB + 16:LP], 1.0 / WINDOWS[g], u[:, 16:SEQ],
                                         ALU.mult, ALU.subtract)
                us = u[:, SEQ:T].rearrange("p (b l) -> p b l", b=DEC_B)
                dve.scalar_tensor_tensor(us, ss_[:, g, :, PB:LS], 1.0 / WINDOWS[g], us, ALU.mult, ALU.subtract)\
                   .then_inc(S_["pm"], 1)
            mod_rows(y_modb, 2 * KD, 4 * KD)
            drain_wait(dve, 1, y_modb)
            dve.wait_ge(S_["pm"], G)
            for t, (t0, w) in enumerate(TOK):
                read_wait(dve, 0, z_kt[t])
                dst, dec = (ktok[:, t, :], C_KDEC) if t < 2 else (ktoks, C_KDECS)
                last = dve.tensor_tensor(dst.rearrange("p (h d) -> p h d", h=G),
                                         src(0, z_kt[t])[0:w, :].rearrange("p (h d) -> p h d", h=G),
                                         bcast(cst[0:w, dec:dec + G], 2, P), ALU.mult)
                freed(last, 0, z_kt[t])
            drain_wait(dve, 0, z_kt[2])
            for b in range(DEC_B):
                last = dve.tensor_scalar(kblk[:, b, :], ktoks, cst[0:NS, C_ROWB + b:C_ROWB + b + 1], None, ALU.mult)
            last.then_inc(S_["kbl"], 1)

            def masked(h):
                n = y_sc[h]
                read_wait(dve, 1, n)
                dve.tensor_tensor(sT[:, h % 2, 0:SEQ].rearrange("p (c q) -> p c q", c=2),
                                  src(1, n)[:, 0:SEQ].rearrange("p (c q) -> p c q", c=2),
                                  bcast(cst[:, C_INTRA + h * P:C_INTRA + (h + 1) * P], 1, 2), ALU.mult)
                freed(dve.tensor_tensor(sT[0:NS, h % 2, SEQ:T], src(1, n)[0:NS, SEQ:T],
                                        cst[0:NS, C_INTRAS + h * NS:C_INTRAS + (h + 1) * NS], ALU.mult), 1, n)
                read_wait(dve, 1, y_s0[h])
                freed(dve.tensor_copy(SP0[:, h, :], src(1, y_s0[h])[:, 0:DV]), 1, y_s0[h])

            for h in range(G + 1):
                if h < G:
                    masked(h)
                if h > 0:
                    g = h - 1
                    read_wait(dve, 1, y_s1[g])
                    drain_wait(dve, 1, y_s0[g])
                    freed(dve.scalar_tensor_tensor(SP0[:, g, :], SP0[:, g, :], s_dec[g], src(1, y_s1[g])[:, 0:DV],
                                                   ALU.mult, ALU.add), 1, y_s1[g])
                    for bp in range(DEC_B // 2):
                        n = y_ss[g][bp]
                        read_wait(dve, 1, n)
                        st = S[:, g, 2 * bp:2 * bp + 2, :].rearrange("p b e -> p (b e)")
                        freed(dve.scalar_tensor_tensor(st, st, s_dec_s[g], src(1, n)[:, :], ALU.mult, ALU.add), 1, n)
            dve.wait_ge(S_["sig_ab"], 1)
            for j in range(KD):
                read_wait(dve, 0, z_a[j])
                a = zT[:, Z_A + j, :]
                freed(dve.tensor_tensor(a, a, src(0, z_a[j])[:, 0:T], ALU.mult), 0, z_a[j])
            dve.wait_ge(S_["silu_g"], 1)
            for h in range(G):
                drain_wait(dve, 1, y_hn[h])
                u = zT[:, Z_U + h, :]
                link(dve.reciprocal(u, u))
                gg = zT[:, Z_G + 2 * h:Z_G + 2 * h + 2, :]
                link(dve.tensor_tensor(gg, gg, bcast(u, 1, 2), ALU.mult))
                for et in range(2):
                    o = zT[:, (Z_Q, Z_K)[et] + h, :]
                    g_ = zT[:, Z_G + 2 * h + et, :]
                    last = dve.tensor_tensor(g_, g_, o, ALU.mult)
                last.then_inc(S_["gated"], 1)
            for j in range(KD):
                read_wait(dve, 0, z_r[j])
                b = zT[:, Z_B + j, :]
                freed(dve.tensor_tensor(b, b, src(0, z_r[j])[:, 0:T], ALU.mult), 0, z_r[j])
                drain_wait(dve, 0, z_r[j])
                drain_wait(dve, 0, z_a[j])
                dve.tensor_tensor(zT[:, Z_A + j, :], zT[:, Z_A + j, :], b, ALU.add).then_inc(S_["merged"], 1)

            def residual(z, k, gate, last_sem):
                read_wait(dve, 0, z)
                m = src(0, z)
                tmp = zT[:, 8 + k, SEQ:T]
                dve.scalar_tensor_tensor(xT[:, k, 0:SEQ], m[:, 0:SEQ], modT[:, gate + k, 0:1], xT[:, k, 0:SEQ],
                                         ALU.mult, ALU.add)
                freed(dve.tensor_tensor(tmp.rearrange("p (b l) -> p b l", b=DEC_B),
                                        m[:, SEQ:T].rearrange("p (b l) -> p b l", b=DEC_B),
                                        bcast(modT[:, gate + k, 1:NSEQ], 2, DEC_L), ALU.mult), 0, z)
                drain_wait(dve, 0, z)
                link(dve.tensor_tensor(xT[:, k, SEQ:T], xT[:, k, SEQ:T], tmp, ALU.add))
                dve.tensor_tensor(zT[:, k, :], xT[:, k, :], xT[:, k, :], ALU.mult).then_inc(last_sem, 1)

            for k in range(KD):
                residual(z_m[k], k, 2 * KD, S_["x1_sq"])
            modulate(V_G2, 3 * KD, 4 * KD, (1, y_n2)).then_inc(S_["h2"], 1)

            dve.wait_ge(stored, 16 * N_FRONT_STORES)
            dve.memset(sc_s[:, :, :], 0.5).then_inc(S_["router_set"], 1)
            for t in range(3):
                m_drain_wait(dve, m_rt[t])
            dve.wait_ge(ld["router"], 32)
            dve.memset(gsc[:, :, 8:12], LOW)
            dve.memset(etop[:, :, :], LOW)
            link(dve.tensor_tensor(sc_b, sc_s, bcast(brow[:, :], 1, 3), ALU.add))
            for t in range(3):
                for g in range(NG):
                    last = dve.max(gtop[:, t, g, :], sc_b[:, t, g * EG:(g + 1) * EG])
            link(last)
            link(dve.tensor_tensor(gsc[:, :, 0:NG], gtop[:, :, :, 0], gtop[:, :, :, 1], ALU.add))
            for t in range(3):
                last = dve.max(gsort[:, t, :], gsc[:, t, 0:NG])
            link(last)
            link(dve.tensor_copy(etop[:, :, 0:4], gsort[:, :, 0:4]))
            for t in range(3):
                last = dve.match_replace(grep[:, t, :], etop[:, t, :], gsc[:, t, :], 2 * LOW)
            link(last)
            link(dve.tensor_scalar(gmask, grep[:, :, 0:NG], 1.5 * LOW, None, ALU.is_le))
            link(dve.tensor_scalar(gfill, gmask, 1.0, -LOW, ALU.subtract, ALU.mult))
            by_group = lambda ap: ap.rearrange("p t (g e) -> p (t g) e", g=NG)
            one = lambda ap: bcast(ap.rearrange("p t g -> p (t g)"), 2, EG)
            link(dve.tensor_tensor(by_group(sc_m), by_group(sc_b), one(gmask), ALU.mult))
            link(dve.tensor_tensor(by_group(sc_m), by_group(sc_m), one(gfill), ALU.add))
            for t in range(3):
                last = dve.max(etop[:, t, :], sc_m[:, t, :])
            link(last)
            for t in range(3):
                last = dve.match_replace(sc_r[:, t, :], etop[:, t, :], sc_m[:, t, :], 2 * LOW)
            link(last)
            dve.tensor_scalar(sel, sc_r, 1.5 * LOW, None, ALU.is_le).then_inc(S_["sel_s"], 1)
            dve.wait_ge(S_["sel_s"], 1)
            link(dve.tensor_tensor(gates, sel, sc_s, ALU.mult))
            link(dve.tensor_reduce(wsum, gates, AX_X, ALU.add))
            link(dve.reciprocal(winv, wsum))
            link(dve.tensor_scalar(winv, winv, SCALE_OUT, None, ALU.mult))
            link(dve.tensor_tensor(gates, gates, bcast(winv, 2, E), ALU.mult))

            def msrc(n):
                return bank[n % 8]

            def mfreed(ins, n):
                ins.then_inc(mfree[n % 8], 1)

            for f in range(2):
                m_drain_wait(dve, m_sgu[f])
                m_read_wait(dve, m_sgu[2 + f])
                mfreed(dve.tensor_tensor(hidS[:, f, :], sgS[:, f, :], msrc(m_sgu[2 + f])[:, 0:T], ALU.mult), m_sgu[2 + f])
            m_read_wait(dve, m_rank)
            link(dve.memset(keys, 0.0))
            for t, (t0, w) in enumerate(TOK):
                last = dve.scalar_tensor_tensor(keys[0:w, t, :], msrc(m_rank)[0:w, t * E:(t + 1) * E], KEY0, sel[0:w, t, :],
                                                ALU.add, ALU.mult)
                if t == 2:
                    mfreed(last, m_rank)
            for t, (t0, w) in enumerate(TOK):
                for c in range(2):
                    n = m_hx[2 * t + c]
                    m_read_wait(dve, n)
                    dve.wait_ge(S_["yh_s"], 2 * t + c + 1)
                    cc = slice(c * BC, (c + 1) * BC)
                    hi, lo = (xh[:, t, cc], xl[:, t, cc]) if t < 2 else (xs[0:NS, cc], xs[NS:2 * NS, cc])
                    mfreed(dve.tensor_tensor(lo, msrc(n)[0:w, :], hi.bitcast(F32), ALU.subtract), n)
            m_read_wait(dve, m_keyT)
            dve.tensor_copy(keyT[:, 0:T], msrc(m_keyT)[0:E, 0:T])
            mfreed(dve.tensor_copy(keyT[:, T:T + NS], msrc(m_keyT)[0:E, SEQ:T]), m_keyT)
            m_read_wait(dve, m_gateT)
            mfreed(dve.tensor_copy(gateT[:, :], msrc(m_gateT)[0:E, 0:T]), m_gateT)
            m_drain_wait(dve, m_keyT)
            chosen = sgE
            link(dve.tensor_scalar(chosen, keyT[:, 0:T], 0.5 * KEY0, None, ALU.is_ge))
            link(dve.tensor_reduce(e_cnt, chosen, AX_X, ALU.add))
            link(dve.tensor_scalar(e_full, cst[0:E, C_FULL:C_FULL + 4], e_cnt, None, ALU.is_lt))
            dve.tensor_reduce(e_no, e_full, AX_X, ALU.add).then_inc(S_["no_s"], 1)
            m_read_wait(dve, m_ob)
            mfreed(dve.tensor_copy(e_ob, msrc(m_ob)[0:E, 0:1]), m_ob)
            m_drain_wait(dve, m_ob)
            dve.tensor_copy(selc[:, 0:E], ident[0:E, 0:E])
            dve.memset(selb[:, 0:E], 0.0)
            over, later, right = selc[:, E:NCH], selb[:, E:NCH], oE
            dve.wait_ge(S_["no_s"], 1)
            link(dve.tensor_scalar(later, cst[0:E, C_OVER:C_OVER + 40], e_ob, None, ALU.subtract))
            link(dve.tensor_scalar(right, later, e_no, None, ALU.is_lt))
            link(dve.scalar_tensor_tensor(over, later, 0.0, right, ALU.is_ge, ALU.mult))
            link(dve.tensor_scalar(later, later, 1.0, -float(C), ALU.add, ALU.mult))
            dve.tensor_tensor(later, later, over, ALU.mult).then_inc(S_["tables_s"], 1)
            m_read_wait(dve, m_ids)
            dve.tensor_scalar(q_full, cst[0:1, C_QUAD:C_QUAD + 9], msrc(m_ids)[0:1, NCH:NCH + 1], None, ALU.is_lt)\
               .then_inc(dve_chain, 1)
            chain[0] += 1
            dve.wait_ge(dve_chain, chain[0])
            mfreed(dve.tensor_copy(ids[:, :], msrc(m_ids)[0:1, 0:NCH]), m_ids)
            link(dve.tensor_reduce(q_n, q_full, AX_X, ALU.add))
            m_drain_wait(dve, m_ids)
            dve.tensor_scalar(nquads[:, :], q_n, float(MIN_Q), None, ALU.add).then_inc(S_["chunks_s"], 1)
            dve.memset(keyc[:, :, :], 0.0)
            link(dve.memset(gatec[:, :, :], 0.0))
            for n, dst in ((m_keyc, keyc), (m_gatec, gatec)):
                m_read_wait(dve, n)
                dve.tensor_copy(dst[:, 0:2, :].rearrange("p t c -> p (t c)"), msrc(n)[:, 0:2 * NCH])
                w = 2 * NS if n == m_keyc else NS
                mfreed(dve.tensor_copy(dst[0:w, 2, :], msrc(n)[0:w, 2 * NCH:3 * NCH]), n)
            m_drain_wait(dve, m_keyc)
            m_drain_wait(dve, m_gatec)

            def slots(chunk, before):
                if before is not None:
                    dve.wait_ge(S_["ohg_s"], before)
                two = keyc[:, :, bass.ds(chunk, 2)]
                row = bcast(bcast(cst[:, C_SLOT:C_SLOT + C], 1, 2), 1, 3)
                dve.tensor_tensor(oh[:, :, :].rearrange("p t (j s) -> p t j s", j=2), row, bcast(two, 3, C),
                                  ALU.is_equal).then_inc(S_["oh_s"], 1)

            def gated_slots(chunk, count):
                dve.wait_ge(S_["oh_s"], count)
                two = gatec[:, :, bass.ds(chunk, 2)]
                dve.tensor_tensor(ohg[:, :, :].rearrange("p t (j s) -> p t j s", j=2),
                                  oh[:, :, :].bitcast(F32).rearrange("p t (j s) -> p t j s", j=2), bcast(two, 3, C),
                                  ALU.mult).then_inc(S_["ohg_s"], 1)

            def low_parts(n0, buf, highs, more=0):
                for c in range(2):
                    dve.wait_ge(S_["yh_s"], highs + (c + 1))
                    cc = slice(c * BC, (c + 1) * BC)
                    mfreed(dve.scalar_tensor_tensor(yl[:, cc], msrc(n0 + c)[:, :], gslot[buf][:, 0:1],
                                                    yh[:, cc].bitcast(F32), ALU.mult, ALU.subtract), n0 + c)

            def add_up(n0, more=0):
                for k in range(KD):
                    m_read_wait(dve, n0 + k, more)
                    mfreed(dve.tensor_tensor(acc[:, k, :], acc[:, k, :], msrc(n0 + k)[:, 0:T], ALU.add), n0 + k)

            slots(0, None)
            gated_slots(0, 1)
            for n in m_sd:
                m_drain_wait(dve, n)
            dve.memset(pt[1][:, :].bitcast(F32), 0.0)
            dve.memset(gslot[1][:, :], 0.0).then_inc(S_["pt_s"], 1)
            dve.memset(yT[:, :, :], 0.0).then_inc(S_["zero_s"], 1)
            turns = load_turns(dve)
            m_read_wait(dve, m_a0[1])
            with dve.Fori(0, turns) as q:
                for s in range(2):
                    base = m_loop + s * M_PAIR
                    more = q * 4
                    m_read_wait(dve, base + M_A + 1 - M_PAIR, more)
                    slots(q * 4 + (2 * s + 2), q * 2 + (s + 1))
                    m_read_wait(dve, base + M_B, more)
                    dve.wait_ge(S_["sg_s"], q * 2 + (s + 1))
                    mfreed(dve.tensor_tensor(hid[:, :, :].rearrange("p f s -> p (f s)"),
                                             sg[:, :, :].rearrange("p f s -> p (f s)"), msrc(base + M_B)[:, 4 * C:8 * C],
                                             ALU.mult), base + M_B)
                    m_read_wait(dve, base + M_T, more)
                    dve.tensor_reduce(gslot[s][:, :], msrc(base + M_T)[:, 0:T], AX_X, ALU.add).then_inc(S_["pt_s"], 1)
                    mfreed(dve.tensor_scalar(pt[s][:, :], msrc(base + M_T)[:, 0:T], 0.0, None, ALU.is_gt), base + M_T)
                    gated_slots(q * 4 + (2 * s + 2), q * 2 + (s + 2))
                    m_read_wait(dve, base + M_D + 1, more)
                    low_parts(base + M_D, 1 - s, q * 4 + (6 + 2 * s))
                    add_up(base + M_E, more)
            more = turns * 4
            low_parts(m_dl[0], 1, turns * 4 + 6)
            add_up(m_el[0], more)
            for k in range(KD):
                m_drain_wait(dve, m_el[k], more)
                dve.scalar_tensor_tensor(xT[:, k, 0:SEQ], acc[:, k, 0:SEQ], modT[:, 5 * KD + k, 0:1], xT[:, k, 0:SEQ],
                                         ALU.mult, ALU.add)
            fs = toks(acc[:, :, SEQ:T])
            link(dve.tensor_tensor(fs, fs, bcast(modT[:, 5 * KD:6 * KD, 1:NSEQ], 3, DEC_L), ALU.mult))
            link(dve.tensor_tensor(xT[:, :, SEQ:T], xT[:, :, SEQ:T], acc[:, :, SEQ:T], ALU.add))
            for k in range(KD):
                dve.tensor_tensor(sq2[:, k, :], xT[:, k, :], xT[:, k, :], ALU.mult).then_inc(S_["x2_sq"], 1)
            m_drain_wait(dve, m_nf, more)
            link(dve.reciprocal(rstd[:, :], rstd[:, :]))
            link(dve.tensor_tensor(hT[:, :, :], xT[:, :, :], bcast(rstd[:, :], 1, KD), ALU.mult))
            dve.tensor_tensor(hT[:, :, :], hT[:, :, :], bcast(vecT[:, V_GF:V_GF + KD], 2, T), ALU.mult)\
               .then_inc(S_["yT"], 1)


_INS = ["x_prompt", "x_sample", "c_prompt", "c_sample", "state_pool", "state_ret", "w_ada", "b_ada", "g_norm1",
        "w_in", "w_pool_group", "pool_scale", "w_branch_pool", "w_branch_ret", "w_out", "g_norm2", "w_router",
        "b_router", "w_exp_gate", "w_exp_up", "w_exp_down", "w_sh_gate", "w_sh_up", "w_sh_down", "g_final"]
_OUTS = [(1, SEQ, D), (DEC_B, DEC_L, D), (1, 1, PB, 512), (1, 1, G, P, DV), (1, DEC_B, PB, 512), (1, DEC_B, G, P, DV)]


def kernel(**inputs):
    import concourse.bacc as bacc
    from concourse.bass_utils import run_bass_kernel_spmd

    nc = bacc.Bacc("TRN2", target_bir_lowering=False, num_devices=1)
    arrays = {"consts": shape_constants()}
    args = [nc.dram_tensor("consts", arrays["consts"].shape, F32, kind="ExternalInput").ap()]
    for name in _INS:
        arrays[f"in_{name}"] = np.ascontiguousarray(inputs[name])
        args.append(nc.dram_tensor(f"in_{name}", arrays[f"in_{name}"].shape, F32, kind="ExternalInput").ap())
    for i, shape in enumerate(_OUTS):
        args.append(nc.dram_tensor(f"out_{i}", shape, F32, kind="ExternalOutput").ap())
    build(nc, *args)
    r = run_bass_kernel_spmd(nc, [arrays], core_ids=[0])
    return tuple(r.results[0][f"out_{i}"] for i in range(len(_OUTS)))
```

```python
from contextlib import ExitStack

import numpy as np
import concourse.bass as bass
from concourse import mybir

ALU = mybir.AluOpType
ACT = mybir.ActivationFunctionType
F32 = mybir.dt.float32
F32R = mybir.dt.float32r
I32 = mybir.dt.int32
AX_X = mybir.AxisListType.X

P = 128
D = 1024
KD = D // P
SEQ, DEC_B, DEC_L = 256, 8, 4
NS = DEC_B * DEC_L
T = SEQ + NS
TOK = [(0, P), (P, P), (SEQ, NS)]
PAST = 2048
WINDOWS = (2, 4, 8, 16)
PB = 15
G = 4
DV = 256
CHUNK = 128
NMOD = 6
NSEQ = 1 + DEC_B
E = 64
NG, EG = 8, 8
DE = 256
SCALE_OUT = 2.5
EPS = 1e-6
BC = 512
RING = 3
LOW = -1e30

C_ID, C_SWAP, C_ONES = 0, P, 2 * P
C_COS = 3 * P
C_SIN = C_COS + T
C_INTRA = C_SIN + T
C_QDEC = C_INTRA + G * P
C_INTRAS = C_QDEC + G * (CHUNK + NS)
C_ICNT = C_INTRAS + G * NS
C_KDEC = C_ICNT + G * 16
C_KDECS = C_KDEC + G
C_ROWB = C_KDECS + G
C_UP = C_ROWB + DEC_B
C_SLOT = C_UP + P
C_ENUM = C_SLOT + 64
C_OVER = C_ENUM + 1
C_FULL = C_OVER + 40
C_QUAD = C_FULL + 4
C_TWO = C_QUAD + 9
NC_COLS = C_TWO + 64

C = 64
KEY0 = 1000.0
MAX_OVER = 36
NCH = E + 40
MIN_Q, MAX_Q = E // 4, (E + MAX_OVER) // 4

Z_U, Z_Q, Z_K, Z_G, Z_A, Z_B = 0, 4, 8, 12, 20, 28
NZ = 36

V_ADA, V_G1, V_G2, V_GF, V_PS = 0, 48, 56, 64, 72
NV = 76


def log_decays():
    f = np.float32
    return np.log(f(1.0) - np.power(f(2.0), f(-5.0) - np.arange(G, dtype=f))).astype(f)


def shape_constants():
    c = np.zeros((P, NC_COLS), np.float64)
    c[:, C_ID:C_ID + P] = np.eye(P)
    c[:, C_SWAP:C_SWAP + P] = np.roll(np.eye(P), P // 2, axis=0)
    c[:, C_ONES:C_ONES + P] = 1.0
    f = np.float32
    inv = np.power(f(10000.0), -np.arange(64, dtype=f) / f(64)).astype(f)
    pos = np.concatenate([np.arange(SEQ), np.tile(PAST + np.arange(DEC_L), DEC_B)]).astype(f)
    ang = (np.concatenate([inv, inv])[:, None] * pos[None, :]).astype(f).astype(np.float64)
    c[:, C_COS:C_COS + T] = np.cos(ang)
    c[:, C_SIN:C_SIN + T] = np.sin(ang) * np.where(np.arange(P) < 64, -1.0, 1.0)[:, None]
    lg = log_decays().astype(np.float64)
    ks = P ** -0.5
    m, q = np.arange(P)[:, None], np.arange(P)[None, :]
    ms, qs = np.arange(NS)[:, None], np.arange(NS)[None, :]
    for h in range(G):
        c[:, C_INTRA + h * P:C_INTRA + (h + 1) * P] = np.where(q >= m, np.exp(lg[h] * np.maximum(q - m, 0)), 0) * ks
        c[:NS, C_INTRAS + h * NS:C_INTRAS + (h + 1) * NS] = np.where(
            (qs >= ms) & (qs // DEC_L == ms // DEC_L), np.exp(lg[h] * np.maximum(qs - ms, 0)), 0) * ks
        w = C_QDEC + h * (CHUNK + NS)
        c[:, w:w + CHUNK] = np.exp(lg[h] * (np.arange(CHUNK) + 1.0))[None, :]
        c[:, w + CHUNK:w + CHUNK + NS] = np.exp(lg[h] * (np.arange(NS) % DEC_L + 1.0))[None, :]
        c[:, C_KDEC + h] = np.exp(lg[h] * (CHUNK - 1.0 - np.arange(P))) * ks
        c[:NS, C_KDECS + h] = np.exp(lg[h] * (DEC_L - 1.0 - np.arange(NS) % DEC_L)) * ks
        c[:, C_ICNT + h * 16:C_ICNT + (h + 1) * 16] = 1.0 / np.minimum(WINDOWS[h], np.arange(16) + 1.0)[None, :]
    for b in range(DEC_B):
        c[b * DEC_L:(b + 1) * DEC_L, C_ROWB + b] = 1.0
    c[:, C_UP:C_UP + P] = m < q
    c[:, C_SLOT:C_SLOT + C] = KEY0 + np.arange(C)
    c[:, C_ENUM] = np.arange(P)
    c[:, C_OVER:C_OVER + 40] = np.arange(40)
    c[:, C_FULL:C_FULL + 4] = C * (1 + np.arange(4))
    c[:, C_QUAD:C_QUAD + 9] = 4 * np.arange(9)
    c[:, C_TWO:C_TWO + C] = np.tile(np.eye(C), (2, 1))
    return c.astype(np.float32)


def bcast(ap, at, n):
    wide = ap.unsqueeze(at)
    shape = list(wide.shape)
    shape[at] = n
    return wide.broadcast_to(shape)


def build(nc, consts, x_prompt, x_sample, c_prompt, c_sample, state_pool, state_ret, w_ada, b_ada, g_norm1,
          w_in, w_pool_group, pool_scale, w_branch_pool, w_branch_ret, w_out, g_norm2, w_router, b_router,
          w_exp_gate, w_exp_up, w_exp_down, w_sh_gate, w_sh_up, w_sh_down, g_final,
          y_prompt, y_sample, new_pool_prompt, new_ret_prompt, new_pool_sample, new_ret_sample):
    lg = log_decays().astype(np.float64)
    s_dec = [float(np.exp(v * CHUNK)) for v in lg]
    s_dec_s = [float(np.exp(v * DEC_L)) for v in lg]

    with ExitStack() as ctx:
        def sb(name, shape):
            return ctx.enter_context(nc.sbuf_tensor(name, shape, F32))

        def sb_r(name, shape):
            return ctx.enter_context(nc.sbuf_tensor(name, shape, F32R))

        def sem(name):
            return ctx.enter_context(nc.semaphore(name))

        xT = sb("xT", [P, KD, T])
        hT = sb("hT", [P, KD, T])
        cst = sb("cst", [P, NC_COLS])
        modT = sb("modT", [P, NMOD * KD, NSEQ])
        vecT = sb("vecT", [P, NV])
        cT = sb("cT", [P, KD, NSEQ])
        gs = sb("gs", [P, KD, NSEQ])
        rstd = sb("rstd", [P, T])
        wpg = sb("wpg", [P, G, P])
        wrt = sb("wrt", [P, KD, E])
        brow = sb("brow", [P, E])
        eps_col = sb("eps_col", [P, 1])

        mixer = ExitStack()

        def mb(name, shape):
            return mixer.enter_context(nc.sbuf_tensor(name, shape, F32))

        ring = mb("ring", [P, RING, KD * BC])
        split = ExitStack()
        t_hi, t_lo = ([split.enter_context(nc.sbuf_tensor(f"t_{name}{j}", [P, KD, P], F32R)) for j in range(4)]
                      for name in ("hi", "lo"))
        x_hi = split.enter_context(nc.sbuf_tensor("x_hi", [P, KD, T], F32R))
        x_lo = split.enter_context(nc.sbuf_tensor("x_lo", [P, KD, T], F32R))
        split.close()
        S = mb("S", [P, G, DEC_B, DV])
        scratch = mb("scratch", [P, 5100])
        v = mb("v", [P, 3, D])
        zT = mb("zT", [P, NZ, T])
        SP0 = mb("SP0", [P, G, DV])
        ktok = mb("ktok", [P, 2, G * P])
        qd = mb("qd", [P, G, CHUNK + NS])
        sT = mb("sT", [P, 2, T])
        stT = mb("stT", [P, G, DEC_B * PB])
        ptail = mb("ptail", [NS, 2, G * P])
        mixer.close()

        PC = 4 * 2 * DE
        w_hi = [sb_r(f"w_hi{j}", [P, PC]) for j in range(4)]
        w_lo = [sb_r(f"w_lo{j}", [P, PC]) for j in range(4)]
        raw0 = sb("raw0", [P, PC])
        yh = sb_r("yh", [P, D])
        yl = sb_r("yl", [P, D])
        raw123 = sb("raw123", [P, 3, PC])
        raw = [raw0[:, :]] + [raw123[:, j, :] for j in range(3)]
        xsel = sb_r("xsel", [P, KD, 4, 2 * C])
        hr = sb_r("hr", [P, 2, 2, 4 * C])
        xh = sb_r("xh", [P, 2, D])
        xl = sb_r("xl", [P, 2, D])
        xs = sb_r("xs", [2 * NS, D])
        ohg = sb("ohg", [P, 3, 2 * C])
        pt = [sb_r(f"pt{j}", [P, T]) for j in range(2)]
        gslot = [sb(f"gslot{j}", [P, 1]) for j in range(2)]
        hidS = sb("hidS", [P, 2, T])
        sgS = sb("sgS", [P, 2, T])
        hid, sg = (a[:, :, :].rearrange("p f t -> p (f t)")[:, 0:4 * C].rearrange("p (f s) -> p f s", f=2)
                   for a in (hidS, sgS))
        keyT = sb("keyT", [E, T + NS])
        gateT = sb("gateT", [E, T])
        selc = sb("selc", [E, NCH])
        selb = sb("selb", [E, NCH])
        ework = sb("ework", [E, 64])
        keyc = sb("keyc", [P, 3, NCH])
        gatec = sb("gatec", [P, 3, NCH])
        ids = ctx.enter_context(nc.sbuf_tensor("ids", [1, NCH], I32))
        nquads = ctx.enter_context(nc.sbuf_tensor("nquads", [1, 1], I32))
        routing = ExitStack()
        rwork = routing.enter_context(nc.sbuf_tensor("rwork", [P, 1800], F32))
        routing.close()
        oh = sb_r("oh", [P, 3, 4 * C])
        gu = [sb(f"gu{j}", [P, 2 * DE]) for j in range(2)]
        acc = hT
        raws = raw123[:, :, :].rearrange("p j c -> p (j c)")
        ystage = raws[:, 0:3 * D].rearrange("p (t d) -> p t d", t=3)

        ident = cst[:, C_ID:C_ID + P]
        swap = cst[:, C_SWAP:C_SWAP + P]
        ones = cst[:, C_ONES:C_ONES + P]
        xin = scratch[:, 0:3 * D].rearrange("p (t d) -> p t d", t=3)
        vrow = scratch[:, 3072:3072 + P]
        crow = scratch[0:NSEQ, 3200:3200 + D]
        prow = sT[:, :, :].rearrange("p u t -> p (u t)")[0:DEC_B * PB, 0:G * P]
        LP, LS = SEQ + PB, DEC_L + PB
        PW = G * LP + G * DEC_B * LS
        extp = scratch[:, 0:G * LP].rearrange("p (g l) -> p g l", g=G)
        exts = scratch[:, G * LP:PW].rearrange("p (g b l) -> p g b l", g=G, b=DEC_B)
        sumA = scratch[:, PW:2 * PW]
        sumB = scratch[:, 2 * PW:3 * PW]
        assert 3 * PW <= 5100
        arow = SP0[0:NSEQ, :, :].rearrange("p h e -> p (h e)").rearrange("p (u c) -> p u c", u=2)
        kblk = scratch[0:NS, 0:DEC_B * G * P].rearrange("p (b n) -> p b n", b=DEC_B)
        ktoks = sT[:, :, :].rearrange("p u t -> p (u t)")[0:NS, 0:G * P]

        bank = [ctx.enter_context(nc.psum_tensor(f"bank{i}", [P, 512], F32)) for i in range(8)]
        ready = [sem(f"ready{i}") for i in range(8)]
        free = [sem(f"free{i}") for i in range(8)]

        class Tiles:
            def __init__(self):
                self.n = 0

            def take(self, k=1):
                a = self.n
                self.n += k
                return a if k == 1 else range(a, a + k)

        def bk(ringno, n):
            return ringno * 4 + n % 4

        def fill_wait(pe, r, n, more=0):
            if isinstance(more, int) and n + 4 * more < 4:
                return
            pe.wait_ge(free[bk(r, n)], n // 4 + more)

        def read_wait(eng, r, n, more=0):
            eng.wait_ge(ready[bk(r, n)], n // 4 + 1 + more)

        def drain_wait(eng, r, n, more=0):
            eng.wait_ge(free[bk(r, n)], n // 4 + 1 + more)

        Z, Y = Tiles(), Tiles()
        z_x = Z.take(KD)
        z_vec = Z.take()
        z_n1 = Z.take()
        z_ara = Z.take(4)
        y_moda = Y.take()
        z_vt = Z.take(8)
        z_uqk = Z.take(12)
        z_swap = Z.take(8)
        z_v = Z.take(6)
        z_pool = Z.take()
        z_tail = Z.take(2)
        z_kt = Z.take(3)
        z_fm = Z.take(24)
        z_arb = Z.take(8)
        y_modb = Y.take()
        z_pg = Z.take(4)
        y_sc, y_s0, y_s1, y_ss, y_hn, z_o = [], [], [], [], [], []
        for h in range(G + 1):
            if h < G:
                y_sc.append(Y.take())
                y_s0.append(Y.take())
            if h > 0:
                z_o.append(Z.take(2))
                y_s1.append(Y.take())
                y_ss.append(Y.take(4))
            if h > 1:
                y_hn.append(Y.take())
        z_a = Z.take(KD)
        y_hn.append(Y.take())
        z_r = Z.take(KD)
        z_m = Z.take(KD)
        y_n2 = Y.take()
        Z_END, Y_END = Z.n, Y.n

        mready = [sem(f"mready{i}") for i in range(8)]
        mfree = [sem(f"mfree{i}") for i in range(8)]
        M = Tiles()
        m_rt = M.take(3)
        m_sgu = M.take(4)
        m_rank = M.take()
        m_hx = M.take(6)
        m_keyT = M.take()
        m_gateT = M.take()
        m_sd = M.take(KD)
        m_ob = M.take()
        m_ids = M.take()
        m_keyc = M.take()
        m_gatec = M.take()
        m_a0 = M.take(4)
        m_loop = M.n
        M_TURN = 32
        m_gu, m_b, m_t, m_a, m_e, m_c = [], [], [], [], [], []
        loop_fills = Tiles()
        loop_fills.n = m_loop
        for s in range(2):
            m_gu.append(loop_fills.take(2))
            m_b.append(loop_fills.take())
            m_t.append(loop_fills.take())
            if s == 1:
                m_a = loop_fills.take(4)
            m_e.append(loop_fills.take(KD))
            m_c.append(loop_fills.take(2))
        assert loop_fills.n == m_loop + M_TURN
        m_c_before = ([n - M_TURN for n in m_c[1]], m_c[0])
        m_el = M.take(KD)
        m_nf = M.take()
        m_y = M.take(6)

        def m_fill_wait(pe, n, more=0):
            if n >= 8:
                pe.wait_ge(mfree[n % 8], n // 8 + more)

        def m_read_wait(eng, n, more=0):
            eng.wait_ge(mready[n % 8], n // 8 + 1 + more)

        def m_drain_wait(eng, n, more=0):
            eng.wait_ge(mfree[n % 8], n // 8 + 1 + more)

        ld = {k: sem(f"loaded_{k}") for k in ("consts", "x", "small", "pool", "state", "wpg", "router")}
        ring_in = [sem(f"ring_in{i}") for i in range(RING)]
        stored = sem("stored")
        S_ = {}
        for name in ("eps", "arow_t", "xT_sq", "h1", "rot", "qd_s", "pm", "kbl", "osq", "sig_ab", "silu_g",
                     "gated", "merged", "x1_sq", "h2", "router_set", "x2_sq", "yT", "yh_s", "sg_s",
                     "xs_hi", "hh_s", "hl_s", "w_used", "y_staged", "hi_done", "tile_hi", "tile_lo", "x_hi", "x_lo",
                     "lo_done", "lo_pool",
                     "sel_s", "no_s", "chunks_s", "tables_s", "oh_s", "ohg_s", "zero_s"):
            S_[name] = sem(name)
        dve_chain = sem("dve_chain")

        N_ADA_A, N_UQK, N_V, N_FM, N_ADA_B = 4, 3, 2, 6, 8
        n_v = N_ADA_A
        n_uqk = n_v + N_V
        n_fm = n_uqk + N_UQK
        n_adab = n_fm + N_FM
        n_bp = n_adab + N_ADA_B
        n_br = n_bp + 1
        n_wo = n_br + 2

        last_fill = {n_bp: (0, z_a[-1])}
        last_fill.update({j: (0, z_ara[j]) for j in range(N_ADA_A)})
        last_fill.update({n_adab + j: (0, z_arb[j]) for j in range(N_ADA_B)})
        N_TILES = 4 * (N_V + N_UQK + N_FM)
        TILES_PER_TURN = 4 * RING

        def raw_tile(t):
            return wblk(N_ADA_A + t // 4)[:, :, t % 4 * P:(t % 4 + 1) * P]
        last_fill.update({n_br + j: (0, z_r[4 * j + 3]) for j in range(2)})
        last_fill.update({n_wo + j: (0, z_m[4 * j + 3]) for j in range(2)})

        def slot(n):
            return n % RING

        def wblk(n):
            return ring[:, slot(n), :].rearrange("p (k c) -> p k c", k=KD)

        def arrived(pe, n, more=0):
            pe.wait_ge(ring_in[slot(n)], 16 * (n // RING + 1) + more)

        def cols(w, c0):
            return w.rearrange("(k p) c -> p k c", p=P)[:, :, bass.ds(c0, BC)]

        win, wada = w_in[0], w_ada[0]

        raw_in = [sem(f"raw_in{j}") for j in range(4)]
        shared_in = [sem(f"shared_in{j}") for j in range(3)]

        loads = [16 if i % 6 >= 4 else 32 for i in range(12)]
        PER_TURN = sum(loads[i] for i in range(0, 12, 4))

        def piece_loaded(eng, i, q):
            v = (i // 12) * PER_TURN + sum(loads[j] for j in range(i % 4, i % 12 + 1, 4))
            eng.wait_ge(raw_in[i % 4], q * PER_TURN + v)

        def gate_up_rows(ap):
            return ap.rearrange("p (k f) -> p k f", k=4)

        def low_wait(eng, kind, s, q):
            if kind in (0, 4):
                eng.wait_ge(S_["lo_pool"], q * 4 + (2 * s + {0: 1, 4: 2}[kind]))
            else:
                eng.wait_ge(S_["lo_done"], q * 8 + (4 * s + {1: 1, 2: 2, 3: 3, 5: 4}[kind]))

        def by_chunk(ap):
            return ap.rearrange("p f (j s) -> p f j s", j=2)

        def down_rows(ap):
            return ap.rearrange("p (f d) -> p f d", f=2)

        rat = [0]

        def part(n):
            rat[0] += n
            return rwork[:, rat[0] - n:rat[0]]

        def by_token(n):
            return part(3 * n).rearrange("p (t e) -> p t e", t=3)

        sc_s, sc_b, sc_m, sc_r, gates, sel, keys = (by_token(E) for _ in range(7))
        gtop = part(3 * NG * 8).rearrange("p (t g e) -> p t g e", t=3, g=NG)
        gsc, grep = by_token(12), by_token(12)
        gsort, gmask, gfill, etop = (by_token(8) for _ in range(4))
        wsum, winv = part(3), part(3)
        e_cnt, e_no, e_ob = ework[:, 0:1], ework[:, 1:2], ework[:, 2:3]
        e_full = ework[:, 4:8]
        sgE = sgS[0:E, 0, :]
        oE = ework[:, 22:62]
        sq2 = raws[:, 3 * D:3 * D + KD * T].rearrange("p (k t) -> p k t", k=KD)
        q_full, q_n = ework[0:1, 8:17], ework[0:1, 18:19]
        N_FRONT_STORES = 1 + 2 + 1 + G

        block = ctx.enter_context(nc.Block())

        def load_turns(eng):
            eng.wait_ge(S_["chunks_s"], 1)
            return eng.value_load(nquads[0:1, 0:1], min_val=MIN_Q, max_val=MAX_Q)

        @block.sync
        def _(sp):
            sp.dma_start(xin[:, 0:2, :], x_prompt[0].rearrange("(t p) d -> p t d", p=P)).then_inc(ld["x"], 16)
            sp.dma_start(xin[0:NS, 2, :], x_sample.rearrange("b l d -> (b l) d")).then_inc(ld["x"], 16)
            sp.dma_start(cst[:, :], consts).then_inc(ld["consts"], 16)
            sp.dma_start(crow[0:1, :], c_prompt).then_inc(ld["small"], 16)
            sp.dma_start(crow[1:NSEQ, :], c_sample).then_inc(ld["small"], 16)
            for row, src, n in ((V_ADA, b_ada, 48), (V_G1, g_norm1, 8), (V_G2, g_norm2, 8), (V_PS, pool_scale, 4)):
                sp.dma_start(vrow[row:row + n, :], src[0].rearrange("(r c) -> r c", c=P)).then_inc(ld["small"], 16)
            sp.dma_start(vrow[V_GF:V_GF + 8, :], g_final.rearrange("(r c) -> r c", c=P)).then_inc(ld["small"], 16)

            def used(n):
                if n in last_fill:
                    read_wait(sp, *last_fill[n])
                if N_ADA_A <= n <= n_adab:
                    sp.wait_ge(S_["tile_lo"], 4 * (n - N_ADA_A + 1))

            def stream(n, src):
                if n >= RING:
                    used(n - RING)
                sp.dma_start(wblk(n), src).then_inc(ring_in[slot(n)], 16)

            def load_gate_up(dst, wg, wu, half, arrive):
                for m, w in enumerate((wg, wu)):
                    sp.dma_start(gate_up_rows(dst)[:, :, m * DE:(m + 1) * DE], w[:, 4 * half:4 * half + 4, :])\
                      .then_inc(arrive, 16)

            def routed(e):
                return (w_exp_gate[0, bass.ds(e, 1)].rearrange("a (k p) f -> p (a k) f", p=P),
                        w_exp_up[0, bass.ds(e, 1)].rearrange("a (k p) f -> p (a k) f", p=P),
                        w_exp_down[0, bass.ds(e, 1)].rearrange("a (f p) d -> p (a f) d", p=P))

            for j in range(N_ADA_A):
                stream(j, cols(wada, BC * j))
            sp.dma_start(prow, state_pool[0].rearrange("b r c -> (b r) c")).then_inc(ld["pool"], 16)
            for j in range(N_V):
                stream(n_v + j, cols(win, BC * (N_UQK + j)))
            for j in range(N_UQK):
                stream(n_uqk + j, cols(win, BC * j))
            sp.dma_start(wpg[:, :, :], w_pool_group[0].rearrange("g c d -> c g d")).then_inc(ld["wpg"], 16)
            sp.dma_start(wrt[:, :, :], w_router[0].rearrange("(k p) e -> p k e", p=P)).then_inc(ld["router"], 16)
            sp.dma_start(brow[:, :], bcast(b_router[0], 0, P)).then_inc(ld["router"], 16)
            for j in range(N_FM):
                stream(n_fm + j, cols(win, BC * (N_UQK + N_V + j)))
            sp.dma_start(new_pool_sample[0, :, 0:PB - DEC_L, :], state_pool[0, :, DEC_L:PB, :]).then_inc(stored, 16)
            for j in range(N_ADA_B):
                if j == RING:
                    read_wait(sp, 0, z_fm[-1])
                    sp.wait_ge(S_["tile_lo"], N_TILES + 4)
                    for h in range(G):
                        sp.dma_start(S[:, h, :, :], state_ret[0, :, h].rearrange("b d e -> d b e"))\
                          .then_inc(ld["state"], 16)
                stream(n_adab + j, cols(wada, BC * (N_ADA_A + j)))
            used(n_bp - RING)
            sp.dma_start(ring[:, slot(n_bp), :].rearrange("p (k c) -> p k c", k=G),
                         w_branch_pool[0].rearrange("(k p) c -> p k c", p=P)).then_inc(ring_in[slot(n_bp)], 16)
            for n in z_tail:
                drain_wait(sp, 0, n)
            sp.dma_start(new_pool_prompt[0, 0], ptail[0:PB, 0, :]).then_inc(stored, 16)
            sp.dma_start(new_pool_sample[0, :, PB - DEC_L:PB, :],
                         ptail[0:NS, 1, :]).then_inc(stored, 16)
            for j in range(2):
                stream(n_br + j, cols(w_branch_ret[0], BC * j))
            read_wait(sp, 0, z_o[-1][1])
            read_wait(sp, 1, y_ss[-1][3])
            for h in range(2):
                load_gate_up(raw[1 + h], w_sh_gate[0].rearrange("(k p) f -> p k f", p=P),
                             w_sh_up[0].rearrange("(k p) f -> p k f", p=P), h, shared_in[h])
            sp.dma_start(down_rows(raw[3]), w_sh_down[0].rearrange("(f p) d -> p f d", p=P)).then_inc(shared_in[2], 16)
            for j in range(2):
                stream(n_wo + j, cols(w_out[0], BC * j))
            drain_wait(sp, 1, y_s1[G - 1])
            sp.dma_start(new_ret_prompt[0, 0].rearrange("h d e -> d h e"), SP0[:, :, :]).then_inc(stored, 16)
            for h in range(G):
                for n in y_ss[h]:
                    drain_wait(sp, 1, n)
                sp.dma_start(new_ret_sample[0, :, h].rearrange("b d e -> d b e"), S[:, h, :, :]).then_inc(stored, 16)

            sp.wait_ge(stored, 16 * N_FRONT_STORES)
            for i in range(4):
                if i == 1:
                    m_read_wait(sp, m_sgu[3])
                if i == 3:
                    m_read_wait(sp, m_sd[-1])
                load_gate_up(raw[i], *routed(i // 2)[0:2], i % 2, raw_in[i])
            turns = load_turns(sp)
            with sp.Fori(0, turns) as q:
                experts = [routed(sp.value_load(ids[0:1, bass.ds(q * 4 + c, 1)], min_val=0, max_val=E - 1))
                           for c in range(6)]
                for s in range(2):
                    for j in range(2):
                        i = 6 * s + 4 + j
                        low_wait(sp, j, s, q)
                        sp.dma_start(down_rows(raw[i % 4]), experts[2 * s + j][2]).then_inc(raw_in[i % 4], 16)
                    for j in range(2):
                        for h in range(2):
                            i = 6 * s + 6 + 2 * j + h
                            if j == 0:
                                low_wait(sp, 2 + h, s, q)
                            else:
                                low_wait(sp, 4 + h, s, q)
                            load_gate_up(raw[i % 4], *experts[2 * s + 2 + j][0:2], h, raw_in[i % 4])
            for c in range(2):
                sp.wait_ge(S_["y_staged"], 3 * (c + 1))
                cc = slice(c * BC, (c + 1) * BC)
                sp.dma_start(y_prompt[0].rearrange("(t p) d -> p t d", p=P)[:, :, cc], ystage[:, 0:2, cc])\
                  .then_inc(stored, 16)
                sp.dma_start(y_sample.rearrange("b l d -> (b l) d")[:, cc], ystage[0:NS, 2, cc]).then_inc(stored, 16)
            sp.wait_ge(stored, 16 * (N_FRONT_STORES + 4))

        @block.tensor
        def _(pe):
            def done(ins, r, n):
                ins.then_inc(ready[bk(r, n)], 1)

            def out(r, n):
                return bank[bk(r, n)]

            def sums(r, n, rows, arrive=None):
                fill_wait(pe, r, n)
                for k, row in enumerate(rows):
                    if arrive is not None:
                        pe.wait_ge(arrive, k + 1)
                    last = pe.matmul(out(r, n)[:, 0:T], ones, row, start=(k == 0), stop=(k == len(rows) - 1))
                done(last, r, n)

            def ada(n0, z, y):
                fill_wait(pe, 1, y)

                def turn(j):
                    drain_wait(pe, 0, z[j])
                    for f in range(4):
                        c = (4 * j + f) * NSEQ
                        last = pe.transpose(out(1, y)[:, c:c + NSEQ], arow[:, j % 2, f * P:(f + 1) * P],
                                            ident[0:NSEQ, 0:NSEQ])
                    return last

                for j in range(len(z)):
                    arrived(pe, n0 + j)
                    fill_wait(pe, 0, z[j])
                    for k in range(KD):
                        last = pe.matmul(out(0, z[j])[0:NSEQ, :], cT[:, k, :], wblk(n0 + j)[:, k, :],
                                         start=(k == 0), stop=(k == KD - 1))
                    done(last, 0, z[j])
                    if j > 0:
                        turn(j - 1).then_inc(S_["arow_t"], 1)
                done(turn(len(z) - 1), 1, y)

            def feature_major(z0, w, srcT, kt=KD, nf=4, more=0):
                for f in range(nf):
                    fill_wait(pe, 0, z0 + f, more)
                    for k in range(kt):
                        last = pe.matmul(out(0, z0 + f)[:, 0:T], w[:, k, f * P:(f + 1) * P], srcT[:, k, :],
                                         start=(k == 0), stop=(k == kt - 1))
                    done(last, 0, z0 + f)

            pe.wait_ge(ld["consts"], 16)
            pe.wait_ge(ld["x"], 32)
            for k in range(KD):
                n = z_x[k]
                fill_wait(pe, 0, n)
                for t, (t0, w) in enumerate(TOK):
                    last = pe.transpose(out(0, n)[:, t0:t0 + w], xin[0:w, t, k * P:(k + 1) * P], ident[0:w, 0:w])
                done(last, 0, n)
            pe.wait_ge(ld["small"], 16 * 7)
            fill_wait(pe, 0, z_vec)
            pe.transpose(out(0, z_vec)[:, 0:NV], vrow[0:NV, :], ident[0:NV, 0:NV])
            for k in range(KD):
                last = pe.transpose(out(0, z_vec)[:, P + k * NSEQ:P + (k + 1) * NSEQ],
                                    crow[:, k * P:(k + 1) * P], ident[0:NSEQ, 0:NSEQ])
            done(last, 0, z_vec)
            sums(0, z_n1, [zT[:, k, :] for k in range(KD)], S_["xT_sq"])
            drain_wait(pe, 0, z_vec)
            ada(0, z_ara, y_moda)
            def projected(z, t, more=0):
                fill_wait(pe, 0, z, more)
                pe.wait_ge(S_["tile_lo"], t + 1 + more * 4)
                for k in range(KD):
                    if t == 0:
                        pe.wait_ge(S_["x_lo"], k + 1)
                    pe.matmul(out(0, z)[:, 0:T], t_hi[t % 4][:, k, :], x_hi[:, k, :], start=(k == 0), stop=False)
                    pe.matmul(out(0, z)[:, 0:T], t_hi[t % 4][:, k, :], x_lo[:, k, :], start=False, stop=False)
                    last = pe.matmul(out(0, z)[:, 0:T], t_lo[t % 4][:, k, :], x_hi[:, k, :], start=False,
                                     stop=(k == KD - 1))
                done(last, 0, z)

            for j, z in enumerate([*z_vt, *z_uqk]):
                projected(z, j)
            for j in range(8):
                fill_wait(pe, 0, z_swap[j])
                drain_wait(pe, 0, z_uqk[4 + j])
                done(pe.matmul(out(0, z_swap[j])[:, 0:T], swap, zT[:, Z_Q + j, :], start=True, stop=True), 0, z_swap[j])
            for j in range(N_V):
                for t, (t0, w) in enumerate(TOK):
                    n = z_v[3 * j + t]
                    fill_wait(pe, 0, n)
                    for f in range(4):
                        last = pe.transpose(out(0, n)[0:w, f * P:(f + 1) * P], zT[:, Z_G + 4 * j + f, t0:t0 + w],
                                            ident)
                    done(last, 0, n)
            pe.wait_ge(ld["pool"], 16)
            fill_wait(pe, 0, z_pool)
            for g in range(G):
                last = pe.transpose(out(0, z_pool)[:, g * 120:(g + 1) * 120], prow[:, g * P:(g + 1) * P],
                                    ident[0:120, 0:120])
            done(last, 0, z_pool)
            for t, (t0, w) in enumerate([(SEQ - PB, PB), (SEQ, NS)]):
                fill_wait(pe, 0, z_tail[t])
                for g in range(G):
                    last = pe.transpose(out(0, z_tail[t])[0:w, g * P:(g + 1) * P], zT[:, Z_U + g, t0:t0 + w], ident)
                done(last, 0, z_tail[t])
            pe.wait_ge(S_["rot"], 8)
            for t, (t0, w) in enumerate(TOK):
                fill_wait(pe, 0, z_kt[t])
                for h in range(G):
                    last = pe.transpose(out(0, z_kt[t])[0:w, h * P:(h + 1) * P], zT[:, Z_K + h, t0:t0 + w], ident)
                done(last, 0, z_kt[t])
            with pe.Fori(0, N_FM // RING) as i:
                for j in range(TILES_PER_TURN):
                    projected(z_fm[j], 20 + j, i * 3)
            ada(n_adab, z_arb, y_modb)
            pe.wait_ge(ld["wpg"], 16)
            for g in range(G):
                fill_wait(pe, 0, z_pg[g])
                pe.wait_ge(S_["pm"], g + 1)
                done(pe.matmul(out(0, z_pg[g])[:, 0:T], wpg[:, g, :], zT[:, Z_U + g, :], start=True, stop=True),
                     0, z_pg[g])
            for n in z_v:
                drain_wait(pe, 0, n)
            for n in z_kt:
                drain_wait(pe, 0, n)

            def scores(h):
                n = y_sc[h]
                fill_wait(pe, 1, n)
                for t, (t0, w) in enumerate(TOK):
                    last = pe.matmul(out(1, n)[0:w, t0:t0 + w], zT[:, Z_K + h, t0:t0 + w], zT[:, Z_Q + h, t0:t0 + w],
                                     start=True, stop=True)
                done(last, 1, n)

            def state_step(n, h, c):
                fill_wait(pe, 1, n)
                done(pe.matmul(out(1, n)[:, 0:DV], ktok[:, c, h * P:(h + 1) * P], v[:, c, h * DV:(h + 1) * DV],
                               start=True, stop=True), 1, n)

            def head_sums(h):
                pe.wait_ge(S_["osq"], h + 1)
                sums(1, y_hn[h], [hT[:, 4 + 2 * (h % 2) + et, :] for et in range(2)])

            for h in range(G + 1):
                if h < G:
                    scores(h)
                    state_step(y_s0[h], h, 0)
                if h == 0:
                    pe.wait_ge(ld["state"], 16 * G)
                    pe.wait_ge(S_["qd_s"], G)
                    pe.wait_ge(S_["kbl"], 1)
                    continue
                g = h - 1
                drain_wait(pe, 1, y_sc[g])
                drain_wait(pe, 1, y_s0[g])
                for et in range(2):
                    n = z_o[g][et]
                    e0 = g * DV + et * P
                    o = out(0, n)
                    fill_wait(pe, 0, n)
                    pe.matmul(o[:, 0:P], v[:, 0, e0:e0 + P], sT[:, g % 2, 0:P], start=True, stop=True)
                    pe.matmul(o[:, P:SEQ], v[:, 1, e0:e0 + P], sT[:, g % 2, P:SEQ], start=True, stop=False)
                    pe.matmul(o[:, P:SEQ], SP0[:, g, et * P:(et + 1) * P], qd[:, g, 0:CHUNK], start=False, stop=True)
                    pe.matmul(o[:, SEQ:T], v[0:NS, 2, e0:e0 + P], sT[0:NS, g % 2, SEQ:T], start=True, stop=False,
                              skip_group_check=True)
                    for b in range(DEC_B):
                        c = CHUNK + b * DEC_L
                        last = pe.matmul(o[:, SEQ + b * DEC_L:SEQ + (b + 1) * DEC_L], S[:, g, b, et * P:(et + 1) * P],
                                         qd[:, g, c:c + DEC_L], start=False, stop=(b == DEC_B - 1),
                                         skip_group_check=True)
                    done(last, 0, n)
                state_step(y_s1[g], g, 1)
                for bp in range(DEC_B // 2):
                    n = y_ss[g][bp]
                    fill_wait(pe, 1, n)
                    for u in range(2):
                        last = pe.matmul(out(1, n)[:, u * DV:(u + 1) * DV], kblk[:, 2 * bp + u, g * P:(g + 1) * P],
                                         v[0:NS, 2, g * DV:(g + 1) * DV], start=True, stop=True)
                    done(last, 1, n)
                if h > 1:
                    head_sums(h - 2)
            arrived(pe, n_bp)
            for n in z_pg:
                drain_wait(pe, 0, n)
            wbp = ring[:, slot(n_bp), :].rearrange("p (k c) -> p k c", k=G)
            feature_major(z_a[0], wbp[:, :, 0:BC], hT, kt=G)
            head_sums(G - 1)
            feature_major(z_a[4], wbp[:, :, BC:2 * BC], hT, kt=G)
            pe.wait_ge(S_["gated"], G)
            for j in range(2):
                arrived(pe, n_br + j)
                feature_major(z_r[4 * j], wblk(n_br + j), zT[:, Z_G:Z_G + KD, :])
            pe.wait_ge(S_["merged"], KD)
            for j in range(2):
                arrived(pe, n_wo + j)
                feature_major(z_m[4 * j], wblk(n_wo + j), zT[:, Z_A:Z_A + KD, :])
            sums(1, y_n2, [zT[:, k, :] for k in range(KD)], S_["x1_sq"])
            for b in range(4):
                drain_wait(pe, 0, Z_END - 1 - b)
                drain_wait(pe, 1, Y_END - 1 - b)

            def filled(ins, n):
                ins.then_inc(mready[n % 8], 1)

            def mout(n):
                return bank[n % 8]

            pe.wait_ge(ld["router"], 32)
            for t, (t0, w) in enumerate(TOK):
                m_fill_wait(pe, m_rt[t])
                for k in range(KD):
                    if t == 0:
                        pe.wait_ge(S_["h2"], k + 1)
                    last = pe.matmul(mout(m_rt[t])[0:w, 0:E], hT[:, k, t0:t0 + w], wrt[:, k, :],
                                     start=(k == 0), stop=(k == KD - 1))
                filled(last, m_rt[t])
            for h in range(2):
                pe.wait_ge(shared_in[h], 32)
            for i, (m, f) in enumerate([(0, 0), (0, 1), (1, 0), (1, 1)]):
                m_fill_wait(pe, m_sgu[i])
                for k in range(KD):
                    c0 = m * DE + f * P
                    last = pe.matmul(mout(m_sgu[i])[:, 0:T], gate_up_rows(raw[1 + k // 4])[:, k % 4, c0:c0 + P],
                                     hT[:, k, :], start=(k == 0), stop=(k == KD - 1))
                filled(last, m_sgu[i])
            pe.wait_ge(S_["sel_s"], 1)
            m_fill_wait(pe, m_rank)
            up = cst[:, C_UP:C_UP + P]
            for t, (t0, w) in enumerate(TOK):
                for b in range(t + 1):
                    last = pe.matmul(mout(m_rank)[0:w, t * E:(t + 1) * E], (up if b == t else ones)[0:TOK[b][1], 0:w],
                                     sel[0:TOK[b][1], b, :], start=(b == 0), stop=(b == t))
            filled(last, m_rank)
            for t, (t0, w) in enumerate(TOK):
                for c in range(2):
                    n = m_hx[2 * t + c]
                    m_fill_wait(pe, n)
                    for k in range(4):
                        last = pe.transpose(mout(n)[0:w, k * P:(k + 1) * P], hT[:, 4 * c + k, t0:t0 + w], ident)
                    filled(last, n)
            m_drain_wait(pe, m_rank)
            for n, rows in ((m_keyT, keys), (m_gateT, gates)):
                m_fill_wait(pe, n)
                for t, (t0, w) in enumerate(TOK):
                    last = pe.transpose(mout(n)[0:E, t0:t0 + w], rows[0:w, t, :], ident[0:w, 0:w])
                filled(last, n)
            pe.wait_ge(shared_in[2], 16)
            m_drain_wait(pe, m_sgu[2])
            m_drain_wait(pe, m_sgu[3])
            for k in range(KD):
                m_fill_wait(pe, m_sd[k])
                for f in range(2):
                    last = pe.matmul(mout(m_sd[k])[:, 0:T], down_rows(raw[3])[:, f, k * P:(k + 1) * P], hidS[:, f, :],
                                     start=(f == 0), stop=(f == 1))
                filled(last, m_sd[k])
            pe.wait_ge(S_["no_s"], 1)
            m_fill_wait(pe, m_ob)
            filled(pe.matmul(mout(m_ob)[0:E, 0:1], cst[0:E, C_UP:C_UP + E], e_no, start=True, stop=True), m_ob)
            pe.wait_ge(S_["tables_s"], 1)
            m_fill_wait(pe, m_ids)
            pe.matmul(mout(m_ids)[0:1, 0:NCH], cst[0:E, C_ENUM:C_ENUM + 1], selc[:, :], start=True, stop=True)
            filled(pe.matmul(mout(m_ids)[0:1, NCH:NCH + 1], ones[0:E, 0:1], e_no, start=True, stop=True), m_ids)
            for n, rows in ((m_keyc, keyT), (m_gatec, gateT)):
                m_fill_wait(pe, n)
                for t, (t0, w) in enumerate(TOK):
                    w = 2 * NS if t == 2 and n == m_keyc else w
                    o = mout(n)[0:w, t * NCH:(t + 1) * NCH]
                    last = pe.matmul(o, rows[:, t0:t0 + w], selc[:, :], start=True, stop=(n != m_keyc))
                    if n == m_keyc:
                        last = pe.matmul(o, ones[0:E, 0:w], selb[:, :], start=False, stop=True)
                filled(last, n)

            def gather(n, c, more=0):
                m_fill_wait(pe, n, more)
                for k in range(2):
                    f0 = (2 * c + k) * P
                    o = mout(n)[:, k * 4 * C:(k + 1) * 4 * C]
                    for t in range(2):
                        pe.matmul(o, xh[:, t, f0:f0 + P], oh[:, t, :], start=(t == 0), stop=False)
                        pe.matmul(o, xl[:, t, f0:f0 + P], oh[:, t, :], start=False, stop=False)
                    last = pe.matmul(o, xs[:, f0:f0 + P], oh[0:2 * NS, 2, :], start=False, stop=True)
                filled(last, n)

            def scatter(n0, buf, more=0):
                for k in range(KD):
                    m_fill_wait(pe, n0 + k, more)
                    pe.matmul(mout(n0 + k)[:, 0:T], yh[:, k * P:(k + 1) * P], pt[buf][:, :], start=True, stop=False)
                    filled(pe.matmul(mout(n0 + k)[:, 0:T], yl[:, k * P:(k + 1) * P], pt[buf][:, :],
                                     start=False, stop=True), n0 + k)

            turns = load_turns(pe)
            for n in m_hx:
                m_drain_wait(pe, n)
            pe.wait_ge(S_["oh_s"], 1)
            for c in range(4):
                gather(m_a0[c], c)
            for n in m_a0:
                m_drain_wait(pe, n)
            pe.wait_ge(S_["zero_s"], 1)
            with pe.Fori(0, turns) as q:
                for s in range(2):
                    more = q * 4
                    if s == 0:
                        for n in m_a:
                            m_drain_wait(pe, n - M_TURN, more)
                    for j in range(2):
                        n = m_gu[s][j]
                        m_fill_wait(pe, n, more)
                        for h in range(2):
                            i = 6 * s + 2 * j + h
                            low_wait(pe, 2 * j + h, s, q)
                            for k in range(4):
                                x = xsel[:, 4 * h + k, 2 * s + j, :]
                                pe.matmul(mout(n)[:, :], x, gate_up_rows(w_hi[i % 4][:, :])[:, k, :],
                                          start=(h == 0 and k == 0), stop=False)
                                last = pe.matmul(mout(n)[:, :], x, gate_up_rows(w_lo[i % 4][:, :])[:, k, :],
                                                 start=False, stop=(h == 1 and k == 3))
                            if h == 0:
                                last.then_inc(S_["w_used"], 1)
                        filled(last, n)

                    def halves(j):
                        m_drain_wait(pe, m_gu[s][j], more)
                        for mf in range(4):
                            c0 = mf * 2 * C + j * C
                            last = pe.matmul(mout(m_b[s])[:, c0:c0 + C], gu[j][:, mf * P:(mf + 1) * P],
                                             cst[:, C_TWO:C_TWO + C], start=True, stop=True)
                        return last

                    m_fill_wait(pe, m_b[s], more)
                    halves(0)
                    m_fill_wait(pe, m_t[s], more)
                    pe.wait_ge(S_["ohg_s"], q * 2 + (s + 1))
                    for t, (t0, w) in enumerate(TOK):
                        last = pe.transpose(mout(m_t[s])[:, t0:t0 + w], ohg[0:w, t, :], ident[0:w, 0:w])
                    filled(last, m_t[s])
                    if s == 1:
                        pe.wait_ge(S_["oh_s"], q + 2)
                        gather(m_a[0], 0, more)
                    filled(halves(1), m_b[s])
                    if s == 1:
                        gather(m_a[1], 1, more)
                        gather(m_a[2], 2, more)
                        gather(m_a[3], 3, more)
                    for n in m_c_before[s]:
                        m_drain_wait(pe, n, more)
                    scatter(m_e[s][0], 1 - s, more)
                    pe.wait_ge(S_["hl_s"], q * 2 + (s + 1))
                    for j in range(2):
                        i = 6 * s + 4 + j
                        low_wait(pe, 4 + j, s, q)
                        for c in range(2):
                            n = m_c[s][c]
                            if j == 0:
                                m_fill_wait(pe, n, more)
                            for f in range(2):
                                wh = down_rows(w_hi[i % 4][:, :])[:, f, c * BC:(c + 1) * BC]
                                wl = down_rows(w_lo[i % 4][:, :])[:, f, c * BC:(c + 1) * BC]
                                high, rest = (hr[:, f, u, j * C:j * C + 2 * C] for u in range(2))
                                pe.matmul(mout(n)[:, :], high, wh, start=(j == 0 and f == 0), stop=False)
                                pe.matmul(mout(n)[:, :], high, wl, start=False, stop=False)
                                last = pe.matmul(mout(n)[:, :], rest, wh, start=False, stop=(j == 1 and f == 1))
                            if j == 1:
                                filled(last, n)
                        if j == 0:
                            last.then_inc(S_["w_used"], 1)
            more = turns * 4
            for n in m_c_before[0]:
                m_drain_wait(pe, n, more)
            scatter(m_el[0], 1, more)
            m_fill_wait(pe, m_nf, more)
            for k in range(KD):
                pe.wait_ge(S_["x2_sq"], k + 1)
                last = pe.matmul(mout(m_nf)[:, 0:T], ones, sq2[:, k, :], start=(k == 0), stop=(k == KD - 1))
            filled(last, m_nf)
            for c in range(2):
                pe.wait_ge(S_["yT"], 4 * (c + 1))
                for t, (t0, w) in enumerate(TOK):
                    n = m_y[3 * c + t]
                    m_fill_wait(pe, n, more)
                    for k in range(4):
                        last = pe.transpose(mout(n)[0:w, k * P:(k + 1) * P], hT[:, 4 * c + k, t0:t0 + w], ident)
                    filled(last, n)

        @block.gpsimd
        def _(pool):
            def split_low(i, hi_count):
                pool.wait_ge(S_["hi_done"], hi_count)
                pool.tensor_tensor(w_lo[i % 4][:, :], raw[i % 4], w_hi[i % 4][:, :].bitcast(F32), ALU.subtract)\
                    .then_inc(S_["lo_pool"], 1)

            with pool.Fori(0, (N_TILES + 4) // TILES_PER_TURN) as i:
                for t in range(TILES_PER_TURN):
                    pool.wait_ge(S_["tile_hi"], i * TILES_PER_TURN + (t + 1))
                    pool.tensor_tensor(t_lo[t % 4][:, :, :], raw_tile(t), t_hi[t % 4][:, :, :].bitcast(F32), ALU.subtract)\
                        .then_inc(S_["tile_lo"], 1)
            split_low(0, 1)
            turns = load_turns(pool)
            with pool.Fori(0, turns) as q:
                for s in range(2):
                    for i in (4, 6):
                        split_low(6 * s + i, q * 12 + (6 * s + i + 1))

        @block.scalar
        def _(act):
            def copy(dst, src, **kw):
                return act.activation(dst, src, ACT.Copy, **kw)

            def src(r, n):
                return bank[bk(r, n)]

            def freed(ins, r, n):
                ins.then_inc(free[bk(r, n)], 1)

            def root(r, n, mean_of, dst):
                read_wait(act, r, n)
                act.wait_ge(S_["eps"], 1)
                freed(act.activation(dst, src(r, n)[:, 0:T], ACT.Sqrt, scale=1.0 / mean_of, bias=eps_col[:, 0:1]), r, n)

            def ada_rows(z, turned):
                for j, n in enumerate(z):
                    read_wait(act, 0, n)
                    if j >= 2:
                        act.wait_ge(S_["arow_t"], turned + j - 1)
                    freed(copy(arow[:, j % 2, :], src(0, n)[0:NSEQ, :]), 0, n)

            for k in range(KD):
                read_wait(act, 0, z_x[k])
                freed(copy(xT[:, k, :], src(0, z_x[k])[:, 0:T]), 0, z_x[k])
            root(0, z_n1, D, rstd[:, :])
            ada_rows(z_ara, 0)
            def tile_high(t, turn=0):
                if t % 4 == 0:
                    arrived(act, N_ADA_A + t // 4, turn * 16)
                copy(t_hi[t % 4][:, :, :], raw_tile(t)).then_inc(S_["tile_hi"], 1)

            for t in range(4):
                tile_high(t)
            for k in range(KD):
                act.wait_ge(S_["h1"], k + 1)
                copy(x_hi[:, k, :], hT[:, k, :]).then_inc(S_["x_hi"], 1)
            for t, n in enumerate([*z_vt, *z_uqk]):
                read_wait(act, 0, n)
                freed(copy(zT[:, Z_G + t if t < 8 else Z_U + t - 8, :], src(0, n)[:, 0:T]), 0, n)
                tile_high(t + 4)
            for j in range(N_V):
                for t, (t0, w) in enumerate(TOK):
                    n = z_v[3 * j + t]
                    read_wait(act, 0, n)
                    freed(copy(v[0:w, t, j * BC:(j + 1) * BC], src(0, n)[0:w, :]), 0, n)
            read_wait(act, 0, z_pool)
            freed(copy(stT[:, :, :].rearrange("p g r -> p (g r)"), src(0, z_pool)[:, 0:480]), 0, z_pool)
            for t, w in enumerate([PB, NS]):
                read_wait(act, 0, z_tail[t])
                freed(copy(ptail[0:w, t, :], src(0, z_tail[t])[0:w, :]), 0, z_tail[t])
            with act.Fori(0, N_FM // RING) as i:
                for j in range(TILES_PER_TURN):
                    n = z_fm[j]
                    read_wait(act, 0, n, i * 3)
                    freed(copy(zT[:, bass.ds(i * 12 + (Z_G + j), 1), :].rearrange("p a t -> p (a t)"),
                               src(0, n)[:, 0:T]), 0, n)
                    tile_high(24 + j, i)
            ada_rows(z_arb, N_ADA_A - 1)
            for n in z_fm[-4:]:
                drain_wait(act, 0, n)
            act.activation(zT[:, Z_A:Z_A + 16, :], zT[:, Z_A:Z_A + 16, :], ACT.Sigmoid).then_inc(S_["sig_ab"], 1)
            act.activation(zT[:, Z_G:Z_G + 8, :], zT[:, Z_G:Z_G + 8, :], ACT.Silu).then_inc(S_["silu_g"], 1)
            for g in range(G):
                read_wait(act, 0, z_pg[g])
                freed(act.activation(hT[:, g, :], src(0, z_pg[g])[:, 0:T], ACT.Copy,
                                     scale=vecT[:, V_PS + g:V_PS + g + 1]), 0, z_pg[g])
            for h in range(G):
                for et in range(2):
                    n = z_o[h][et]
                    read_wait(act, 0, n)
                    freed(copy(zT[:, (Z_Q, Z_K)[et] + h, :], src(0, n)[:, 0:T]), 0, n)
                if h >= 2:
                    read_wait(act, 1, y_hn[h - 2])
                for et in range(2):
                    drain_wait(act, 0, z_o[h][et])
                    last = act.activation(hT[:, 4 + 2 * (h % 2) + et, :], zT[:, (Z_Q, Z_K)[et] + h, :], ACT.Square)
                last.then_inc(S_["osq"], 1)
                if h > 0:
                    root(1, y_hn[h - 1], DV, zT[:, Z_U + h - 1, :])
            root(1, y_hn[G - 1], DV, zT[:, Z_U + G - 1, :])
            root(1, y_n2, D, rstd[:, :])
            def msrc(n):
                return bank[n % 8]

            def mfreed(ins, n):
                ins.then_inc(mfree[n % 8], 1)

            act.wait_ge(S_["router_set"], 1)
            for t, (t0, w) in enumerate(TOK):
                m_read_wait(act, m_rt[t])
                mfreed(act.activation(sc_s[0:w, t, :], msrc(m_rt[t])[0:w, 0:E], ACT.Sigmoid), m_rt[t])
            for f in range(2):
                m_read_wait(act, m_sgu[f])
                mfreed(act.activation(sgS[:, f, :], msrc(m_sgu[f])[:, 0:T], ACT.Silu), m_sgu[f])
            for t, (t0, w) in enumerate(TOK):
                for c in range(2):
                    n = m_hx[2 * t + c]
                    m_read_wait(act, n)
                    dst = xh[:, t, c * BC:(c + 1) * BC] if t < 2 else xs[0:NS, c * BC:(c + 1) * BC]
                    copy(dst, msrc(n)[0:w, :]).then_inc(S_["yh_s"], 1)
            for k in range(KD):
                m_read_wait(act, m_sd[k])
                mfreed(copy(acc[:, k, :], msrc(m_sd[k])[:, 0:T]), m_sd[k])

            def split_high(i, q=None):
                if q is None:
                    act.wait_ge(raw_in[i], loads[i])
                else:
                    piece_loaded(act, i, q)
                copy(w_hi[i % 4][:, :], raw[i % 4]).then_inc(S_["hi_done"], 1)

            def slots_high(n, c, more=0):
                m_read_wait(act, n, more)
                copy(xsel[:, 2 * c:2 * c + 2, :, 0:C],
                     msrc(n)[:, :].rearrange("p (k j s) -> p k j s", k=2, j=4)).then_inc(S_["xs_hi"], 1)

            for i in range(4):
                split_high(i)
            for c in range(4):
                slots_high(m_a0[c], c)
            turns = load_turns(act)
            act.wait_ge(S_["zero_s"], 1)
            with act.Fori(0, turns) as q:
                for s in range(2):
                    more = q * 4

                    def gate_up_out(j):
                        n = m_gu[s][j]
                        m_read_wait(act, n, more)
                        mfreed(copy(gu[j][:, :], msrc(n)[:, :]), n)

                    act.wait_ge(S_["w_used"], q * 6 + (3 * s + 1))
                    split_high(6 * s + 4, q)
                    gate_up_out(0)
                    split_high(6 * s + 5, q)
                    gate_up_out(1)
                    if s == 1:
                        split_high(6 * s + 6, q)
                        slots_high(m_a[0], 0, more)
                    m_read_wait(act, m_b[s], more)
                    act.activation(sg.rearrange("p f s -> p (f s)"), msrc(m_b[s])[:, 0:4 * C], ACT.Silu)\
                       .then_inc(S_["sg_s"], 1)
                    m_drain_wait(act, m_b[s], more)
                    copy(by_chunk(hr[:, :, 0, :])[:, :, :, 0:C], by_chunk(hid)).then_inc(S_["hh_s"], 1)
                    if s == 1:
                        for c in (1, 2, 3):
                            slots_high(m_a[c], c, more)
                    else:
                        split_high(6 * s + 6, q)
                    split_high(6 * s + 7, q)
                    act.wait_ge(S_["w_used"], q * 6 + (3 * s + 3))
                    split_high(6 * s + 8, q)
                    m_read_wait(act, m_c[s][1], more)
                    split_high(6 * s + 9, q)
                    for c in range(2):
                        n = m_c[s][c]
                        m_read_wait(act, n, more)
                        act.activation(yh[:, c * BC:(c + 1) * BC], msrc(n)[:, :], ACT.Copy, scale=gslot[s][:, 0:1])\
                           .then_inc(S_["yh_s"], 1)
            more = turns * 4
            m_read_wait(act, m_nf, more)
            mfreed(act.activation(rstd[:, :], msrc(m_nf)[:, 0:T], ACT.Sqrt, scale=1.0 / D, bias=eps_col[:, 0:1]), m_nf)
            for c in range(2):
                for t, (t0, w) in enumerate(TOK):
                    n = m_y[3 * c + t]
                    m_read_wait(act, n, more)
                    copy(ystage[0:w, t, c * BC:(c + 1) * BC], msrc(n)[0:w, :]).then_inc(S_["y_staged"], 1)

        @block.vector
        def _(dve):
            chain = [0]

            def link(ins):
                chain[0] += 1
                ins.then_inc(dve_chain, 1)
                dve.wait_ge(dve_chain, chain[0])

            def src(r, n):
                return bank[bk(r, n)]

            def freed(ins, r, n):
                ins.then_inc(free[bk(r, n)], 1)

            def toks(ap):
                return ap.rearrange("p k (b l) -> p k b l", b=DEC_B)

            def normed(sums_at):
                drain_wait(dve, *sums_at)
                link(dve.reciprocal(rstd[:, :], rstd[:, :]))
                link(dve.tensor_tensor(hT[:, :, :], xT[:, :, :], bcast(rstd[:, :], 1, KD), ALU.mult))

            def modulation_scale(g_at, scale):
                link(dve.scalar_tensor_tensor(gs[:, :, :], modT[:, scale:scale + KD, :], 1.0,
                                              bcast(vecT[:, g_at:g_at + KD], 2, NSEQ), ALU.add, ALU.mult))

            def modulate(shift, modulated):
                hs = toks(hT[:, :, SEQ:T])
                link(dve.tensor_tensor(hs, hs, bcast(gs[:, :, 1:NSEQ], 3, DEC_L), ALU.mult))
                dve.tensor_tensor(hs, hs, bcast(modT[:, shift:shift + KD, 1:NSEQ], 3, DEC_L), ALU.add)
                for k in range(KD):
                    dve.tensor_scalar(hT[:, k, 0:SEQ], hT[:, k, 0:SEQ], gs[:, k, 0:1], modT[:, shift + k, 0:1],
                                      ALU.mult, ALU.add).then_inc(modulated, 1)

            def mod_rows(y, j0, count):
                read_wait(dve, 1, y)
                freed(dve.tensor_tensor(modT[:, j0:j0 + count, :],
                                        src(1, y)[:, 0:count * NSEQ].rearrange("p (j s) -> p j s", s=NSEQ),
                                        bcast(vecT[:, V_ADA + j0:V_ADA + j0 + count], 2, NSEQ), ALU.add), 1, y)

            dve.memset(eps_col[:, :], EPS).then_inc(S_["eps"], 1)
            for k in range(KD):
                drain_wait(dve, 0, z_x[k])
                dve.tensor_tensor(zT[:, k, :], xT[:, k, :], xT[:, k, :], ALU.mult).then_inc(S_["xT_sq"], 1)
            read_wait(dve, 0, z_vec)
            link(dve.tensor_copy(vecT[:, :], src(0, z_vec)[:, 0:NV]))
            freed(dve.tensor_copy(cT[:, :, :], src(0, z_vec)[:, P:P + KD * NSEQ].rearrange("p (k s) -> p k s", s=NSEQ)),
                  0, z_vec)
            normed((0, z_n1))
            mod_rows(y_moda, 0, 2 * KD)
            drain_wait(dve, 1, y_moda)
            modulation_scale(V_G1, KD)
            modulate(0, S_["h1"])
            for k in range(KD):
                dve.wait_ge(S_["x_hi"], k + 1)
                dve.tensor_tensor(x_lo[:, k, :], hT[:, k, :], x_hi[:, k, :].bitcast(F32), ALU.subtract)\
                   .then_inc(S_["x_lo"], 1)
            rt = qd[:, :, :].rearrange("p h c -> p (h c)")
            for j in range(8):
                q = zT[:, Z_Q + j, :]
                read_wait(dve, 0, z_swap[j])
                dve.tensor_tensor(rt[:, 0:T], q, cst[:, C_COS:C_COS + T], ALU.mult)
                freed(dve.tensor_tensor(rt[:, T:2 * T], src(0, z_swap[j])[:, 0:T], cst[:, C_SIN:C_SIN + T], ALU.mult),
                      0, z_swap[j])
                drain_wait(dve, 0, z_swap[j])
                dve.tensor_tensor(q, rt[:, 0:T], rt[:, T:2 * T], ALU.add).then_inc(S_["rot"], 1)
                dve.wait_ge(S_["rot"], j + 1)
            for h in range(G):
                w = C_QDEC + h * (CHUNK + NS)
                dve.tensor_tensor(qd[:, h, :], zT[:, Z_Q + h, CHUNK:T], cst[:, w:w + CHUNK + NS], ALU.mult)\
                   .then_inc(S_["qd_s"], 1)
            for t, (t0, w) in enumerate(TOK):
                read_wait(dve, 0, z_kt[t])
                dst, dec = (ktok[:, t, :], C_KDEC) if t < 2 else (ktoks, C_KDECS)
                last = dve.tensor_tensor(dst.rearrange("p (h d) -> p h d", h=G),
                                         src(0, z_kt[t])[0:w, :].rearrange("p (h d) -> p h d", h=G),
                                         bcast(cst[0:w, dec:dec + G], 2, P), ALU.mult)
                freed(last, 0, z_kt[t])
            drain_wait(dve, 0, z_kt[2])
            read_wait(dve, 0, z_fm[-1])
            link(dve.memset(extp[:, :, 0:PB], 0.0))
            dve.tensor_copy(extp[:, :, PB:LP], zT[:, Z_U:Z_U + G, 0:SEQ])
            for g in range(G):
                if g == 0:
                    drain_wait(dve, 0, z_pool)
                dve.tensor_copy(exts[:, g, :, 0:PB], stT[:, g, :].rearrange("p (b r) -> p b r", b=DEC_B))
                last = dve.tensor_copy(exts[:, g, :, PB:LS], zT[:, Z_U + g, SEQ:T].rearrange("p (b l) -> p b l", b=DEC_B))
            link(last)
            views = []
            for area_ in (sumA, sumB):
                views.append((area_[:, 0:G * LP].rearrange("p (g l) -> p g l", g=G),
                              area_[:, G * LP:PW].rearrange("p (g b l) -> p g b l", g=G, b=DEC_B)))
            prev = (extp, exts)
            for s in range(G):
                cur = views[s % 2]
                sh, lo = 1 << s, (2 << s) - 1
                dve.tensor_tensor(cur[0][:, s:G, lo:LP], prev[0][:, s:G, lo:LP], prev[0][:, s:G, lo - sh:LP - sh],
                                  ALU.add)
                for g in range(s, G):
                    last = dve.tensor_tensor(cur[1][:, g, :, lo:LS], prev[1][:, g, :, lo:LS],
                                             prev[1][:, g, :, lo - sh:LS - sh], ALU.add)
                link(last)
                prev = cur
            for t in range(2):
                read_wait(dve, 0, z_tail[t])
            for g in range(G):
                sp_, ss_ = views[g % 2]
                u = zT[:, Z_U + g, :]
                link(dve.tensor_tensor(sp_[:, g, PB:PB + 16], sp_[:, g, PB:PB + 16],
                                       cst[:, C_ICNT + 16 * g:C_ICNT + 16 * (g + 1)], ALU.mult))
                dve.tensor_tensor(u[:, 0:16], sp_[:, g, PB:PB + 16], u[:, 0:16], ALU.subtract)
                dve.scalar_tensor_tensor(u[:, 16:SEQ], sp_[:, g, PB + 16:LP], 1.0 / WINDOWS[g], u[:, 16:SEQ],
                                         ALU.mult, ALU.subtract)
                us = u[:, SEQ:T].rearrange("p (b l) -> p b l", b=DEC_B)
                dve.scalar_tensor_tensor(us, ss_[:, g, :, PB:LS], 1.0 / WINDOWS[g], us, ALU.mult, ALU.subtract)\
                   .then_inc(S_["pm"], 1)
            dve.wait_ge(S_["pm"], G)
            for b in range(DEC_B):
                last = dve.tensor_scalar(kblk[:, b, :], ktoks, cst[0:NS, C_ROWB + b:C_ROWB + b + 1], None, ALU.mult)
            last.then_inc(S_["kbl"], 1)
            mod_rows(y_modb, 2 * KD, 4 * KD)
            drain_wait(dve, 1, y_modb)

            def masked(h):
                n = y_sc[h]
                read_wait(dve, 1, n)
                dve.tensor_tensor(sT[:, h % 2, 0:SEQ].rearrange("p (c q) -> p c q", c=2),
                                  src(1, n)[:, 0:SEQ].rearrange("p (c q) -> p c q", c=2),
                                  bcast(cst[:, C_INTRA + h * P:C_INTRA + (h + 1) * P], 1, 2), ALU.mult)
                freed(dve.tensor_tensor(sT[0:NS, h % 2, SEQ:T], src(1, n)[0:NS, SEQ:T],
                                        cst[0:NS, C_INTRAS + h * NS:C_INTRAS + (h + 1) * NS], ALU.mult), 1, n)
                read_wait(dve, 1, y_s0[h])
                freed(dve.tensor_copy(SP0[:, h, :], src(1, y_s0[h])[:, 0:DV]), 1, y_s0[h])

            def under_gate(h):
                dve.wait_ge(S_["silu_g"], 1)
                drain_wait(dve, 1, y_hn[h])
                u = zT[:, Z_U + h, :]
                link(dve.reciprocal(u, u))
                gg = zT[:, Z_G + 2 * h:Z_G + 2 * h + 2, :]
                link(dve.tensor_tensor(gg, gg, bcast(u, 1, 2), ALU.mult))
                for et in range(2):
                    o = zT[:, (Z_Q, Z_K)[et] + h, :]
                    g_ = zT[:, Z_G + 2 * h + et, :]
                    last = dve.tensor_tensor(g_, g_, o, ALU.mult)
                last.then_inc(S_["gated"], 1)

            for h in range(G + 1):
                if h < G:
                    masked(h)
                if h > 0:
                    g = h - 1
                    read_wait(dve, 1, y_s1[g])
                    drain_wait(dve, 1, y_s0[g])
                    freed(dve.scalar_tensor_tensor(SP0[:, g, :], SP0[:, g, :], s_dec[g], src(1, y_s1[g])[:, 0:DV],
                                                   ALU.mult, ALU.add), 1, y_s1[g])
                    for bp in range(DEC_B // 2):
                        n = y_ss[g][bp]
                        read_wait(dve, 1, n)
                        st = S[:, g, 2 * bp:2 * bp + 2, :].rearrange("p b e -> p (b e)")
                        freed(dve.scalar_tensor_tensor(st, st, s_dec_s[g], src(1, n)[:, :], ALU.mult, ALU.add), 1, n)
                if h > 2:
                    under_gate(h - 3)
            under_gate(G - 2)
            dve.wait_ge(S_["sig_ab"], 1)
            for j in range(KD):
                if j == 4:
                    under_gate(G - 1)
                read_wait(dve, 0, z_a[j])
                a = zT[:, Z_A + j, :]
                freed(dve.tensor_tensor(a, a, src(0, z_a[j])[:, 0:T], ALU.mult), 0, z_a[j])
            for j in range(KD):
                read_wait(dve, 0, z_r[j])
                b = zT[:, Z_B + j, :]
                freed(dve.tensor_tensor(b, b, src(0, z_r[j])[:, 0:T], ALU.mult), 0, z_r[j])
                drain_wait(dve, 0, z_r[j])
                drain_wait(dve, 0, z_a[j])
                dve.tensor_tensor(zT[:, Z_A + j, :], zT[:, Z_A + j, :], b, ALU.add).then_inc(S_["merged"], 1)

            def residual(z, k, gate, last_sem):
                read_wait(dve, 0, z)
                m = src(0, z)
                tmp = zT[:, 8 + k, SEQ:T]
                dve.scalar_tensor_tensor(xT[:, k, 0:SEQ], m[:, 0:SEQ], modT[:, gate + k, 0:1], xT[:, k, 0:SEQ],
                                         ALU.mult, ALU.add)
                freed(dve.tensor_tensor(tmp.rearrange("p (b l) -> p b l", b=DEC_B),
                                        m[:, SEQ:T].rearrange("p (b l) -> p b l", b=DEC_B),
                                        bcast(modT[:, gate + k, 1:NSEQ], 2, DEC_L), ALU.mult), 0, z)
                drain_wait(dve, 0, z)
                link(dve.tensor_tensor(xT[:, k, SEQ:T], xT[:, k, SEQ:T], tmp, ALU.add))
                dve.tensor_tensor(zT[:, k, :], xT[:, k, :], xT[:, k, :], ALU.mult).then_inc(last_sem, 1)

            for k in range(KD):
                residual(z_m[k], k, 2 * KD, S_["x1_sq"])
            modulation_scale(V_G2, 4 * KD)
            normed((1, y_n2))
            modulate(3 * KD, S_["h2"])

            dve.wait_ge(stored, 16 * N_FRONT_STORES)
            dve.memset(sc_s[:, :, :], 0.5).then_inc(S_["router_set"], 1)
            dve.memset(pt[1][:, :].bitcast(F32), 0.0)
            dve.memset(hr[:, :, :, :].bitcast(F32), 0.0)
            dve.memset(yh[:, :].bitcast(F32), 0.0)
            dve.memset(yl[:, :].bitcast(F32), 0.0).then_inc(S_["zero_s"], 1)
            for t in range(3):
                m_drain_wait(dve, m_rt[t])
            dve.wait_ge(ld["router"], 32)
            dve.memset(gsc[:, :, 8:12], LOW)
            dve.memset(etop[:, :, :], LOW)
            link(dve.tensor_tensor(sc_b, sc_s, bcast(brow[:, :], 1, 3), ALU.add))
            for t in range(3):
                for g in range(NG):
                    last = dve.max(gtop[:, t, g, :], sc_b[:, t, g * EG:(g + 1) * EG])
            link(last)
            link(dve.tensor_tensor(gsc[:, :, 0:NG], gtop[:, :, :, 0], gtop[:, :, :, 1], ALU.add))
            for t in range(3):
                last = dve.max(gsort[:, t, :], gsc[:, t, 0:NG])
            link(last)
            link(dve.tensor_copy(etop[:, :, 0:4], gsort[:, :, 0:4]))
            for t in range(3):
                last = dve.match_replace(grep[:, t, :], etop[:, t, :], gsc[:, t, :], 2 * LOW)
            link(last)
            link(dve.tensor_scalar(gmask, grep[:, :, 0:NG], 1.5 * LOW, None, ALU.is_le))
            link(dve.tensor_scalar(gfill, gmask, 1.0, -LOW, ALU.subtract, ALU.mult))
            by_group = lambda ap: ap.rearrange("p t (g e) -> p (t g) e", g=NG)
            one = lambda ap: bcast(ap.rearrange("p t g -> p (t g)"), 2, EG)
            link(dve.tensor_tensor(by_group(sc_m), by_group(sc_b), one(gmask), ALU.mult))
            link(dve.tensor_tensor(by_group(sc_m), by_group(sc_m), one(gfill), ALU.add))
            for t in range(3):
                last = dve.max(etop[:, t, :], sc_m[:, t, :])
            link(last)
            for t in range(3):
                last = dve.match_replace(sc_r[:, t, :], etop[:, t, :], sc_m[:, t, :], 2 * LOW)
            link(last)
            dve.tensor_scalar(sel, sc_r, 1.5 * LOW, None, ALU.is_le).then_inc(S_["sel_s"], 1)
            dve.wait_ge(S_["sel_s"], 1)
            link(dve.tensor_tensor(gates, sel, sc_s, ALU.mult))
            link(dve.tensor_reduce(wsum, gates, AX_X, ALU.add))
            link(dve.reciprocal(winv, wsum))
            link(dve.tensor_scalar(winv, winv, SCALE_OUT, None, ALU.mult))
            link(dve.tensor_tensor(gates, gates, bcast(winv, 2, E), ALU.mult))

            def msrc(n):
                return bank[n % 8]

            def mfreed(ins, n):
                ins.then_inc(mfree[n % 8], 1)

            for f in range(2):
                m_drain_wait(dve, m_sgu[f])
                m_read_wait(dve, m_sgu[2 + f])
                mfreed(dve.tensor_tensor(hidS[:, f, :], sgS[:, f, :], msrc(m_sgu[2 + f])[:, 0:T], ALU.mult), m_sgu[2 + f])
            m_read_wait(dve, m_rank)
            link(dve.memset(keys, 0.0))
            for t, (t0, w) in enumerate(TOK):
                last = dve.scalar_tensor_tensor(keys[0:w, t, :], msrc(m_rank)[0:w, t * E:(t + 1) * E], KEY0, sel[0:w, t, :],
                                                ALU.add, ALU.mult)
                if t == 2:
                    mfreed(last, m_rank)
            for t, (t0, w) in enumerate(TOK):
                for c in range(2):
                    n = m_hx[2 * t + c]
                    m_read_wait(dve, n)
                    dve.wait_ge(S_["yh_s"], 2 * t + c + 1)
                    cc = slice(c * BC, (c + 1) * BC)
                    hi, lo = (xh[:, t, cc], xl[:, t, cc]) if t < 2 else (xs[0:NS, cc], xs[NS:2 * NS, cc])
                    mfreed(dve.tensor_tensor(lo, msrc(n)[0:w, :], hi.bitcast(F32), ALU.subtract), n)
            m_read_wait(dve, m_keyT)
            dve.tensor_copy(keyT[:, 0:T], msrc(m_keyT)[0:E, 0:T])
            mfreed(dve.tensor_copy(keyT[:, T:T + NS], msrc(m_keyT)[0:E, SEQ:T]), m_keyT)
            m_read_wait(dve, m_gateT)
            mfreed(dve.tensor_copy(gateT[:, :], msrc(m_gateT)[0:E, 0:T]), m_gateT)
            m_drain_wait(dve, m_keyT)
            chosen = sgE
            link(dve.tensor_scalar(chosen, keyT[:, 0:T], 0.5 * KEY0, None, ALU.is_ge))
            link(dve.tensor_reduce(e_cnt, chosen, AX_X, ALU.add))
            link(dve.tensor_scalar(e_full, cst[0:E, C_FULL:C_FULL + 4], e_cnt, None, ALU.is_lt))
            dve.tensor_reduce(e_no, e_full, AX_X, ALU.add).then_inc(S_["no_s"], 1)
            m_read_wait(dve, m_ob)
            mfreed(dve.tensor_copy(e_ob, msrc(m_ob)[0:E, 0:1]), m_ob)
            m_drain_wait(dve, m_ob)
            dve.tensor_copy(selc[:, 0:E], ident[0:E, 0:E])
            dve.memset(selb[:, 0:E], 0.0)
            over, later, right = selc[:, E:NCH], selb[:, E:NCH], oE
            dve.wait_ge(S_["no_s"], 1)
            link(dve.tensor_scalar(later, cst[0:E, C_OVER:C_OVER + 40], e_ob, None, ALU.subtract))
            link(dve.tensor_scalar(right, later, e_no, None, ALU.is_lt))
            link(dve.scalar_tensor_tensor(over, later, 0.0, right, ALU.is_ge, ALU.mult))
            link(dve.tensor_scalar(later, later, 1.0, -float(C), ALU.add, ALU.mult))
            dve.tensor_tensor(later, later, over, ALU.mult).then_inc(S_["tables_s"], 1)
            m_read_wait(dve, m_ids)
            dve.tensor_scalar(q_full, cst[0:1, C_QUAD:C_QUAD + 9], msrc(m_ids)[0:1, NCH:NCH + 1], None, ALU.is_lt)\
               .then_inc(dve_chain, 1)
            chain[0] += 1
            dve.wait_ge(dve_chain, chain[0])
            mfreed(dve.tensor_copy(ids[:, :], msrc(m_ids)[0:1, 0:NCH]), m_ids)
            link(dve.tensor_reduce(q_n, q_full, AX_X, ALU.add))
            m_drain_wait(dve, m_ids)
            dve.tensor_scalar(nquads[:, :], q_n, float(MIN_Q), None, ALU.add).then_inc(S_["chunks_s"], 1)
            dve.memset(keyc[:, :, :], 0.0)
            link(dve.memset(gatec[:, :, :], 0.0))
            for n, dst in ((m_keyc, keyc), (m_gatec, gatec)):
                m_read_wait(dve, n)
                dve.tensor_copy(dst[:, 0:2, :].rearrange("p t c -> p (t c)"), msrc(n)[:, 0:2 * NCH])
                w = 2 * NS if n == m_keyc else NS
                mfreed(dve.tensor_copy(dst[0:w, 2, :], msrc(n)[0:w, 2 * NCH:3 * NCH]), n)
            m_drain_wait(dve, m_keyc)
            m_drain_wait(dve, m_gatec)

            def slots(chunk, before):
                if before is not None:
                    dve.wait_ge(S_["ohg_s"], before)
                four = keyc[:, :, bass.ds(chunk, 4)]
                row = bcast(bcast(cst[:, C_SLOT:C_SLOT + C], 1, 4), 1, 3)
                dve.tensor_tensor(oh[:, :, :].rearrange("p t (j s) -> p t j s", j=4), row, bcast(four, 3, C),
                                  ALU.is_equal).then_inc(S_["oh_s"], 1)

            def gated_slots(chunk, pair, count):
                dve.wait_ge(S_["oh_s"], count)
                two = gatec[:, :, bass.ds(chunk, 2)]
                ones_ = oh[:, :, pair * 2 * C:(pair + 1) * 2 * C].bitcast(F32)
                dve.tensor_tensor(ohg[:, :, :].rearrange("p t (j s) -> p t j s", j=2),
                                  ones_.rearrange("p t (j s) -> p t j s", j=2), bcast(two, 3, C),
                                  ALU.mult).then_inc(S_["ohg_s"], 1)

            def split_low(i, hi_count):
                dve.wait_ge(S_["hi_done"], hi_count)
                dve.tensor_tensor(w_lo[i % 4][:, :], raw[i % 4], w_hi[i % 4][:, :].bitcast(F32), ALU.subtract)\
                   .then_inc(S_["lo_done"], 1)

            def slots_low(n, c, count):
                dve.wait_ge(S_["xs_hi"], count)
                x = xsel[:, 2 * c:2 * c + 2, :, :]
                mfreed(dve.tensor_tensor(x[:, :, :, C:2 * C], msrc(n)[:, :].rearrange("p (k j s) -> p k j s", k=2, j=4),
                                         x[:, :, :, 0:C].bitcast(F32), ALU.subtract), n)

            def add_up(n0, more=0, ks=range(KD)):
                for k in ks:
                    m_read_wait(dve, n0 + k, more)
                    mfreed(dve.tensor_tensor(acc[:, k, :], acc[:, k, :], msrc(n0 + k)[:, 0:T], ALU.add), n0 + k)

            slots(0, None)
            gated_slots(0, 0, 1)
            for n in m_sd:
                m_drain_wait(dve, n)
            split_low(1, 2)
            for c in range(4):
                slots_low(m_a0[c], c, c + 1)
            split_low(2, 3)
            split_low(3, 4)
            turns = load_turns(dve)
            with dve.Fori(0, turns) as q:
                for s in range(2):
                    more = q * 4
                    if s == 1:
                        m_read_wait(dve, m_a[3] - M_TURN, more)
                        slots(q * 4 + 4, q * 2 + 2)
                    split_low(6 * s + 5, q * 12 + (6 * s + 6))

                    def multiply():
                        dve.wait_ge(S_["sg_s"], q * 2 + (s + 1))
                        mfreed(dve.tensor_tensor(hid.rearrange("p f s -> p (f s)"), sg.rearrange("p f s -> p (f s)"),
                                                 msrc(m_b[s])[:, 4 * C:8 * C], ALU.mult), m_b[s])

                    def hidden_low():
                        dve.wait_ge(S_["hh_s"], q * 2 + (s + 1))
                        dve.tensor_tensor(by_chunk(hr[:, :, 1, :])[:, :, :, 0:C], by_chunk(hid),
                                          by_chunk(hr[:, :, 0, :])[:, :, :, 0:C].bitcast(F32), ALU.subtract)\
                           .then_inc(S_["hl_s"], 1)

                    def by_slots():
                        m_read_wait(dve, m_t[s], more)
                        dve.tensor_reduce(gslot[s][:, :], msrc(m_t[s])[:, 0:T], AX_X, ALU.add)
                        mfreed(dve.tensor_scalar(pt[s][:, :], msrc(m_t[s])[:, 0:T], 0.0, None, ALU.is_gt), m_t[s])

                    def next_gated():
                        gated_slots(q * 4 + (2 * s + 2), 1 - s, q + (s + 1))

                    if s == 0:
                        multiply()
                        by_slots()
                        hidden_low()
                        add_up(m_e[s][0], more)
                        next_gated()
                    else:
                        by_slots()
                        next_gated()
                        slots_low(m_a[0], 0, q * 4 + 5)
                        multiply()
                        hidden_low()
                        for c in (1, 2, 3):
                            slots_low(m_a[c], c, q * 4 + (5 + c))
                        add_up(m_e[s][0], more)
                    for i in (7, 8, 9):
                        split_low(6 * s + i, q * 12 + (6 * s + i + 1))
                    for c in range(2):
                        n = m_c[s][c]
                        dve.wait_ge(S_["yh_s"], q * 4 + (6 + 2 * s + c + 1))
                        cc = slice(c * BC, (c + 1) * BC)
                        last = dve.scalar_tensor_tensor(yl[:, cc], msrc(n)[:, :], gslot[s][:, 0:1],
                                                        yh[:, cc].bitcast(F32), ALU.mult, ALU.subtract)
                        mfreed(last, n)
            more = turns * 4
            add_up(m_el[0], more)
            for k in range(KD):
                m_drain_wait(dve, m_el[k], more)
                dve.scalar_tensor_tensor(xT[:, k, 0:SEQ], acc[:, k, 0:SEQ], modT[:, 5 * KD + k, 0:1], xT[:, k, 0:SEQ],
                                         ALU.mult, ALU.add)
            fs = toks(acc[:, :, SEQ:T])
            link(dve.tensor_tensor(fs, fs, bcast(modT[:, 5 * KD:6 * KD, 1:NSEQ], 3, DEC_L), ALU.mult))
            link(dve.tensor_tensor(xT[:, :, SEQ:T], xT[:, :, SEQ:T], acc[:, :, SEQ:T], ALU.add))
            dve.wait_ge(S_["lo_pool"], turns * 4 + 1)
            for k in range(KD):
                dve.tensor_tensor(sq2[:, k, :], xT[:, k, :], xT[:, k, :], ALU.mult).then_inc(S_["x2_sq"], 1)
            m_drain_wait(dve, m_nf, more)
            link(dve.reciprocal(rstd[:, :], rstd[:, :]))
            for k in range(KD):
                dve.scalar_tensor_tensor(hT[:, k, :], xT[:, k, :], vecT[:, V_GF + k:V_GF + k + 1], rstd[:, :],
                                         ALU.mult, ALU.mult).then_inc(S_["yT"], 1)


_INS = ["x_prompt", "x_sample", "c_prompt", "c_sample", "state_pool", "state_ret", "w_ada", "b_ada", "g_norm1",
        "w_in", "w_pool_group", "pool_scale", "w_branch_pool", "w_branch_ret", "w_out", "g_norm2", "w_router",
        "b_router", "w_exp_gate", "w_exp_up", "w_exp_down", "w_sh_gate", "w_sh_up", "w_sh_down", "g_final"]
_OUTS = [(1, SEQ, D), (DEC_B, DEC_L, D), (1, 1, PB, 512), (1, 1, G, P, DV), (1, DEC_B, PB, 512), (1, DEC_B, G, P, DV)]


def kernel(**inputs):
    import concourse.bacc as bacc
    from concourse.bass_utils import run_bass_kernel_spmd

    nc = bacc.Bacc("TRN2", target_bir_lowering=False, num_devices=1)
    arrays = {"consts": shape_constants()}
    args = [nc.dram_tensor("consts", arrays["consts"].shape, F32, kind="ExternalInput").ap()]
    for name in _INS:
        arrays[f"in_{name}"] = np.ascontiguousarray(inputs[name])
        args.append(nc.dram_tensor(f"in_{name}", arrays[f"in_{name}"].shape, F32, kind="ExternalInput").ap())
    for i, shape in enumerate(_OUTS):
        args.append(nc.dram_tensor(f"out_{i}", shape, F32, kind="ExternalOutput").ap())
    build(nc, *args)
    r = run_bass_kernel_spmd(nc, [arrays], core_ids=[0])
    return tuple(r.results[0][f"out_{i}"] for i in range(len(_OUTS)))
```
